# Optimizing a Trainium2 kernel written in Bass

```python
import jax, jax.numpy as jnp
from jax import lax
import numpy as np
import math

D_MODEL = 1024
BATCH = 1
SEQ = 512
DEPTH = 1

MEM_LEN = 256

HEAD_DIM = 64
NSA_HEADS = D_MODEL // 128
NSA_KV_HEADS = NSA_HEADS // 4
NSA_GROUP = NSA_HEADS // NSA_KV_HEADS
NSA_WIDTH = NSA_HEADS * HEAD_DIM
NSA_KV_WIDTH = NSA_KV_HEADS * HEAD_DIM
CMP_BLOCK = 32
CMP_STRIDE = 16
CMP_HIDDEN = 2 * HEAD_DIM
SLC_BLOCK = 64
N_SELECT = 8
WINDOW = 256
NSA_QBLOCK = SLC_BLOCK

GLA_HEADS = 4
GLA_DK = 64
GLA_DV = 128
GLA_KEY_WIDTH = GLA_HEADS * GLA_DK
GLA_VAL_WIDTH = GLA_HEADS * GLA_DV
GLA_GATE_RANK = 16
GLA_TAU = 16.0
GLA_CHUNK = 64

XATTN_HEADS = 4
XATTN_HEAD_DIM = 128
XATTN_WIDTH = XATTN_HEADS * XATTN_HEAD_DIM

FFN_DIM = 2816
CONV_WIDTH = 3

RMS_EPS = 1e-6
NEG_INF = -1e30

IN_SPLITS = (NSA_WIDTH, 6 * NSA_KV_WIDTH, 3 * NSA_HEADS,
             GLA_KEY_WIDTH, GLA_KEY_WIDTH, GLA_VAL_WIDTH, GLA_VAL_WIDTH, GLA_GATE_RANK,
             2 * D_MODEL)
IN_WIDTH = (NSA_WIDTH + 6 * NSA_KV_WIDTH + 3 * NSA_HEADS + 2 * GLA_KEY_WIDTH
            + 2 * GLA_VAL_WIDTH + GLA_GATE_RANK + 2 * D_MODEL)


def rms_norm(x, g):
    x32 = x.astype(jnp.float32)
    y = x32 * lax.rsqrt(jnp.mean(x32 * x32, axis=-1, keepdims=True) + RMS_EPS)
    return (y * g.astype(jnp.float32)).astype(x.dtype)

def alibi_slopes(n):
    return 2.0 ** (-8.0 * jnp.arange(1, n + 1, dtype=jnp.float32) / n)

def masked_softmax(s, mask):
    s = jnp.where(mask, s, NEG_INF)
    return jnp.where(mask, jax.nn.softmax(s, axis=-1), 0.0)

def compress_blocks(kv, pos_emb, w1, w2):
    B, S, H, dh = kv.shape
    c = kv.reshape(B, S // CMP_STRIDE, CMP_STRIDE, H, dh)
    blocks = jnp.concatenate([c[:, :-1], c[:, 1:]], axis=2) + pos_emb[None, None, :, None, :]
    n_cmp = blocks.shape[1]
    flat = blocks.transpose(0, 1, 3, 2, 4).reshape(B, n_cmp, H, CMP_BLOCK * dh)
    return jax.nn.gelu(flat @ w1) @ w2

def nsa_attention(q, kc, vc, ks, vs, kw, vw, gate_logits,
                  cmp_pos_k, cmp_w1_k, cmp_w2_k, cmp_pos_v, cmp_w1_v, cmp_w2_v):
    B, S = q.shape[:2]
    f32 = jnp.float32
    q = q.reshape(B, S, NSA_KV_HEADS, NSA_GROUP, HEAD_DIM) * (HEAD_DIM ** -0.5)
    kv_shape = (B, S, NSA_KV_HEADS, HEAD_DIM)
    kc, vc, ks, vs, kw, vw = [a.reshape(kv_shape) for a in (kc, vc, ks, vs, kw, vw)]
    gates = jax.nn.sigmoid(gate_logits.astype(f32)).reshape(B, S, NSA_KV_HEADS, NSA_GROUP, 3)
    slopes = alibi_slopes(NSA_HEADS).reshape(NSA_KV_HEADS, NSA_GROUP)

    k_cmp = compress_blocks(kc, cmp_pos_k, cmp_w1_k, cmp_w2_k)
    v_cmp = compress_blocks(vc, cmp_pos_v, cmp_w1_v, cmp_w2_v)
    n_cmp = k_cmp.shape[1]
    cmp_end = jnp.arange(n_cmp) * CMP_STRIDE + CMP_BLOCK - 1

    n_slc = S // SLC_BLOCK
    n_sel = min(N_SELECT, n_slc)
    cmp_tok = jnp.arange(n_cmp)[:, None] * CMP_STRIDE + jnp.arange(CMP_BLOCK)[None, :]
    overlap = jax.nn.one_hot(cmp_tok // SLC_BLOCK, n_slc, dtype=f32).sum(axis=1) / CMP_BLOCK

    ks_blk = ks.reshape(B, n_slc, SLC_BLOCK, NSA_KV_HEADS, HEAD_DIM).transpose(0, 3, 1, 2, 4)
    vs_blk = vs.reshape(B, n_slc, SLC_BLOCK, NSA_KV_HEADS, HEAD_DIM).transpose(0, 3, 1, 2, 4)
    kw_pad = jnp.pad(kw, ((0, 0), (WINDOW, 0), (0, 0), (0, 0)))
    vw_pad = jnp.pad(vw, ((0, 0), (WINDOW, 0), (0, 0), (0, 0)))
    b_ix = jnp.arange(B)[:, None, None, None]
    h_ix = jnp.arange(NSA_KV_HEADS)[None, :, None, None]
    forced_score = float(NSA_GROUP + 1)

    def query_block(i):
        t0 = i * NSA_QBLOCK
        qb = lax.dynamic_slice_in_dim(q, t0, NSA_QBLOCK, axis=1)
        gb = lax.dynamic_slice_in_dim(gates, t0, NSA_QBLOCK, axis=1)
        t = t0 + jnp.arange(NSA_QBLOCK)

        dist = (t[:, None] - cmp_end[None, :]).astype(f32)
        s = jnp.einsum('bqhgd,bnhd->bhgqn', qb, k_cmp).astype(f32)
        s = s - slopes[:, :, None, None] * dist
        p_cmp = masked_softmax(s, dist >= 0)
        o_cmp = jnp.einsum('bhgqn,bnhd->bqhgd', p_cmp.astype(v_cmp.dtype), v_cmp)

        imp = jnp.einsum('bhgqn,nj->bhqj', p_cmp, overlap)
        cur = t // SLC_BLOCK
        j = jnp.arange(n_slc)
        forced = (j[None, :] == 0) | (j[None, :] == cur[:, None]) | (j[None, :] == cur[:, None] - 1)
        future = j[None, :] > cur[:, None]
        imp = jnp.where(forced, forced_score, jnp.where(future, -1.0, imp))
        _, idx = lax.top_k(imp, n_sel)
        kg = ks_blk[b_ix, h_ix, idx]
        vg = vs_blk[b_ix, h_ix, idx]
        kpos = idx[..., None] * SLC_BLOCK + jnp.arange(SLC_BLOCK)
        dist = (t[:, None, None] - kpos).astype(f32)[:, :, None]
        s = jnp.einsum('bqhgd,bhqnld->bhgqnl', qb, kg).astype(f32)
        s = s - slopes[None, :, :, None, None, None] * dist
        n_keys = n_sel * SLC_BLOCK
        s = s.reshape(B, NSA_KV_HEADS, NSA_GROUP, NSA_QBLOCK, n_keys)
        mask = (dist >= 0).reshape(B, NSA_KV_HEADS, 1, NSA_QBLOCK, n_keys)
        p_slc = masked_softmax(s, mask)
        vg = vg.reshape(B, NSA_KV_HEADS, NSA_QBLOCK, n_keys, HEAD_DIM)
        o_slc = jnp.einsum('bhgqk,bhqkd->bqhgd', p_slc.astype(vg.dtype), vg)

        kwb = lax.dynamic_slice_in_dim(kw_pad, t0, NSA_QBLOCK + WINDOW, axis=1)
        vwb = lax.dynamic_slice_in_dim(vw_pad, t0, NSA_QBLOCK + WINDOW, axis=1)
        kpos = t0 - WINDOW + jnp.arange(NSA_QBLOCK + WINDOW)
        dist_i = t[:, None] - kpos[None, :]
        mask = (dist_i >= 0) & (dist_i < WINDOW) & (kpos[None, :] >= 0)
        s = jnp.einsum('bqhgd,bkhd->bhgqk', qb, kwb).astype(f32)
        s = s - slopes[:, :, None, None] * dist_i.astype(f32)
        p_win = masked_softmax(s, mask)
        o_win = jnp.einsum('bhgqk,bkhd->bqhgd', p_win.astype(vwb.dtype), vwb)

        return gb[..., 0:1] * o_cmp + gb[..., 1:2] * o_slc + gb[..., 2:3] * o_win

    out = lax.map(query_block, jnp.arange(S // NSA_QBLOCK))
    out = out.transpose(1, 0, 2, 3, 4, 5).reshape(B, S, NSA_WIDTH)
    return out.astype(q.dtype)

def gla(q, k, v, r, a_low, w_alpha2, b_alpha, norm_g):
    B, S = q.shape[:2]
    f32 = jnp.float32
    nc = S // GLA_CHUNK
    shp_k = (B, nc, GLA_CHUNK, GLA_HEADS, GLA_DK)
    shp_v = (B, nc, GLA_CHUNK, GLA_HEADS, GLA_DV)
    q = q.reshape(shp_k).astype(f32) * (GLA_DK ** -0.5)
    k = k.reshape(shp_k).astype(f32)
    v = v.reshape(shp_v).astype(f32)
    log_a = jax.nn.log_sigmoid((a_low @ w_alpha2 + b_alpha).astype(f32)) / GLA_TAU
    b = jnp.cumsum(log_a.reshape(shp_k), axis=2)
    b_last = b[:, :, -1:]
    q_d = q * jnp.exp(b)
    k_d = k * jnp.exp(-b)
    k_s = k * jnp.exp(b_last - b)
    causal = jnp.tril(jnp.ones((GLA_CHUNK, GLA_CHUNK), dtype=bool))
    att = jnp.where(causal, jnp.einsum('bnihd,bnjhd->bnhij', q_d, k_d), 0.0)
    o_intra = jnp.einsum('bnhij,bnjhe->bnihe', att, v)
    state_inc = jnp.einsum('bnjhd,bnjhe->bnhde', k_s, v)
    decay = jnp.exp(b_last[:, :, 0])

    def step(state, xs):
        dec, inc = xs
        return dec[..., None] * state + inc, state

    init = jnp.zeros((B, GLA_HEADS, GLA_DK, GLA_DV), f32)
    _, states = lax.scan(step, init, (decay.swapaxes(0, 1), state_inc.swapaxes(0, 1)))
    states = states.swapaxes(0, 1)
    o_inter = jnp.einsum('bnihd,bnhde->bnihe', q_d, states)
    o = (o_intra + o_inter).reshape(B, S, GLA_HEADS, GLA_DV)
    o = o * lax.rsqrt(jnp.mean(o * o, axis=-1, keepdims=True) + RMS_EPS) * norm_g.astype(f32)
    o = o * jax.nn.silu(r.reshape(B, S, GLA_HEADS, GLA_DV).astype(f32))
    return o.reshape(B, S, GLA_VAL_WIDTH).astype(r.dtype)

def memory_cross_attention(h, mem_n, w_xq, w_xkv, w_xo):
    B, S = h.shape[:2]
    M = mem_n.shape[1]
    q = (h @ w_xq).reshape(B, S, XATTN_HEADS, XATTN_HEAD_DIM) * (XATTN_HEAD_DIM ** -0.5)
    k, v = jnp.split(mem_n @ w_xkv, 2, axis=-1)
    k = k.reshape(B, M, XATTN_HEADS, XATTN_HEAD_DIM)
    v = v.reshape(B, M, XATTN_HEADS, XATTN_HEAD_DIM)
    p = jax.nn.softmax(jnp.einsum('bshd,bmhd->bhsm', q, k).astype(jnp.float32), axis=-1)
    o = jnp.einsum('bhsm,bmhd->bshd', p.astype(v.dtype), v).reshape(B, S, XATTN_WIDTH)
    return o @ w_xo

def conv_ffn(h, w_up, conv_w, conv_b, w_down):
    S = h.shape[1]
    u, g = jnp.split(h @ w_up, 2, axis=-1)
    u_pad = jnp.pad(u, ((0, 0), (CONV_WIDTH - 1, 0), (0, 0)))
    u = sum(conv_w[tap] * u_pad[:, tap:tap + S] for tap in range(CONV_WIDTH)) + conv_b
    return (jax.nn.gelu(u) * g) @ w_down

def first_inputs(seed: int = 0) -> dict:
    key = jax.random.key(seed)
    ks = jax.random.split(key, 28)
    f32 = jnp.float32
    L = DEPTH

    def dense(k, shape, fan_in):
        return jax.random.normal(k, shape, f32) * fan_in ** -0.5

    def gain(k, shape):
        return 1.0 + 0.02 * jax.random.normal(k, shape, f32)

    def small(k, shape, scale):
        return scale * jax.random.normal(k, shape, f32)

    return {
        "x": jax.random.normal(ks[0], (BATCH, SEQ, D_MODEL), f32),
        "mem": jax.random.normal(ks[1], (BATCH, MEM_LEN, D_MODEL), f32),
        "ln_mix_g": gain(ks[2], (L, D_MODEL)),
        "w_in": dense(ks[3], (L, D_MODEL, IN_WIDTH), D_MODEL),
        "nsa_gate_b": small(ks[4], (L, 3 * NSA_HEADS), 0.1),
        "cmp_pos_k": small(ks[5], (L, CMP_BLOCK, HEAD_DIM), 0.1),
        "cmp_w1_k": dense(ks[6], (L, CMP_BLOCK * HEAD_DIM, CMP_HIDDEN), CMP_BLOCK * HEAD_DIM),
        "cmp_w2_k": dense(ks[7], (L, CMP_HIDDEN, HEAD_DIM), CMP_HIDDEN),
        "cmp_pos_v": small(ks[8], (L, CMP_BLOCK, HEAD_DIM), 0.1),
        "cmp_w1_v": dense(ks[9], (L, CMP_BLOCK * HEAD_DIM, CMP_HIDDEN), CMP_BLOCK * HEAD_DIM),
        "cmp_w2_v": dense(ks[10], (L, CMP_HIDDEN, HEAD_DIM), CMP_HIDDEN),
        "gla_w_alpha2": dense(ks[11], (L, GLA_GATE_RANK, GLA_KEY_WIDTH), GLA_GATE_RANK),
        "gla_b_alpha": small(ks[12], (L, GLA_KEY_WIDTH), 0.1),
        "gla_norm_g": gain(ks[13], (L, GLA_DV)),
        "w_branch_nsa": dense(ks[14], (L, NSA_WIDTH, D_MODEL), NSA_WIDTH),
        "w_branch_gla": dense(ks[15], (L, GLA_VAL_WIDTH, D_MODEL), GLA_VAL_WIDTH),
        "w_out": dense(ks[16], (L, D_MODEL, D_MODEL), D_MODEL),
        "ln_x_g": gain(ks[17], (L, D_MODEL)),
        "ln_mem_g": gain(ks[18], (L, D_MODEL)),
        "w_xq": dense(ks[19], (L, D_MODEL, XATTN_WIDTH), D_MODEL),
        "w_xkv": dense(ks[20], (L, D_MODEL, 2 * XATTN_WIDTH), D_MODEL),
        "w_xo": dense(ks[21], (L, XATTN_WIDTH, D_MODEL), XATTN_WIDTH),
        "ln_ffn_g": gain(ks[22], (L, D_MODEL)),
        "w_up": dense(ks[23], (L, D_MODEL, 2 * FFN_DIM), D_MODEL),
        "conv_w": dense(ks[24], (L, CONV_WIDTH, FFN_DIM), CONV_WIDTH),
        "conv_b": small(ks[25], (L, FFN_DIM), 0.02),
        "w_down": dense(ks[26], (L, FFN_DIM, D_MODEL), FFN_DIM),
        "ln_final_g": gain(ks[27], (D_MODEL,)),
    }

def first_block(x, mem, ln_mix_g, w_in, nsa_gate_b, cmp_pos_k, cmp_w1_k, cmp_w2_k,
              cmp_pos_v, cmp_w1_v, cmp_w2_v, gla_w_alpha2, gla_b_alpha, gla_norm_g,
              w_branch_nsa, w_branch_gla, w_out, ln_x_g, ln_mem_g, w_xq, w_xkv, w_xo,
              ln_ffn_g, w_up, conv_w, conv_b, w_down, ln_final_g):
    split_points = np.cumsum(IN_SPLITS)[:-1].tolist()
    for l in range(DEPTH):
        h = rms_norm(x, ln_mix_g[l])
        q_a, kv_a, gate_a, q_b, k_b, v_b, r_b, alpha_b, merge = jnp.split(h @ w_in[l], split_points, axis=-1)
        kc, vc, ks_, vs_, kw, vw = jnp.split(kv_a, 6, axis=-1)
        o_nsa = nsa_attention(q_a, kc, vc, ks_, vs_, kw, vw, gate_a + nsa_gate_b[l],
                              cmp_pos_k[l], cmp_w1_k[l], cmp_w2_k[l],
                              cmp_pos_v[l], cmp_w1_v[l], cmp_w2_v[l])
        o_gla = gla(q_b, k_b, v_b, r_b, alpha_b, gla_w_alpha2[l], gla_b_alpha[l], gla_norm_g[l])
        g_nsa, g_gla = jnp.split(jax.nn.sigmoid(merge), 2, axis=-1)
        mix = g_nsa * (o_nsa @ w_branch_nsa[l]) + g_gla * (o_gla @ w_branch_gla[l])
        x = x + (mix @ w_out[l]).astype(x.dtype)
        mem_n = rms_norm(mem, ln_mem_g[l])
        x = x + memory_cross_attention(rms_norm(x, ln_x_g[l]), mem_n, w_xq[l], w_xkv[l], w_xo[l]).astype(x.dtype)
        x = x + conv_ffn(rms_norm(x, ln_ffn_g[l]), w_up[l], conv_w[l], conv_b[l], w_down[l]).astype(x.dtype)
    return rms_norm(x, ln_final_g)


DEPTH_2 = 2

N_MIXERS = 2
EPS = 1e-6
BLOCK = 128
RET_HEADS = D_MODEL // 256
RET_DK = 256
RET_DV = 2 * RET_DK
RET_QK = RET_HEADS * RET_DK
RET_V = RET_HEADS * RET_DV
RET_IN = 2 * RET_QK + 2 * RET_V
ROPE_BASE = 10000.0
SB_HEADS = D_MODEL // 64
SB_DH = 64
SB_IN = 3 * SB_HEADS * SB_DH
D_FF = 2816
CONV_W = 3


def _rmsnorm(x, g):
    xf = x.astype(jnp.float32)
    y = xf * lax.rsqrt(jnp.mean(xf * xf, axis=-1, keepdims=True) + EPS)
    return (y * g.astype(jnp.float32)).astype(x.dtype)

def _rotary(x, cos, sin):
    x1, x2 = jnp.split(x, 2, axis=-1)
    c = cos[None, :, None, :]
    s = sin[None, :, None, :]
    return jnp.concatenate([x1 * c - x2 * s, x1 * s + x2 * c], axis=-1)

def _retention(h, w_in, w_out):
    B_, S_, _ = h.shape
    nc = S_ // BLOCK
    proj = h @ w_in
    q, k, v, g = jnp.split(proj, [RET_QK, 2 * RET_QK, 2 * RET_QK + RET_V], axis=-1)
    pos = jnp.arange(S_, dtype=jnp.float32)
    inv_freq = ROPE_BASE ** (-jnp.arange(0, RET_DK, 2, dtype=jnp.float32) / RET_DK)
    ang = pos[:, None] * inv_freq[None, :]
    cos, sin = jnp.cos(ang), jnp.sin(ang)
    q = _rotary(q.reshape(B_, S_, RET_HEADS, RET_DK).astype(jnp.float32), cos, sin)
    k = _rotary(k.reshape(B_, S_, RET_HEADS, RET_DK).astype(jnp.float32), cos, sin) * (RET_DK ** -0.5)
    v = v.reshape(B_, S_, RET_HEADS, RET_DV).astype(jnp.float32)
    qc = q.transpose(0, 2, 1, 3).reshape(B_, RET_HEADS, nc, BLOCK, RET_DK)
    kc = k.transpose(0, 2, 1, 3).reshape(B_, RET_HEADS, nc, BLOCK, RET_DK)
    vc = v.transpose(0, 2, 1, 3).reshape(B_, RET_HEADS, nc, BLOCK, RET_DV)
    log_g = jnp.log(1.0 - 2.0 ** (-5.0 - jnp.arange(RET_HEADS, dtype=jnp.float32)))
    cpos = jnp.arange(BLOCK, dtype=jnp.float32)
    diff = cpos[:, None] - cpos[None, :]
    dmat = jnp.where(diff[None] >= 0,
                     jnp.exp(jnp.maximum(diff, 0.0)[None] * log_g[:, None, None]), 0.0)
    scores = jnp.einsum('bhncd,bhnkd->bhnck', qc, kc) * dmat[None, :, None]
    intra = jnp.einsum('bhnck,bhnke->bhnce', scores, vc)
    q_dec = qc * jnp.exp((cpos + 1.0)[None, :] * log_g[:, None])[None, :, None, :, None]
    k_dec = kc * jnp.exp((BLOCK - 1.0 - cpos)[None, :] * log_g[:, None])[None, :, None, :, None]
    chunk_decay = jnp.exp(BLOCK * log_g)[None, :, None, None]

    def step(state, xs):
        qd, kd, vv = xs
        out = jnp.einsum('bhcd,bhde->bhce', qd, state)
        state = chunk_decay * state + jnp.einsum('bhkd,bhke->bhde', kd, vv)
        return state, out

    state0 = jnp.zeros((B_, RET_HEADS, RET_DK, RET_DV), jnp.float32)
    _, cross = lax.scan(step, state0, (jnp.moveaxis(q_dec, 2, 0), jnp.moveaxis(k_dec, 2, 0),
                                       jnp.moveaxis(vc, 2, 0)))
    o = intra + jnp.moveaxis(cross, 0, 2)
    o = o.reshape(B_, RET_HEADS, S_, RET_DV)
    o = o * lax.rsqrt(jnp.mean(o * o, axis=-1, keepdims=True) + EPS)
    o = o.transpose(0, 2, 1, 3).reshape(B_, S_, RET_V)
    y = jax.nn.silu(g.astype(jnp.float32)) * o
    return y.astype(h.dtype) @ w_out

def _stick_breaking(h, w_in, w_out):
    B_, S_, _ = h.shape
    nb = S_ // BLOCK
    scale = 1.0 / math.sqrt(SB_DH)
    proj = h @ w_in
    q, k, v = jnp.split(proj, 3, axis=-1)
    to_heads = lambda a: a.reshape(B_, S_, SB_HEADS, SB_DH).transpose(0, 2, 1, 3).astype(jnp.float32)
    q, k, v = to_heads(q), to_heads(k), to_heads(v)
    outs = []
    for i in range(nb):
        qb = q[:, :, i * BLOCK:(i + 1) * BLOCK]
        t_pos = i * BLOCK + jnp.arange(BLOCK)
        kp = jnp.moveaxis(k[:, :, :(i + 1) * BLOCK].reshape(B_, SB_HEADS, i + 1, BLOCK, SB_DH), 2, 0)
        vp = jnp.moveaxis(v[:, :, :(i + 1) * BLOCK].reshape(B_, SB_HEADS, i + 1, BLOCK, SB_DH), 2, 0)

        def step(carry, xs, qb=qb, t_pos=t_pos):
            suffix, acc = carry
            kb, vb, j = xs
            z = jnp.einsum('bhqd,bhkd->bhqk', qb, kb) * scale
            s_pos = j * BLOCK + jnp.arange(BLOCK)
            mask = s_pos[None, :] < t_pos[:, None]
            log1m = jnp.where(mask, jax.nn.log_sigmoid(-z), 0.0)
            excl = lax.cumsum(log1m, axis=3, reverse=True) - log1m
            log_a = jax.nn.log_sigmoid(z) + excl + suffix[..., None]
            a = jnp.where(mask, jnp.exp(log_a), 0.0)
            acc = acc + jnp.einsum('bhqk,bhkd->bhqd', a, vb)
            suffix = suffix + jnp.sum(log1m, axis=3)
            return (suffix, acc), None

        init = (jnp.zeros((B_, SB_HEADS, BLOCK), jnp.float32),
                jnp.zeros((B_, SB_HEADS, BLOCK, SB_DH), jnp.float32))
        (_, acc), _ = lax.scan(step, init, (kp, vp, jnp.arange(i + 1)), reverse=True)
        outs.append(acc)
    o = jnp.concatenate(outs, axis=2)
    o = o.transpose(0, 2, 1, 3).reshape(B_, S_, SB_HEADS * SB_DH)
    return o.astype(h.dtype) @ w_out

def _conv_ffn(h, w_up, conv_w, conv_b, w_down):
    u = h @ w_up
    u = lax.conv_general_dilated(u, conv_w[:, None, :].astype(u.dtype), window_strides=(1,),
                                 padding=[(CONV_W - 1, 0)],
                                 dimension_numbers=('NWC', 'WIO', 'NWC'),
                                 feature_group_count=2 * D_FF) + conv_b
    gate, val = jnp.split(u, 2, axis=-1)
    return (jax.nn.silu(gate) * val) @ w_down

def second_inputs(seed: int = 0) -> dict:
    key = jax.random.key(seed)
    ks = jax.random.split(key, 16)
    n_ret = (DEPTH_2 + 1) // 2
    n_sb = DEPTH_2 // 2
    nrm = lambda k, shape, fan_in: jax.random.normal(k, shape, jnp.float32) * fan_in ** -0.5
    gain = lambda k, shape: 1.0 + 0.02 * jax.random.normal(k, shape, jnp.float32)
    return {
        "x": jax.random.normal(ks[0], (BATCH, SEQ, D_MODEL), jnp.float32),
        "ret_norm": gain(ks[1], (n_ret, D_MODEL)),
        "ret_w_in": nrm(ks[2], (n_ret, D_MODEL, RET_IN), D_MODEL),
        "ret_w_out": nrm(ks[3], (n_ret, RET_V, D_MODEL), RET_V),
        "sb_norm": gain(ks[4], (n_sb, D_MODEL)),
        "sb_w_in": nrm(ks[5], (n_sb, D_MODEL, SB_IN), D_MODEL),
        "sb_w_out": nrm(ks[6], (n_sb, SB_HEADS * SB_DH, D_MODEL), SB_HEADS * SB_DH),
        "ffn_norm": gain(ks[7], (DEPTH_2, D_MODEL)),
        "ffn_w_up": nrm(ks[8], (DEPTH_2, D_MODEL, 2 * D_FF), D_MODEL),
        "ffn_conv_w": nrm(ks[9], (DEPTH_2, CONV_W, 2 * D_FF), CONV_W),
        "ffn_conv_b": 0.02 * jax.random.normal(ks[10], (DEPTH_2, 2 * D_FF), jnp.float32),
        "ffn_w_down": nrm(ks[11], (DEPTH_2, D_FF, D_MODEL), D_FF),
        "final_norm": gain(ks[12], (D_MODEL,)),
    }

def second_block(x, ret_norm, ret_w_in, ret_w_out, sb_norm, sb_w_in, sb_w_out,
              ffn_norm, ffn_w_up, ffn_conv_w, ffn_conv_b, ffn_w_down, final_norm):
    for i in range(DEPTH_2):
        j = i // N_MIXERS
        if i % N_MIXERS == 0:
            x = x + _retention(_rmsnorm(x, ret_norm[j]), ret_w_in[j], ret_w_out[j])
        else:
            x = x + _stick_breaking(_rmsnorm(x, sb_norm[j]), sb_w_in[j], sb_w_out[j])
        x = x + _conv_ffn(_rmsnorm(x, ffn_norm[i]), ffn_w_up[i], ffn_conv_w[i],
                          ffn_conv_b[i], ffn_w_down[i])
    return _rmsnorm(x, final_norm)


def setup_inputs(seed=0):
    out = dict(first_inputs(seed))
    for name, value in second_inputs(seed + 1).items():
        if name != "x":
            out[name + "_2"] = value
    return out


def reference(
    x, mem, ln_mix_g, w_in, nsa_gate_b, cmp_pos_k, cmp_w1_k, cmp_w2_k, cmp_pos_v, cmp_w1_v,
    cmp_w2_v, gla_w_alpha2, gla_b_alpha, gla_norm_g, w_branch_nsa, w_branch_gla, w_out, ln_x_g,
    ln_mem_g, w_xq, w_xkv, w_xo, ln_ffn_g, w_up, conv_w, conv_b, w_down, ln_final_g, ret_norm_2,
    ret_w_in_2, ret_w_out_2, sb_norm_2, sb_w_in_2, sb_w_out_2, ffn_norm_2, ffn_w_up_2,
    ffn_conv_w_2, ffn_conv_b_2, ffn_w_down_2, final_norm_2,
):
    x = first_block(
        x, mem, ln_mix_g, w_in, nsa_gate_b, cmp_pos_k, cmp_w1_k, cmp_w2_k, cmp_pos_v, cmp_w1_v,
        cmp_w2_v, gla_w_alpha2, gla_b_alpha, gla_norm_g, w_branch_nsa, w_branch_gla, w_out,
        ln_x_g, ln_mem_g, w_xq, w_xkv, w_xo, ln_ffn_g, w_up, conv_w, conv_b, w_down, ln_final_g,
    )
    return second_block(
        x, ret_norm_2, ret_w_in_2, ret_w_out_2, sb_norm_2, sb_w_in_2, sb_w_out_2, ffn_norm_2,
        ffn_w_up_2, ffn_conv_w_2, ffn_conv_b_2, ffn_w_down_2, final_norm_2,
    )


_drawn_inputs = setup_inputs


def setup_inputs(seed=0):
    import zlib

    import numpy as np

    out = dict(_drawn_inputs(seed))
    spreads = {}
    factors = {'nsa_gate_b': 4.388,
     'cmp_pos_k': 8.0,
     'gla_norm_g': 4.832,
     'ln_x_g': 8.0,
     'ln_mem_g': 8.0,
     'conv_b': 3.3,
     'sb_norm_2': 5.123,
     'ffn_norm_2': 3.049,
     'ffn_conv_b_2': 3.1,
     'final_norm_2': 7.974,
     'ln_ffn_g': 4.583}
    for name, (base, spread) in spreads.items():
        noise = np.random.default_rng([zlib.crc32(name.encode()), seed]).standard_normal(out[name].shape)
        drawn = base * np.exp(spread * noise) if base else spread * noise
        out[name] = __import__('jax').numpy.asarray(drawn.astype(out[name].dtype))
    for name, factor in factors.items():
        out[name] = (out[name] * factor).astype(out[name].dtype)
    return out
```

```python
from contextlib import ExitStack

import numpy as np

import concourse.bass as bass
from concourse import mybir

ALU = mybir.AluOpType
ACT = mybir.ActivationFunctionType
F32 = mybir.dt.float32
F32R = mybir.dt.float32r
AX_X = mybir.AxisListType.X

P = 128
SEQ = 512
D = 1024
MEM = 256
KT = D // P
TT = SEQ // P
FFN = 2816
FT = FFN // P
HEADS = 8
KVH = 2
GRP = HEADS // KVH
HD = 64
NCMP = SEQ // 16 - 1
CMPB = 32
WIN = 256
GH = 4
CH = 64
NCH = SEQ // CH
XH = 4
RH = 4
SH = 16
EPS = 1e-6
MASKED = -1e30
FAR = 40.0

C_Q, C_KV, C_GATE, C_QB = 0, 512, 1280, 1304
C_VB, C_RB, C_AL, C_MERGE = C_QB + 512, C_QB + 1024, C_QB + 1536, C_QB + 1552
TOKW = 2 * P + 3 * HEADS + 16

RING = 4
RAW_RING = 4


class Chain:

    def __init__(self, eng, sem):
        self.eng, self.sem, self.n, self.i, self.per, self.used = eng, sem, 0, None, 0, 0

    def value(self):
        if self.i is None:
            return self.n
        return self.i * self.per + (self.n + self.used)

    def mark(self, ins):
        if self.i is None:
            self.n += 1
        else:
            self.used += 1
        ins.then_inc(self.sem, 1)
        return self.value()

    def wait(self):
        self.eng.wait_ge(self.sem, self.value())

    def __call__(self, ins):
        self.mark(ins)
        self.wait()

    def loop(self, count, per):
        with self.eng.Fori(0, count) as i:
            self.i, self.per, self.used = i, per, 0
            yield i
            assert self.used == per, (self.used, per)
        self.n += count * per
        self.i = None


NSA = [(qt, h) for qt in range(TT) for h in range(HEADS)]
SLOPES = [2.0 ** -(h + 1) for h in range(HEADS)]
SH_D = 64
SB = [(pair, j, e) for pair in range(4) for j in reversed(range(TT)) for e in range(2)]
ROWS = (83, 4 * FT, 4 * FT, 4 * FT, 4 * FT, 4 * FT)
N_ROW_LOADS = 12 + 5 * 4
RET_DECAY = [1.0 - 2.0 ** (-5 - h) for h in range(RH)]

V_GAIN, V_BALPHA, V_GLAG = 0, 80, 82
NORMS = ("ln_mix_g", "ln_mem_g", "ln_x_g", "ln_ffn_g", "ln_final_g",
         "ret_norm_2", "ffn_norm_2a", "sb_norm_2", "ffn_norm_2b", "final_norm_2")

GROUPS = ([("q", 4), ("kv", 4), ("tok", 4), ("qkb", 4), ("vb", 4), ("rb", 4)]
          + [(n + str(h), s) for h in range(2) for n, s in (("mn", 4), ("mg", 4), ("bn", 2), ("bg", 2))]
          + [("out0", 4), ("out1", 4), ("xk", 4), ("xv", 4), ("xq", 4), ("xo0", 2), ("xo1", 2)]
          + [(f"up1_{n}", 4) for n in range(11)] + [("down1_0", 11), ("down1_1", 11)]
          + [(f"{n}{h}", 4) for h in range(RH) for n in ("rqk", "rv", "rg")]
          + [("ro0", 8), ("ro1", 8)]
          + [(f"up2_{n}", 4) for n in range(11)] + [("down2_0", 11), ("down2_1", 11)]
          + [(f"{n}{h}", 4) for h in range(2) for n in ("sq", "sk", "sv")]
          + [("so0", 4), ("so1", 4)]
          + [(f"up3_{n}", 4) for n in range(11)] + [("down3_0", 11), ("down3_1", 11)])
GIDX = {n: i for i, (n, _) in enumerate(GROUPS)}
SLOT0 = [0]
for _n, _s in GROUPS:
    SLOT0.append(SLOT0[-1] + _s)
N_SLOTS = SLOT0[-1]
FIRST_PIECED = 12


def build(nc, a, out):
    with ExitStack() as ctx:
        def sb(name, shape, dt=F32, stack=ctx):
            return stack.enter_context(nc.sbuf_tensor(name, shape, dt))

        def sem(name):
            return ctx.enter_context(nc.semaphore(name))

        ps = ctx.enter_context(nc.psum_tensor("ps", [P, 8, 512], F32))
        x = sb("x", [P, KT, SEQ])
        h_hi = sb("h_hi", [P, KT, SEQ], F32R)
        h_lo = sb("h_lo", [P, KT, SEQ], F32R)
        w_raw = sb("w_raw", [P, RAW_RING, 2, 512])
        w_hi = sb("w_hi", [P, RING, 2, 512], F32R)
        w_lo = sb("w_lo", [P, RING, 2, 512], F32R)
        ident = sb("ident", [P, P])
        mean = sb("mean", [P, P])
        vecs = sb("vecs", [P, 6, 4 * FT])
        rstd = sb("rstd", [P, SEQ])
        eps = sb("eps", [P, 1])
        zero = sb("zero", [P, 1])
        sq = sb("sq", [P, 2, SEQ])
        full = sb("full", [P, 2, SEQ])

        with ExitStack() as m:
            o_hi = sb("o_hi", [P, 8, SEQ], F32R, m)
            o_lo = sb("o_lo", [P, 8, SEQ], F32R, m)
            with ExitStack() as m1:
                tok = sb("tok", [P, TT, TOKW], F32, m1)
                gates = sb("gates", [P, TT, 3 * HEADS], F32, m1)
                gate_b = sb("gate_b", [P, 3 * HEADS], F32, m1)
                qkb = sb("qkb", [P, 4, SEQ], F32, m1)
                vb = sb("vb", [P, TT, 512], F32, m1)
                d_slc = sb("d_slc", [P, SEQ], F32, m1)
                d_win = sb("d_win", [P, WIN + P], F32, m1)
                d_cmp = sb("d_cmp", [P, TT, 32], F32, m1)
                row_ok = sb("row_ok", [P, 1], F32, m1)
                keep = sb("keep", [P, SEQ], F32, m1)
                attT = sb("attT", [P, 2, P], F32, m1)
                caus = sb("caus", [P, CH], F32, m1)
                with ExitStack() as m2:
                    qT = sb("qT", [P, 4, SEQ], F32, m2)
                    kvT = sb("kvT", [P, 4, SEQ], F32, m2)
                    kcT = sb("kcT", [P, 32], F32, m2)
                    vc = sb("vc", [32, KVH, HD], F32, m2)
                    s_buf = sb("s_buf", [P, 2, 928], F32, m2)
                    pT_buf = sb("pT_buf", [P, 2, 8, P], F32, m2)
                    att_st = sb("att_st", [P, 2, 16], F32, m2)
                with ExitStack() as m2:
                    rT = sb("rT", [P, GH, SEQ], F32, m2)
                    alT = sb("alT", [16, SEQ], F32, m2)
                    wal = sb("wal", [16, 256], F32, m2)
                    la = sb("la", [P, SEQ], F32, m2)
                    bcum = sb("bcum", [P, SEQ], F32, m2)
                    ebuf = sb("ebuf", [P, SEQ], F32, m2)
                    ks_t = sb("ks_t", [P, SEQ], F32, m2)
                    ks_tok = sb("ks_tok", [P, TT, P], F32, m2)
                    kd = sb("kd", [P, SEQ], F32, m2)
                    qd = sb("qd", [P, SEQ], F32, m2)
                    dec = sb("dec", [P, NCH], F32, m2)
                    states = sb("states", [P, NCH, P], F32, m2)
            with ExitStack() as m1:
                gN = sb("gN", [P, 4, SEQ], F32, m1)
                gG = sb("gG", [P, 4, SEQ], F32, m1)
                mx_hi = sb("mx_hi", [P, KT, SEQ], F32R, m1)
                mx_lo = sb("mx_lo", [P, KT, SEQ], F32R, m1)
        with ExitStack() as m:
            w1c = sb("w1c", [P, CMPB, P], F32, m)
            w2k = sb("w2k", [P, P], F32, m)
            w2v = sb("w2v", [P, HD], F32, m)
            pos = sb("pos", [CMPB, 2, P], F32, m)
            posT = sb("posT", [P, 2, CMPB], F32, m)
            blk = sb("blk", [P, CMPB, 32], F32, m)
            hid = sb("hid", [P, 2, KVH, 32], F32, m)
        with ExitStack() as m:
            rows_in = sb("rows_in", [P, 6, P], F32, m)
            x_tok = sb("x_tok", [P, TT, D], F32, m)
        with ExitStack() as m:
            mem_tok = sb("mem_tok", [P, MEM // P, D], F32, m)
            memT = sb("memT", [P, KT, MEM], F32, m)
            m_hi = sb("m_hi", [P, KT, MEM], F32R, m)
            m_lo = sb("m_lo", [P, KT, MEM], F32R, m)
            xkT = sb("xkT", [P, XH, MEM], F32, m)
            xv = sb("xv", [P, MEM // P, 512], F32, m)
            xqT = sb("xqT", [P, XH, SEQ], F32, m)
            xo_hi = sb("xo_hi", [P, XH, SEQ], F32R, m)
            xo_lo = sb("xo_lo", [P, XH, SEQ], F32R, m)
            xp = sb("xp", [P, 2, MEM], F32, m)
            xpT = sb("xpT", [P, 2, 2, P], F32, m)
            x_st = sb("x_st", [P, 2, 4], F32, m)
        with ExitStack() as m:
            f_hi = sb("f_hi", [P, FT, SEQ], F32R, m)
            f_lo = sb("f_lo", [P, FT, SEQ], F32R, m)
            cu = sb("cu", [P, 2, SEQ], F32, m)
            cv = sb("cv", [P, 2, SEQ], F32, m)
        with ExitStack() as m:
            y_hi = sb("y_hi", [P, 16, SEQ], F32R, m)
            y_lo = sb("y_lo", [P, 16, SEQ], F32R, m)
            rq = sb("rq", [P, 4, SEQ], F32, m)
            rv = sb("rv", [P, TT, 512], F32, m)
            cosT = sb("cosT", [P, SEQ], F32, m)
            sinT = sb("sinT", [P, SEQ], F32, m)
            dmat = sb("dmat", [P, SEQ], F32, m)
            r1 = sb("r1", [P, 2, SEQ], F32, m)
            with ExitStack() as m1:
                rsc = sb("rsc", [P, TT, SEQ], F32, m1)
            with ExitStack() as m1:
                ro = sb("ro", [P, 4, SEQ], F32, m1)
        with ExitStack() as m:
            so_hi = sb("so_hi", [P, 8, SEQ], F32R, m)
            so_lo = sb("so_lo", [P, 8, SEQ], F32R, m)
            sqT = sb("sqT", [P, 4, SEQ], F32, m)
            skT = sb("skT", [P, 4, SEQ], F32, m)
            sv = sb("sv", [P, TT, 512], F32, m)
            s_ez = sb("s_ez", [P, 2, SEQ], F32, m)
            s_sp = sb("s_sp", [P, 2, SEQ], F32, m)
            s_sum = sb("s_sum", [P, 2, SEQ], F32, m)
            s_a = sb("s_a", [P, 2, SEQ], F32, m)
            strict = sb("strict", [P, P], F32, m)
            neg_tri = sb("neg_tri", [P, P], F32, m)
            neg_one = sb("neg_one", [P, P], F32, m)
            unseen_f = sb("unseen_f", [P, P], F32, m)
            unseen = sb("unseen", [P, P], F32R, m)
            ident_r = sb("ident_r", [P, P], F32R, m)
        with ExitStack() as m:
            o_tok = sb("o_tok", [P, TT, D], F32, m)

        raw_loaded = [sem(f"raw_loaded{j}") for j in range(RAW_RING)]
        raw_free = sem("raw_free")
        hi_written = sem("hi_written")
        slot_used = sem("slot_used")
        set_free = [sem("set_free0"), sem("set_free1")]
        in_loaded = sem("in_loaded")
        rows_loaded = sem("rows_loaded")
        gate_loaded = sem("gate_loaded")
        wal_loaded = sem("wal_loaded")
        cw_loaded = sem("cw_loaded")
        cw1_loaded = sem("cw1_loaded")
        cw2_loaded = sem("cw2_loaded")
        mem_loaded = sem("mem_loaded")
        rope_loaded = sem("rope_loaded")
        dmat_loaded = sem("dmat_loaded")
        const_ready = sem("const_ready")
        pool_order = sem("pool_order")
        act_order = sem("act_order")
        dve_order = sem("dve_order")
        turned = sem("turned")
        turned_read = sem("turned_read")
        mem_turned_read = sem("mem_turned_read")
        x_ready = sem("x_ready")
        fin_ready = sem("fin_ready")
        sq_ready = sem("sq_ready")
        sq_used = sem("sq_used")
        root_ready = sem("root_ready")
        rstd_ready = sem("rstd_ready")
        full_ready = sem("full_ready")
        full_hi = sem("full_hi")
        split_ready = sem("split_ready")
        gate_a = sem("gate_a")
        gate_s = sem("gate_s")
        gate_m = sem("gate_m")
        cmp_pe = sem("cmp_pe")
        cmp_blk = sem("cmp_blk")
        cmp_a = sem("cmp_a")
        cmp_b = sem("cmp_b")
        att_s = sem("att_s")
        att_m = sem("att_m")
        att_n = sem("att_n")
        att_e = sem("att_e")
        att_p = sem("att_p")
        att_t = sem("att_t")
        att_c = sem("att_c")
        att_o = sem("att_o")
        att_h = sem("att_h")
        att_r = sem("att_r")
        gla_pe = sem("gla_pe")
        gla_al = sem("gla_al")
        gla_lg = sem("gla_lg")
        gla_x = sem("gla_x")
        gla_v = sem("gla_v")
        gla_ks = sem("gla_ks")
        gla_kt = sem("gla_kt")
        gla_qk = sem("gla_qk")
        gla_st = sem("gla_st")
        gla_sc = sem("gla_sc")
        gla_at = sem("gla_at")
        gla_o = sem("gla_o")
        gla_sq = sem("gla_sq")
        gla_sum = sem("gla_sum")
        gla_rd = sem("gla_rd")
        merged = sem("merged")
        sig_n = sem("sig_n")
        sig_g = sem("sig_g")
        xat_s = sem("xat_s")
        xat_m = sem("xat_m")
        xat_e = sem("xat_e")
        xat_p = sem("xat_p")
        xat_t = sem("xat_t")
        xat_c = sem("xat_c")
        xat_o = sem("xat_o")
        xat_h = sem("xat_h")
        xat_r = sem("xat_r")
        conv_a = sem("conv_a")
        conv_d = sem("conv_d")
        nonlin = sem("nonlin")
        rope_d = sem("rope_d")
        ret_s = sem("ret_s")
        ret_sc = sem("ret_sc")
        ret_o = sem("ret_o")
        ret_cp = sem("ret_cp")
        ret_q = sem("ret_q")
        ret_m = sem("ret_m")
        ret_si = sem("ret_si")
        st_z = sem("st_z")
        st_min = sem("st_min")
        st_l = sem("st_l")
        st_sp = sem("st_sp")
        st_acc = sem("st_acc")
        st_up = sem("st_up")
        st_ex = sem("st_ex")
        st_o = sem("st_o")
        sb_h = sem("sb_h")
        sb_r = sem("sb_r")
        stored = sem("stored")

        block = ctx.enter_context(nc.Block())

        def gain(n, k):
            return vecs[:, 0, 8 * n + k:8 * n + k + 1]

        def bank(n, j):
            return ps[:, 4 * (n % 2) + j, :]

        def vec(r, col):
            return vecs[:, r, col:col + 1] if isinstance(col, int) else vecs[:, r, bass.ds(col, 1)]

        def f_tile(f, t):
            return f[:, t, :] if isinstance(t, int) else f[:, bass.ds(t, 1), :].rearrange("p a n -> p (a n)")

        def inc_at(c):
            u = c // 2
            return ps[:, 2 + 2 * (c % 2) + u // 2, 256 * (u % 2):256 * (u % 2) + 256]

        def updates(half, it):
            pair, j, e = SB[it]
            return 24 * half + 6 * pair + (2 * (TT - 1 - j) + e + 1 if j else 6)

        CONV0 = {1: 0, 2: 2 * 11, 3: 6 * 11}

        SPLITS = {}
        n_split = 0
        for what, n in (("mix", 8), ("gla", 4), ("mx", 8), ("mem", 8), ("xn", 8), ("ffn1n", 8), ("ffn1", FT), ("retn", 8), ("ret", 16),
                        ("ffn2n", 8), ("ffn2", FT), ("sbn", 8), ("ffn3n", 8), ("ffn3", FT)):
            SPLITS[what] = n_split
            n_split += n

        NORM_ORDER = ["mix", "mem", "xn", "ffn1n", "fin1", "retn", "ffn2n", "sbn", "ffn3n", "fin"]
        NORM_AT = {n: i for i, n in enumerate(NORM_ORDER)}
        GAIN_OF = {"mix": 0, "mem": 1, "xn": 2, "ffn1n": 3, "fin1": 4, "retn": 5, "ffn2n": 6,
                   "sbn": 7, "ffn3n": 8, "fin": 9}
        ROOTS = ["mix", "gla0", "gla1", "gla2", "gla3", "mem", "xn", "ffn1n", "fin1", "retn",
                 "ret0", "ret1", "ret2", "ret3", "ffn2n", "sbn", "ffn3n", "fin"]
        ROOT_AT = {n: i for i, n in enumerate(ROOTS)}
        X_AT = {"mix": 0, "xn": 8, "ffn1n": 16, "fin1": 24, "retn": 32, "ffn2n": 40, "sbn": 48,
                "ffn3n": 56, "fin": 64}
        NORM_BANK = {"mix": 7, "mem": 7, "xn": 7, "ffn1n": 7, "fin1": 7, "retn": 7, "ffn2n": 7,
                     "sbn": 7, "ffn3n": 7, "fin": 7}

        @block.sync
        def _(sp):
            x2 = a["x"][0].rearrange("(t p) d -> p t d", p=P)
            for t in range(TT):
                sp.dma_start(x_tok[:, t, :], x2[:, t, :]).then_inc(in_loaded, 16)

            w_in = a["w_in"][0]
            w4 = w_in.rearrange("(k p) n -> p k n", p=P)
            for g in range(FIRST_PIECED):
                if g >= RAW_RING:
                    sp.wait_ge(raw_free, g - RAW_RING + 1)
                k0, j = 2 * (g % 4), g % RAW_RING
                if g < 4:
                    for k in range(2):
                        src = w4[:, k0 + k, C_Q:C_Q + 512].rearrange("p (a i d) -> p i a d", a=2, i=4)
                        for b in range(2):
                            dst = w_raw[:, j, k, :].rearrange("p (i a d) -> p i a d", a=2, i=4)
                            sp.dma_start(dst[:, :, b, :], src[:, :, b, :]).then_inc(raw_loaded[j], 16)
                elif g < 8:
                    for dst0, c0, n in ((0, C_KV, 384), (384, C_KV + 512, 128)):
                        for k in range(2):
                            sp.dma_start(w_raw[:, j, k, dst0:dst0 + n], w4[:, k0 + k, c0:c0 + n])\
                                .then_inc(raw_loaded[j], 16)
                else:
                    for dst0, c0, n in ((0, C_KV + 384, 128), (128, C_KV + 640, 128),
                                        (256, C_GATE, 24), (280, C_AL, 16)):
                        sp.dma_start(w_raw[:, j, :, dst0:dst0 + n], w4[:, k0:k0 + 2, c0:c0 + n])\
                            .then_inc(raw_loaded[j], 16)

            def load(g, first, src):
                j = g % RAW_RING
                sp.wait_ge(raw_free, first - RAW_RING + 1)
                for kk in range(2):
                    dst = w_raw[:, j, kk, :]
                    piece = src(kk)
                    if len(piece.shape) == 3:
                        dst = dst.rearrange("p (a n) -> p a n", a=2)
                    sp.dma_start(dst, piece).then_inc(raw_loaded[j], 16)

            def square(g, w, c0, nk=KT):
                wk = w.rearrange("(k p) n -> p k n", p=P)
                for k0 in range(0, nk, 2):
                    load(g, g, lambda kk: wk[:, k0 + kk, c0:c0 + 512])
                    g += 1
                return g

            def squares(g, w, c0, count):
                wk = w.rearrange("(k p) n -> p k n", p=P)
                with sp.Fori(0, count) as i:
                    for k in range(4):
                        load(g + k, i * 4 + (g + k),
                             lambda kk: wk[:, 2 * k + kk, bass.ds(i * 512 + c0, 512)])
                return g + 4 * count

            g = FIRST_PIECED
            g = square(g, w_in, C_QB)
            g = square(g, w_in, C_VB)
            g = square(g, w_in, C_RB)
            for h in range(2):
                g = square(g, w_in, C_MERGE + 512 * h)
                g = square(g, w_in, C_MERGE + D + 512 * h)
                g = square(g, a["w_branch_nsa"][0], 512 * h, 4)
                g = square(g, a["w_branch_gla"][0], 512 * h, 4)
            g = squares(g, a["w_out"][0], 0, 2)
            g = squares(g, a["w_xkv"][0], 0, 2)
            g = square(g, a["w_xq"][0], 0)
            for h in range(2):
                g = square(g, a["w_xo"][0], 512 * h, 4)

            def ffn(g, up, down):
                up4 = up.rearrange("(k p) (a n) -> p k a n", p=P, a=2)
                with sp.Fori(0, FT // 2) as i:
                    for k in range(4):
                        load(g + k, i * 4 + (g + k),
                             lambda kk: up4[:, 2 * k + kk, :, bass.ds(i * 256, 256)])
                g += 2 * FT
                for h in range(2):
                    g = square(g, down, 512 * h, FT)
                return g

            g = ffn(g, a["w_up"][0], a["w_down"][0])
            assert g == SLOT0[GIDX["rqk0"]]
            w = a["ret_w_in_2"][0]
            wqk = w[:, 0:2 * D].rearrange("(k p) (a n) -> p k a n", p=P, a=2)
            wk = w.rearrange("(k p) n -> p k n", p=P)
            with sp.Fori(0, RH) as i:
                for k in range(4):
                    load(g + k, i * 12 + (g + k),
                         lambda kk: wqk[:, 2 * k + kk, :, bass.ds(i * 256, 256)])
                for b in range(2):
                    for k in range(4):
                        g2 = g + 4 + 4 * b + k
                        load(g2, i * 12 + g2,
                             lambda kk: wk[:, 2 * k + kk, bass.ds(i * 512 + (2 * D + 2 * D * b), 512)])
            g += 12 * RH
            for h in range(2):
                g = square(g, a["ret_w_out_2"][0], 512 * h, 16)
            g = ffn(g, a["ffn_w_up_2"][0], a["ffn_w_down_2"][0])
            wk2 = a["sb_w_in_2"][0].rearrange("(k p) n -> p k n", p=P)
            with sp.Fori(0, 2) as i:
                for b in range(3):
                    for k in range(4):
                        g2 = g + 4 * b + k
                        load(g2, i * 12 + g2,
                             lambda kk: wk2[:, 2 * k + kk, bass.ds(i * 512 + D * b, 512)])
            g += 24
            g = squares(g, a["sb_w_out_2"][0], 0, 2)
            g = ffn(g, a["ffn_w_up_2"][1], a["ffn_w_down_2"][1])
            assert g == N_SLOTS
            out2 = out[0].rearrange("(t p) d -> p t d", p=P)
            for t in range(TT):
                sp.wait_ge(turned_read, 2 * t + 3)
                sp.dma_start(out2[:, t, :], o_tok[:, t, :]).then_inc(stored, 16)
            sp.wait_ge(stored, 16 * TT)

        @block.gpsimd
        def _(pool):
            order = Chain(pool, pool_order)
            order.mark(nc.gpsimd.memset(ident[:], 0.0))
            order.mark(nc.gpsimd.memset(eps[:], EPS))
            order.mark(nc.gpsimd.memset(zero[:], 0.0))
            order(nc.gpsimd.memset(mean[:], 1.0 / D))
            order(nc.gpsimd.affine_select(out=ident[:], in_=ident[:], compare_op=ALU.not_equal, fill=1.0,
                                          base=0, pattern=[[-1, P]], channel_multiplier=1))
            pool.sem_inc(const_ready, 1)

            def split(j, r, first, loaded):
                pool.wait_ge(raw_loaded[r], loaded)
                if not isinstance(first, int) or first >= RING:
                    pool.wait_ge(slot_used, first - RING + 1)
                nc.gpsimd.tensor_tensor(w_hi[:, j], w_raw[:, r], zero[:].unsqueeze(1).to_broadcast([P, 2, 512]),
                                        ALU.add).then_inc(hi_written, 1)
                pool.wait_ge(hi_written, first + 1)
                nc.gpsimd.tensor_tensor(w_lo[:, j], w_raw[:, r], w_hi[:, j].bitcast(F32), ALU.subtract)\
                    .then_inc(raw_free, 1)

            def split_tok(j, r, first, loaded):
                pool.wait_ge(raw_loaded[r], loaded)
                pool.wait_ge(slot_used, first - RING + 1)
                nc.gpsimd.tensor_tensor(w_hi[:, j, :, 0:TOKW], w_raw[:, r, :, 0:TOKW],
                                        zero[:].unsqueeze(1).to_broadcast([P, 2, TOKW]),
                                        ALU.add).then_inc(hi_written, 1)
                pool.wait_ge(hi_written, first + 1)
                nc.gpsimd.tensor_tensor(w_lo[:, j, :, 0:TOKW], w_raw[:, r, :, 0:TOKW],
                                        w_hi[:, j, :, 0:TOKW].bitcast(F32), ALU.subtract).then_inc(raw_free, 1)

            for g in range(4):
                split(g % RING, g % RAW_RING, g, 64 * (g // RAW_RING + 1))
            order.mark(nc.gpsimd.iota(d_slc[:], pattern=[[1, SEQ]], base=-(SEQ - P), channel_multiplier=-1,
                                      allow_small_or_imprecise_dtypes=True))
            order.mark(nc.gpsimd.iota(d_win[:], pattern=[[1, WIN + P]], base=-WIN, channel_multiplier=-1,
                                      allow_small_or_imprecise_dtypes=True))
            order.mark(nc.gpsimd.iota(d_cmp[:], pattern=[[-P, TT], [16, 32]], base=CMPB - 1, channel_multiplier=-1,
                                      allow_small_or_imprecise_dtypes=True))
            order.mark(nc.gpsimd.memset(row_ok[:], 1.0))
            order(nc.gpsimd.memset(keep[:], 1.0))
            order.mark(nc.gpsimd.affine_select(out=d_slc[:], in_=d_slc[:], compare_op=ALU.is_ge, fill=MASKED,
                                               base=SEQ - P, pattern=[[-1, SEQ]], channel_multiplier=1))
            order.mark(nc.gpsimd.affine_select(out=d_win[:], in_=d_win[:], compare_op=ALU.is_ge, fill=MASKED,
                                               base=WIN, pattern=[[-1, WIN + P]], channel_multiplier=1))
            order.mark(nc.gpsimd.affine_select(out=d_cmp[:], in_=d_cmp[:], compare_op=ALU.is_ge, fill=MASKED,
                                               base=-(CMPB - 1), pattern=[[P, TT], [-16, 32]],
                                               channel_multiplier=1))
            order(nc.gpsimd.affine_select(out=row_ok[:], in_=row_ok[:], compare_op=ALU.is_ge, fill=0.0,
                                          base=-(CMPB - 1), pattern=[[0, 1]], channel_multiplier=1))
            order.mark(nc.gpsimd.affine_select(out=d_win[:], in_=d_win[:], compare_op=ALU.is_ge, fill=MASKED,
                                               base=-1, pattern=[[1, WIN + P]], channel_multiplier=-1))
            order.mark(nc.gpsimd.affine_select(out=keep[:], in_=keep[:], compare_op=ALU.not_equal, fill=0.0,
                                               base=0, pattern=[[0, NCH], [1, CH]], channel_multiplier=0))
            order(nc.gpsimd.memset(attT[:], 0.0))
            for e in range(2):
                order.mark(nc.gpsimd.memset(caus[64 * e:64 * e + 64, :], 1.0))
            order.wait()
            for e in range(2):
                order.mark(nc.gpsimd.affine_select(out=caus[64 * e:64 * e + 64, :], in_=caus[64 * e:64 * e + 64, :],
                                                   compare_op=ALU.is_ge, fill=0.0, base=0, pattern=[[1, CH]],
                                                   channel_multiplier=-1))
            order.wait()
            pool.sem_inc(const_ready, 1)
            for g in range(4, 8):
                split(g % RING, g % RAW_RING, g, 64 * (g // RAW_RING + 1))
            for g in range(8, FIRST_PIECED):
                split_tok(g % RING, g % RAW_RING, g, 64 * (g // RAW_RING + 1))
            base = 64 * (FIRST_PIECED // RAW_RING)
            rest = SLOT0[GIDX["sk0"]] - FIRST_PIECED
            turns = rest // RING

            def rounds(g0, turns, base):
                with pool.Fori(0, turns) as i:
                    for j in range(RING):
                        split((g0 + j) % RING, (g0 + j) % RAW_RING, i * RING + (g0 + j), i * 32 + (base + 32))
                return g0 + turns * RING, base + 32 * turns

            g, base = rounds(FIRST_PIECED, turns, base)
            order.mark(nc.gpsimd.memset(strict[:], 1.0))
            order.mark(nc.gpsimd.memset(neg_tri[:], -1.0))
            order.mark(nc.gpsimd.memset(unseen_f[:], 0.0))
            order.mark(nc.gpsimd.tensor_copy(ident_r[:], ident[:]))
            order(nc.gpsimd.memset(neg_one[:], -1.0))
            order.mark(nc.gpsimd.affine_select(out=unseen_f[:], in_=unseen_f[:], compare_op=ALU.is_gt,
                                               fill=MASKED, base=0, pattern=[[1, P]], channel_multiplier=-1))
            order.mark(nc.gpsimd.affine_select(out=strict[:], in_=strict[:], compare_op=ALU.is_gt, fill=0.0,
                                               base=0, pattern=[[1, P]], channel_multiplier=-1))
            order(nc.gpsimd.affine_select(out=neg_tri[:], in_=neg_tri[:], compare_op=ALU.is_ge, fill=0.0,
                                          base=0, pattern=[[-1, P]], channel_multiplier=1))
            order(nc.gpsimd.tensor_copy(unseen[:], unseen_f[:]))
            pool.sem_inc(const_ready, 1)
            left = N_SLOTS - g
            g, base = rounds(g, left // RING, base)
            for n in range(N_SLOTS - g):
                split(g % RING, g % RAW_RING, g, base + 32)
                g += 1
            assert g == N_SLOTS

        @block.tensor
        def _(pe):
            def mm(o, l, r, start, stop):
                return nc.tensor.matmul(o, l, r, start=start, stop=stop, skip_group_check=True)

            def three(o, w, xx, start, stop):
                mm(o, w[0], xx[0], start, False)
                mm(o, w[0], xx[1], False, False)
                return mm(o, w[1], xx[0], False, stop)

            def bank_free(n):
                if n >= 2:
                    pe.wait_ge(set_free[n % 2], 4 * (n // 2))

            def evacuated(n):
                pe.wait_ge(set_free[n % 2], 4 * (n // 2 + 1))

            def by_feature(n, act_hi, act_lo, width=SEQ, ready=None, g0=None, first=0, k0=0, last=True, i4=0,
                           hook=None, slots=None):
                g0 = SLOT0[n] if g0 is None else g0
                slots = GROUPS[n][1] if slots is None else slots
                for sl in range(slots):
                    g = g0 + sl
                    pe.wait_ge(raw_free, i4 + (g + 1))
                    for kk in range(2):
                        k = k0 + 2 * sl + kk
                        if ready is not None:
                            pe.wait_ge(split_ready, ready + 2 * sl + kk + 1)
                        for j in range(4):
                            last_mm = three(ps[:, 4 * (n % 2) + j, 0:width],
                                            [w[:, g % RING, kk, P * j:P * j + P] for w in (w_hi, w_lo)],
                                            [t[:, k, 0:width] for t in (act_hi, act_lo)],
                                            first + sl + kk == 0, sl == slots - 1 and kk == 1)
                    last_mm.then_inc(slot_used, 1)
                    if hook and sl in hook:
                        hook[sl]()

            def by_token(n, act_hi, act_lo, tiles=TT, width=512, i4=0, ready=None):
                g0 = SLOT0[n]
                for sl in range(GROUPS[n][1]):
                    g = g0 + sl
                    pe.wait_ge(raw_free, i4 + (g + 1))
                    for kk in range(2):
                        k = 2 * sl + kk
                        if ready is not None:
                            pe.wait_ge(split_ready, ready + k + 1)
                        for j in range(tiles):
                            last_mm = three(ps[:, 4 * (n % 2) + j, 0:width],
                                            [t[:, k, P * j:P * j + P] for t in (act_hi, act_lo)],
                                            [w[:, g % RING, kk, 0:width] for w in (w_hi, w_lo)],
                                            k == 0, k == KT - 1)
                    last_mm.then_inc(slot_used, 1)


            def norm_sum(name, width=SEQ):
                g = 8 * NORM_AT[name]
                for k in range(KT):
                    pe.wait_ge(sq_ready, g + k + 1)
                    mm(ps[:, NORM_BANK[name], 0:width], mean[:], sq[:, k % 2, 0:width], k == 0, k == KT - 1)\
                        .then_inc(sq_used, 1)

            def norm_read(name):
                pe.wait_ge(root_ready, ROOT_AT[name] + 1)

            pe.wait_ge(const_ready, 1)
            pe.wait_ge(rows_loaded, 16 * N_ROW_LOADS)
            for r in range(6):
                last = nc.tensor.transpose(ps[:, r // 4, P * (r % 4):P * (r % 4) + ROWS[r]], rows_in[0:ROWS[r], r, :],
                                           ident[0:ROWS[r], 0:ROWS[r]])
            last.then_inc(turned, 1)
            pe.wait_ge(in_loaded, 16 * TT)
            for k in range(KT):
                b = 2 + k % 4
                if k >= 4:
                    pe.wait_ge(x_ready, k - 3)
                for t in range(TT):
                    last = nc.tensor.transpose(ps[:, b, P * t:P * t + P], x_tok[:, t, P * k:P * k + P], ident[:])
                last.then_inc(turned, 1)
            norm_sum("mix")
            pe.wait_ge(turned_read, 1)
            norm_read("mix")

            G = GIDX
            h_ = (h_hi, h_lo)
            by_feature(G["q"], *h_, ready=SPLITS["mix"])
            by_feature(G["kv"], *h_)
            bank_free(G["tok"])
            by_token(G["tok"], *h_, width=TOKW)
            bank_free(G["qkb"])
            by_feature(G["qkb"], *h_)
            bank_free(G["vb"])
            by_token(G["vb"], *h_)
            evacuated(G["vb"])
            evacuated(G["qkb"])

            pe.wait_ge(cw_loaded, 16 * 4)
            for kv in range(2):
                nc.tensor.transpose(ps[:, 4, CMPB * kv:CMPB * kv + CMPB], pos[0:CMPB, kv, :],
                                    ident[0:CMPB, 0:CMPB]).then_inc(cmp_pe, 1)
            for kv in range(2):
                pe.wait_ge(cw1_loaded, 16 * 2 * (kv + 1))
                pe.wait_ge(cmp_blk, kv + 1)
                for h in range(KVH):
                    r = slice(HD * h, HD * h + HD)
                    for c in range(CMPB):
                        last = mm(ps[:, 2 * kv + h, 0:NCMP], w1c[r, c, :], blk[r, c, 0:NCMP], c == 0, c == CMPB - 1)
                last.then_inc(cmp_pe, 1)
            pe.wait_ge(cw2_loaded, 48)
            pe.wait_ge(cmp_a, 2)
            pe.wait_ge(cmp_b, 1)
            for h in range(KVH):
                mm(ps[:, 4 + h, 0:NCMP], w2k[:], hid[:, 0, h, 0:NCMP], True, True)
                last = mm(ps[0:NCMP, 6 + h, 0:HD], hid[:, 1, h, 0:NCMP], w2v[:], True, True)
            last.then_inc(cmp_pe, 1)
            pe.wait_ge(cmp_b, 2)

            def nsa_scores(it):
                qt, h = NSA[it]
                r = slice(HD * (h // GRP), HD * (h // GRP) + HD)
                q = qT[r, h % GRP, P * qt:P * qt + P]
                b = 2 * (it % 2)
                if it >= 2:
                    pe.wait_ge(att_m, it - 1)
                mm(ps[:, b, 0:P * (qt + 1)], q, kvT[r, 2, 0:P * (qt + 1)], True, True)
                w0 = P * max(0, qt - 2)
                mm(ps[:, b + 1, 0:P * (qt + 1) - w0], q, kvT[r, 3, w0:P * (qt + 1)], True, True)
                mm(ps[:, b + 1, 384:384 + NCMP], q, kcT[r, 0:NCMP], True, True).then_inc(att_s, 1)

            def nsa_blocks(qt):
                return ([(P * t, P, tok[:, t, 0:P]) for t in range(qt + 1)]
                        + [(512 + P * n, P, tok[:, t, P:2 * P])
                           for n, t in enumerate(range(max(0, qt - 2), qt + 1))]
                        + [(896, NCMP, None)])

            def nsa_turn(it):
                qt, h = NSA[it]
                pe.wait_ge(att_p, it + 1)
                if it >= 1:
                    pe.wait_ge(att_c, it)
                for n, (col, rows, _) in enumerate(nsa_blocks(qt)):
                    last = nc.tensor.transpose(ps[0:rows, 4 + n // 4, P * (n % 4):P * (n % 4) + P],
                                               s_buf[:, it % 2, col:col + rows], ident[:])
                last.then_inc(att_t, 1)

            def nsa_out(it):
                qt, h = NSA[it]
                pe.wait_ge(att_c, it + 1)
                pr = it // 2
                if pr >= 2:
                    pe.wait_ge(att_r, pr - 1)
                kvh = h // GRP
                o = ps[HD * (h % 2):HD * (h % 2) + HD, 6 + pr % 2, 0:P]
                blocks = nsa_blocks(qt)
                for n, (_, rows, v) in enumerate(blocks):
                    v = vc[0:NCMP, kvh, :] if v is None else v[:, HD * kvh:HD * kvh + HD]
                    last = mm(o, v, pT_buf[0:rows, it % 2, n, :], n == 0, n == len(blocks) - 1)
                last.then_inc(att_o, 1)

            for it in range(len(NSA) + 2):
                if it < len(NSA):
                    nsa_scores(it)
                if it >= 2:
                    nsa_out(it - 2)
                if 1 <= it <= len(NSA):
                    nsa_turn(it - 1)
            pe.wait_ge(att_r, 16)
            by_feature(G["rb"], *h_)
            for t in range(TT):
                last = nc.tensor.transpose(ps[0:16, 0, P * t:P * t + P], tok[:, t, TOKW - 16:TOKW], ident[:])
            last.then_inc(gla_pe, 1)
            pe.wait_ge(gla_al, 1)
            pe.wait_ge(wal_loaded, 16)
            for pr in range(2):
                if pr:
                    pe.wait_ge(gla_lg, 1)
                mm(ps[:, 1, :], wal[:, P * pr:P * pr + P], alT[:], True, True).then_inc(gla_pe, 1)
                pe.wait_ge(gla_ks, pr + 1)
                for t in range(TT):
                    last = nc.tensor.transpose(ps[:, 0, P * t:P * t + P], ks_t[:, P * t:P * t + P], ident[:])
                last.then_inc(gla_pe, 1)
                pe.wait_ge(gla_kt, pr + 1)
                evacuated(G["rb"])
                for c in range(NCH - 1):
                    r = slice(CH * (c % 2), CH * (c % 2) + CH)
                    last = mm(inc_at(c), ks_tok[r, c // 2, :],
                              vb[r, c // 2, 256 * pr:256 * pr + 256], True, True)
                last.then_inc(gla_pe, 1)
                pe.wait_ge(gla_qk, pr + 1)
                pe.wait_ge(gla_st, pr + 1)
                for e in range(2):
                    head = 2 * pr + e
                    r = slice(CH * e, CH * e + CH)
                    evacuated(G["rb"])
                    if head:
                        pe.wait_ge(gla_rd, head)
                    for t in range(TT):
                        u = 4 * head + t
                        if u >= 2:
                            pe.wait_ge(gla_at, u - 1)
                        for q in range(2):
                            s = slice(P * t + CH * q, P * t + CH * q + CH)
                            last = mm(ps[CH * q:CH * q + CH, 2 + u % 2, CH * q:CH * q + CH], kd[r, s], qd[r, s],
                                      True, True)
                        last.then_inc(gla_sc, 1)
                        pe.wait_ge(gla_at, u + 1)
                        mm(ps[:, 6, P * t:P * t + P], vb[:, t, P * head:P * head + P], attT[:, u % 2, :],
                           True, False)
                        for c in (2 * t, 2 * t + 1):
                            if c:
                                last = mm(ps[:, 6, CH * c:CH * c + CH], states[r, c, :],
                                          qd[r, CH * c:CH * c + CH], False, True)
                        last.then_inc(gla_o, 1)
                    pe.wait_ge(gla_sq, head + 1)
                    mm(ps[:, 7, :], mean[:], sq[:, 0, :], True, True).then_inc(gla_sum, 1)
            pe.wait_ge(gla_rd, GH)

            for h in range(2):
                bank_free(G[f"mn{h}"])
                by_feature(G[f"mn{h}"], *h_)
                bank_free(G[f"mg{h}"])
                by_feature(G[f"mg{h}"], *h_)
                pe.wait_ge(split_ready, SPLITS["gla"] + 4)
                pe.wait_ge(att_r, 16)
                bank_free(G[f"bn{h}"])
                by_feature(G[f"bn{h}"], o_hi, o_lo)
                bank_free(G[f"bg{h}"])
                by_feature(G[f"bg{h}"], o_hi, o_lo, k0=4)
            for h in range(2):
                n = G[f"out{h}"]
                bank_free(n)
                by_feature(n, mx_hi, mx_lo, ready=SPLITS["mx"])

            pe.wait_ge(mem_loaded, 16)
            evacuated(G["out0"])
            evacuated(G["out1"])
            for k in range(KT):
                b = k % 4
                if k >= 4:
                    pe.wait_ge(mem_turned_read, k - 3)
                for t in range(MEM // P):
                    last = nc.tensor.transpose(ps[:, b, P * t:P * t + P], mem_tok[:, t, P * k:P * k + P], ident[:])
                last.then_inc(turned, 1)
            norm_sum("mem", MEM)
            norm_read("mem")
            norm_sum("xn")
            norm_read("xn")
            pe.wait_ge(mem_turned_read, 8)
            by_feature(G["xk"], m_hi, m_lo, width=MEM, ready=SPLITS["mem"])
            by_token(G["xv"], m_hi, m_lo, tiles=MEM // P)
            bank_free(G["xq"])
            by_feature(G["xq"], *h_, ready=SPLITS["xn"])
            evacuated(G["xk"])
            evacuated(G["xv"])
            evacuated(G["xq"])

            def x_scores(it):
                h, qt = it // TT, it % TT
                if it >= 2:
                    pe.wait_ge(xat_e, it - 1)
                mm(ps[:, it % 2, 0:MEM], xqT[:, h, P * qt:P * qt + P], xkT[:, h, :], True, True)\
                    .then_inc(xat_s, 1)

            def x_turn(it):
                pe.wait_ge(xat_p, it + 1)
                if it >= 2:
                    pe.wait_ge(xat_c, it - 1)
                for t in range(MEM // P):
                    last = nc.tensor.transpose(ps[:, 2 + it % 2, P * t:P * t + P], xp[:, it % 2, P * t:P * t + P],
                                               ident[:])
                last.then_inc(xat_t, 1)

            def x_out(it):
                h, qt = it // TT, it % TT
                pe.wait_ge(xat_c, it + 1)
                if h >= 2 and qt == 0:
                    pe.wait_ge(xat_r, h - 1)
                for t in range(MEM // P):
                    last = mm(ps[:, 4 + h % 2, P * qt:P * qt + P], xv[:, t, P * h:P * h + P], xpT[:, it % 2, t, :],
                              t == 0, t == 1)
                last.then_inc(xat_o, 1)

            for it in range(XH * TT + 2):
                if it < XH * TT:
                    x_scores(it)
                if it >= 2:
                    x_out(it - 2)
                if 1 <= it <= XH * TT:
                    x_turn(it - 1)
            pe.wait_ge(xat_r, XH)
            by_feature(G["xo0"], xo_hi, xo_lo)
            bank_free(G["xo1"])
            by_feature(G["xo1"], xo_hi, xo_lo)

            def ffn(tag, name):
                n0 = G[f"up{tag}_0"]
                evacuated(n0 - 2)
                evacuated(n0 - 1)
                norm_sum(name)
                norm_read(name)
                by_feature(n0, *h_, ready=SPLITS[name])
                with pe.Fori(0, 5) as i:
                    for e in range(2):
                        n = n0 + 1 + e
                        pe.wait_ge(set_free[n % 2], i * 4 + 4 * (n // 2))
                        by_feature(n, *h_, i4=i * 8)
                for h in range(2):
                    n = G[f"down{tag}_{h}"]
                    bank_free(n)
                    by_feature(n, f_hi, f_lo, ready=SPLITS[f"ffn{tag}"] if h == 0 else None)

            ffn(1, "ffn1n")

            evacuated(G["down1_0"])
            evacuated(G["down1_1"])
            norm_sum("fin1")
            norm_read("fin1")
            norm_sum("retn")
            norm_read("retn")
            for h in range(RH):
                nq, nv, ng = G[f"rqk{h}"], G[f"rv{h}"], G[f"rg{h}"]
                sa, sc = 4 * (nq % 2), 4 * (nv % 2)
                bank_free(nq)
                if h:
                    pe.wait_ge(root_ready, ROOT_AT[f"ret{h}"])
                by_feature(nq, *h_, ready=SPLITS["retn"] if h == 0 else None)
                bank_free(nv)
                by_token(nv, *h_)
                evacuated(nq)
                for j in range(TT):
                    for kk in range(2):
                        last = mm(ps[:, sa + j, 0:SEQ - P * j], rq[:, 2 + kk, P * j:P * j + P],
                                  rq[:, kk, P * j:SEQ], kk == 0, kk == 1)
                    last.then_inc(ret_s, 1)
                evacuated(nv)
                pe.wait_ge(ret_sc, TT * (h + 1))
                for e in range(4):
                    for j in range(TT):
                        last = mm(ps[:, sc + e, P * j:SEQ], rv[:, j, P * e:P * e + P], rsc[:, j, 0:SEQ - P * j],
                                  j == 0, j == TT - 1)
                    last.then_inc(ret_o, 1)

                def mean_squares():
                    pe.wait_ge(ret_cp, 4 * (h + 1))
                    for e in range(4):
                        pe.wait_ge(ret_q, 4 * h + e + 1)
                        mm(ps[:, sc, :], mean[:], sq[:, e % 2, :], e == 0, e == 3).then_inc(ret_m, 1)

                by_feature(ng, *h_, hook={1: mean_squares})
            bank_free(G["ro0"])
            pe.wait_ge(root_ready, ROOT_AT["ret3"] + 1)
            by_feature(G["ro0"], y_hi, y_lo, ready=SPLITS["ret"])
            bank_free(G["ro1"])
            by_feature(G["ro1"], y_hi, y_lo)
            ffn(2, "ffn2n")

            evacuated(G["down2_0"])
            evacuated(G["down2_1"])
            norm_sum("sbn")
            norm_read("sbn")
            pe.wait_ge(const_ready, 3)
            for half in range(2):
                if half:
                    pe.wait_ge(sb_r, 4)
                for name in ("sq", "sk"):
                    n = G[f"{name}{half}"]
                    bank_free(n)
                    by_feature(n, *h_, ready=SPLITS["sbn"] if (name, half) == ("sq", 0) else None)
                n = G[f"sv{half}"]
                bank_free(n)
                by_token(n, *h_)
                for name in ("sq", "sk", "sv"):
                    evacuated(G[f"{name}{half}"])

                def logits(it, o, start, stop):
                    pair, j, e = SB[it]
                    r = slice(SH_D * e, SH_D * e + SH_D)
                    return mm(o[:, 0:SEQ - P * j], skT[r, pair, P * j:P * j + P], sqT[r, pair, P * j:SEQ],
                              start, stop)

                def z(it):
                    g = len(SB) * half + it
                    if it >= 2:
                        pe.wait_ge(st_sp, g - 1)
                    logits(it, ps[:, it % 2, :], True, True).then_inc(st_z, 1)

                def weights(it):
                    g = len(SB) * half + it
                    pair, j, e = SB[it]
                    pe.wait_ge(st_sp, g + 1)
                    if it >= 2:
                        pe.wait_ge(st_ex, g - 1)
                    o = ps[:, 2 + e, :]
                    mm(o[:, 0:SEQ - P * j], neg_tri[:], s_sp[:, e, 0:SEQ - P * j], True, False)
                    mm(o[:, 0:P], ident_r[:], unseen[:], False, False)
                    if j < TT - 1:
                        pe.wait_ge(st_up, updates(half, it - 2))
                        mm(o[:, P:SEQ - P * j], neg_one[:], s_sum[:, e, P * (j + 1):SEQ], False, False)
                    logits(it, o, False, True).then_inc(st_acc, 1)

                def pv(it):
                    g = len(SB) * half + it
                    pair, j, e = SB[it]
                    pe.wait_ge(st_ex, g + 1)
                    if pair >= 2 and j == TT - 1 and e == 0:
                        pe.wait_ge(sb_r, 4 * half + pair - 1)
                    head = 2 * pair + e
                    mm(ps[SH_D * e:SH_D * e + SH_D, 4 + pair % 2, P * j:SEQ], sv[:, j, SH_D * head:SH_D * head + SH_D],
                       s_a[:, e, 0:SEQ - P * j], j == TT - 1, j == 0).then_inc(st_o, 1)

                for it in range(len(SB) + 4):
                    if it < len(SB):
                        z(it)
                    if 1 <= it <= len(SB):
                        weights(it - 1)
                    if 2 <= it < len(SB) + 2:
                        pv(it - 2)
            pe.wait_ge(sb_r, 8)
            for h in range(2):
                by_feature(G[f"so{h}"], so_hi, so_lo)
            ffn(3, "ffn3n")
            evacuated(G["down3_0"])
            evacuated(G["down3_1"])
            norm_sum("fin")
            norm_read("fin")
            for t in range(TT):
                for b in range(2):
                    u = 2 * t + b
                    if u >= 4:
                        pe.wait_ge(turned_read, u - 2)
                    for k in range(4):
                        if t == 0:
                            pe.wait_ge(fin_ready, 4 * b + k + 1)
                        last = nc.tensor.transpose(ps[:, u % 4, P * k:P * k + P],
                                                   x[:, 4 * b + k, P * t:P * t + P], ident[:])
                    last.then_inc(turned, 1)

        @block.scalar
        def _(act):
            order = Chain(act, act_order)
            G = GIDX

            def group_done(n):
                act.wait_ge(slot_used, SLOT0[n + 1])

            loads = [(rows_in[8 * i:8 * i + 8, 0, :], src.rearrange("(k p) -> k p", p=P))
                     for i, src in enumerate((a["ln_mix_g"][0], a["ln_mem_g"][0], a["ln_x_g"][0], a["ln_ffn_g"][0],
                                              a["ln_final_g"], a["ret_norm_2"][0], a["ffn_norm_2"][0],
                                              a["sb_norm_2"][0], a["ffn_norm_2"][1], a["final_norm_2"]))]
            loads += [(rows_in[80:82, 0, :], a["gla_b_alpha"][0].rearrange("(k p) -> k p", p=P)),
                      (rows_in[82:83, 0, :], a["gla_norm_g"][0:1, :])]
            convs = [(a["conv_w"][0], a["conv_b"][0])]
            convs += [(a["ffn_conv_w_2"][l][:, FFN * b:FFN * b + FFN], a["ffn_conv_b_2"][l][FFN * b:FFN * b + FFN])
                      for l in range(2) for b in range(2)]
            for r, (w, bias) in enumerate(convs):
                loads += [(rows_in[FT * t:FT * t + FT, 1 + r, :], w[t].rearrange("(k p) -> k p", p=P))
                          for t in range(3)]
                loads.append((rows_in[3 * FT:4 * FT, 1 + r, :], bias.rearrange("(k p) -> k p", p=P)))
            assert len(loads) == N_ROW_LOADS
            for dst, src in loads:
                act.dma_start(dst, src).then_inc(rows_loaded, 16)
            act.dma_start(gate_b[:], a["nsa_gate_b"][0].partition_broadcast(P)).then_inc(gate_loaded, 16)
            def squares(name, src=x, width=SEQ, ready=x_ready):
                g0 = 8 * NORM_AT[name]
                for k in range(KT):
                    g = g0 + k
                    act.wait_ge(ready, X_AT.get(name, 0) + k + 1)
                    if g >= 2:
                        act.wait_ge(sq_used, g - 1)
                    nc.scalar.activation(sq[:, g % 2, 0:width], src[:, k, 0:width], ACT.Square).then_inc(sq_ready, 1)

            def root(name, src, scale=1.0, width=SEQ):
                nc.scalar.activation(rstd[:, 0:width], src[:, 0:width], ACT.Sqrt, bias=eps[:, 0:1], scale=scale)\
                    .then_inc(root_ready, 1)

            def norm_root(name, width=SEQ):
                act.wait_ge(sq_used, 8 * NORM_AT[name] + 8)
                root(name, ps[:, NORM_BANK[name], :], 1.0, width)

            def high(s, dst, width=SEQ, ready=None):
                act.wait_ge(full_ready, (s if ready is None else ready) + 1)
                nc.scalar.activation(dst, full[:, s % 2, 0:width], ACT.Copy).then_inc(full_hi, 1)

            def highs(name, dst, width=SEQ, n=KT):
                for k in range(n):
                    high(SPLITS[name] + k, dst[:, k, 0:width], width)

            squares("mix")
            norm_root("mix")
            for kv, name in enumerate(("cmp_pos_k", "cmp_pos_v")):
                for h in range(KVH):
                    act.dma_start(pos[:, kv, HD * h:HD * h + HD], a[name][0]).then_inc(cw_loaded, 16)

            def first_weights(name):
                for h in range(KVH):
                    act.dma_start(w1c[HD * h:HD * h + HD, :, :], a[name][0].rearrange("(c d) n -> d c n", d=HD))\
                        .then_inc(cw1_loaded, 16)

            first_weights("cmp_w1_k")
            for h in range(KVH):
                act.dma_start(w2k[:, HD * h:HD * h + HD], a["cmp_w2_k"][0]).then_inc(cw2_loaded, 16)
            act.dma_start(w2v[:], a["cmp_w2_v"][0]).then_inc(cw2_loaded, 16)

            highs("mix", h_hi)
            group_done(G["q"])
            for j in range(4):
                nc.scalar.activation(qT[:, j, :], bank(G["q"], j), ACT.Copy, scale=HD ** -0.5)\
                    .then_inc(set_free[G["q"] % 2], 1)
            act.wait_ge(gate_a, 1)
            nc.scalar.activation(gates[:], gates[:], ACT.Sigmoid).then_inc(gate_s, 1)
            group_done(G["qkb"])
            for j in range(4):
                nc.scalar.activation(qkb[:, j, :], bank(G["qkb"], j), ACT.Copy, scale=CH ** -0.5 if j < 2 else 1.0)\
                    .then_inc(set_free[G["qkb"] % 2], 1)
            act.wait_ge(cmp_pe, 3)
            first_weights("cmp_w1_v")
            for kv in range(2):
                act.wait_ge(cmp_pe, 3 + kv)
                nc.scalar.activation(hid[:, kv, :, 0:NCMP], ps[:, 2 * kv:2 * kv + 2, 0:NCMP], ACT.Gelu_apprx_tanh)\
                    .then_inc(cmp_a, 1)

            def nsa_parts(qt):
                return ((896, NCMP), (0, P * (qt + 1)), (512, P * min(3, qt + 1)))

            def nsa_exp(it):
                qt, b = NSA[it][0], it % 2
                act.wait_ge(att_n, it + 1)
                for n, (c, w) in enumerate(nsa_parts(qt)):
                    last = nc.scalar.activation(s_buf[:, b, c:c + w], s_buf[:, b, c:c + w], ACT.Exp,
                                                bias=att_st[:, b, n:n + 1], accum_out=att_st[:, b, 3 + n:4 + n])
                last.then_inc(att_e, 1)

            def nsa_copy(it):
                qt, b = NSA[it][0], it % 2
                nb = qt + 1 + min(3, qt + 1)
                act.wait_ge(att_t, it + 1)
                if it >= 2:
                    act.wait_ge(att_o, it - 1)
                src = ps[:, 4:6, :].rearrange("p a (b c) -> p (a b) c", c=P)
                nc.scalar.activation(pT_buf[:, b, 0:nb, :], src[:, 0:nb, :], ACT.Copy)
                nc.scalar.activation(pT_buf[0:NCMP, b, nb, :], src[0:NCMP, nb, :], ACT.Copy).then_inc(att_c, 1)

            for it in range(len(NSA) + 3):
                if it < len(NSA):
                    nsa_exp(it)
                if 1 <= it <= len(NSA):
                    nsa_copy(it - 1)
                if it >= 3 and it % 2:
                    pr = (it - 3) // 2
                    qt, i = pr // GRP, pr % GRP
                    act.wait_ge(att_o, 2 * pr + 2)
                    nc.scalar.activation(o_hi[:, i, P * qt:P * qt + P], ps[:, 6 + pr % 2, 0:P], ACT.Copy)\
                        .then_inc(att_h, 1)

            group_done(G["rb"])
            for j in range(4):
                nc.scalar.activation(rT[:, j, :], bank(G["rb"], j), ACT.Silu).then_inc(set_free[G["rb"] % 2], 1)
            act.wait_ge(gla_pe, 1)
            act.dma_start(wal[:], a["gla_w_alpha2"][0]).then_inc(wal_loaded, 16)
            nc.scalar.activation(alT[:], ps[0:16, 0, :], ACT.Copy).then_inc(gla_al, 1)
            for pr in range(2):
                x0 = 6 * pr
                act.wait_ge(gla_v, 3 * pr + 1)
                nc.scalar.activation(ebuf[:], ebuf[:], ACT.Exp, scale=-1.0).then_inc(gla_x, 1)
                act.wait_ge(gla_x, x0 + 1)
                nc.scalar.activation(ebuf[:], ebuf[:], ACT.Ln, bias=1.0).then_inc(gla_x, 1)
                act.wait_ge(gla_v, 3 * pr + 2)
                act.wait_ge(gla_x, x0 + 2)
                nc.scalar.activation(dec[:], bcum[:].rearrange("p (c i) -> p c i", i=CH)[:, :, CH - 1], ACT.Exp,
                                     scale=1.0 / 16).then_inc(gla_x, 1)
                nc.scalar.activation(qd[:], bcum[:], ACT.Exp, scale=1.0 / 16).then_inc(gla_x, 1)
                nc.scalar.activation(kd[:], bcum[:], ACT.Exp, scale=-1.0 / 16).then_inc(gla_x, 1)
                act.wait_ge(gla_v, 3 * pr + 3)
                nc.scalar.activation(ks_t[:], la[:], ACT.Exp, scale=1.0 / 16).then_inc(gla_x, 1)
                act.wait_ge(gla_pe, 3 + 3 * pr)
                nc.scalar.activation(ks_tok[:].rearrange("p t f -> p (t f)"), ps[:, 0, :], ACT.Copy)\
                    .then_inc(gla_kt, 1)
                for e in range(2):
                    head = 2 * pr + e
                    act.wait_ge(gla_o, 4 * head + 4)
                    if head:
                        act.wait_ge(gla_sum, head)
                    nc.scalar.activation(sq[:, 0, :], ps[:, 6, :], ACT.Square).then_inc(gla_sq, 1)
                    act.wait_ge(gla_sum, head + 1)
                    root(f"gla{head}", ps[:, 7, :], float(D) / P)
                    high(SPLITS["gla"] + head, o_hi[:, 4 + head, :])

            for h in range(2):
                for name, dst, s in ((f"mn{h}", gN, sig_n), (f"mg{h}", gG, sig_g)):
                    n = G[name]
                    group_done(n)
                    if h:
                        act.wait_ge(full_ready, SPLITS["mx"] + 4)
                    for j in range(4):
                        nc.scalar.activation(dst[:, j, :], bank(n, j), ACT.Sigmoid).then_inc(set_free[n % 2], 1)
                for j in range(4):
                    high(SPLITS["mx"] + 4 * h + j, mx_hi[:, 4 * h + j, :])
            act.wait_ge(slot_used, SLOT0[G["bg1"] + 1])
            act.dma_start(mem_tok[:], a["mem"][0].rearrange("(t p) d -> p t d", p=P)).then_inc(mem_loaded, 16)

            squares("mem", memT, MEM, mem_turned_read)
            norm_root("mem", MEM)
            squares("xn")
            highs("mem", m_hi, MEM)
            norm_root("xn")
            highs("xn", h_hi)
            group_done(G["xk"])
            for j in range(4):
                nc.scalar.activation(xkT[:, j, :], ps[:, 4 * (G["xk"] % 2) + j, 0:MEM], ACT.Copy)\
                    .then_inc(set_free[G["xk"] % 2], 1)
            group_done(G["xq"])
            for j in range(4):
                nc.scalar.activation(xqT[:, j, :], bank(G["xq"], j), ACT.Copy, scale=P ** -0.5)\
                    .then_inc(set_free[G["xq"] % 2], 1)
            for it in range(XH * TT + 2):
                b = it % 2
                if it < XH * TT:
                    act.wait_ge(xat_m, it + 1)
                    if it >= 2:
                        act.wait_ge(xat_t, it - 1)
                    nc.scalar.activation(xp[:, b, :], ps[:, b, 0:MEM], ACT.Exp, bias=x_st[:, b, 0:1],
                                         accum_out=x_st[:, b, 1:2]).then_inc(xat_e, 1)
                if 1 <= it <= XH * TT:
                    u = it - 1
                    act.wait_ge(xat_t, u + 1)
                    if u >= 2:
                        act.wait_ge(xat_o, u - 1)
                    nc.scalar.activation(xpT[:, u % 2].rearrange("p t q -> p (t q)"), ps[:, 2 + u % 2, 0:MEM],
                                         ACT.Copy).then_inc(xat_c, 1)
                if it >= TT + 1 and (it - 1) % TT == 0:
                    h = (it - 1) // TT - 1
                    act.wait_ge(xat_o, TT * (h + 1))
                    nc.scalar.activation(xo_hi[:, h, :], ps[:, 4 + h % 2, :], ACT.Copy).then_inc(xat_h, 1)

            def ffn(tag, name, func, two):
                squares(name)
                norm_root(name)
                highs(name, h_hi)
                n0 = G[f"up{tag}_0"]
                row = {1: 1, 2: 2, 3: 4}[tag]

                def group(n, i, c0, g, t, s, nl):
                    act.wait_ge(slot_used, SLOT0[n + 1] + g)
                    per = 4 if two else 2
                    for half in range(1 + two):
                        for e in range(2):
                            col = t + e
                            act.wait_ge(full_ready, s + e - 1)
                            nc.scalar.activation((cv if half else cu)[:, e, :],
                                                 ps[:, 4 * (n % 2) + 2 * half + e, :], ACT.Identity,
                                                 bias=vec(row + half, col + 3 * FT),
                                                 scale=vec(row + half, col + 2 * FT)).then_inc(conv_a, 1)
                    for e in range(2):
                        act.wait_ge(conv_d, c0 + per * 0 + e + 1)
                        nc.scalar.activation(cu[:, e, :], cu[:, e, :], func).then_inc(nonlin, 1)
                    for e in range(2):
                        act.wait_ge(full_ready, s + e + 1)
                        nc.scalar.activation(f_tile(f_hi, t + e), full[:, (s0 + e) % 2, :], ACT.Copy)\
                            .then_inc(full_hi, 1)

                s0 = SPLITS[f"ffn{tag}"]
                per = 4 if two else 2
                cd = CONV0[tag]
                group(n0, None, cd, 0, 0, s0, 0)
                with act.Fori(0, 5) as i:
                    for e in range(2):
                        group(n0 + 1 + e, i, i * (2 * per) + (cd + per * (1 + e)), i * 8, i * 4 + 2 * (1 + e),
                              i * 4 + (s0 + 2 * (1 + e)), 0)

            ffn(1, "ffn1n", ACT.Gelu_apprx_tanh, False)

            act.wait_ge(slot_used, SLOT0[G["rqk0"]])
            act.dma_start(cosT[:], a["rope_cos"]).then_inc(rope_loaded, 16)
            act.dma_start(sinT[:], a["rope_sin"]).then_inc(rope_loaded, 16)
            act.dma_start(dmat[:], a["ret_decay"][0]).then_inc(dmat_loaded, 16)
            squares("fin1")
            norm_root("fin1")
            squares("retn")
            norm_root("retn")
            highs("retn", h_hi)
            for h in range(RH):
                nv, ng = G[f"rv{h}"], G[f"rg{h}"]
                group_done(nv)
                if h:
                    act.wait_ge(ret_o, 4 * h)
                for t in range(TT):
                    nc.scalar.activation(rv[:, t, :], bank(nv, t), ACT.Copy).then_inc(set_free[nv % 2], 1)
                act.wait_ge(ret_o, 4 * h + 4)
                if h < RH - 1:
                    act.wait_ge(ret_sc, TT * (h + 1))
                    act.dma_start(dmat[:], a["ret_decay"][h + 1]).then_inc(dmat_loaded, 16)
                for e in range(4):
                    nc.scalar.activation(ro[:, e, :], bank(nv, e), ACT.Copy).then_inc(ret_cp, 1)
                for e in range(4):
                    act.wait_ge(ret_cp, 4 * h + e + 1)
                    if 4 * h + e >= 2:
                        act.wait_ge(ret_m, 4 * h + e - 1)
                    nc.scalar.activation(sq[:, e % 2, :], ro[:, e, :], ACT.Square).then_inc(ret_q, 1)
                act.wait_ge(ret_m, 4 * h + 4)
                root(f"ret{h}", bank(nv, 0), 2.0)
                group_done(ng)
                for e in range(4):
                    s = SPLITS["ret"] + 4 * h + e
                    act.wait_ge(full_ready, s - 1)
                    nc.scalar.activation(r1[:, e % 2, :], bank(ng, e), ACT.Silu).then_inc(set_free[ng % 2], 1)
                    if e:
                        high(s - 1, y_hi[:, 4 * h + e - 1, :])
                high(SPLITS["ret"] + 4 * h + 3, y_hi[:, 4 * h + 3, :])
            ffn(2, "ffn2n", ACT.Silu, True)

            squares("sbn")
            norm_root("sbn")
            highs("sbn", h_hi)
            for half in range(2):
                n = G[f"sq{half}"]
                group_done(n)
                for j in range(4):
                    nc.scalar.activation(sqT[:, j, :], bank(n, j), ACT.Copy, scale=SH_D ** -0.5)\
                        .then_inc(set_free[n % 2], 1)
                n = G[f"sv{half}"]
                group_done(n)
                for j in range(4):
                    nc.scalar.activation(sv[:, j, :], bank(n, j), ACT.Copy).then_inc(set_free[n % 2], 1)
                for it in range(len(SB) + 3):
                    g = len(SB) * half + it
                    if it < len(SB):
                        pair, j, e = SB[it]
                        w = SEQ - P * j
                        act.wait_ge(st_min, g + 1)
                        nc.scalar.activation(s_ez[:, e, 0:w], s_ez[:, e, 0:w], ACT.Exp)\
                            .then_inc(act_order, 1)
                        act.wait_ge(act_order, g + 1)
                        nc.scalar.activation(s_ez[:, e, 0:w], s_ez[:, e, 0:w], ACT.Ln, bias=1.0).then_inc(st_l, 1)
                    if 1 <= it <= len(SB):
                        pair, j, e = SB[it - 1]
                        w = SEQ - P * j
                        act.wait_ge(st_acc, g)
                        if it >= 3:
                            act.wait_ge(st_o, g - 2)
                        nc.scalar.activation(s_a[:, e, 0:w], ps[:, 2 + e, 0:w], ACT.Exp).then_inc(st_ex, 1)
                    if it >= 3 and (it - 2) % 8 == 1 and it > 8:
                        pair = (it - 2) // 8 - 1
                        act.wait_ge(st_o, len(SB) * half + 8 * (pair + 1))
                        nc.scalar.activation(so_hi[:, 4 * half + pair, :], ps[:, 4 + pair % 2, :], ACT.Copy)\
                            .then_inc(sb_h, 1)
                pair = 3
                act.wait_ge(st_o, len(SB) * (half + 1))
                nc.scalar.activation(so_hi[:, 4 * half + pair, :], ps[:, 4 + pair % 2, :], ACT.Copy)\
                    .then_inc(sb_h, 1)
            ffn(3, "ffn3n", ACT.Silu, True)
            squares("fin")
            norm_root("fin")
            for u in range(2 * TT):
                act.wait_ge(turned, 1 + 8 + 8 + u + 1)
                nc.scalar.activation(o_tok[:, u // 2, 512 * (u % 2):512 * (u % 2) + 512], ps[:, u % 4, :], ACT.Copy)\
                    .then_inc(turned_read, 1)

        @block.vector
        def _(dve):
            order = Chain(dve, dve_order)
            G = GIDX
            V = nc.vector

            def group_done(n):
                dve.wait_ge(slot_used, SLOT0[n + 1])

            def scaled_full(s, value):
                if s >= 2:
                    dve.wait_ge(full_hi, s - 1)
                    dve.wait_ge(split_ready, s - 1)
                value(full[:, s % 2, :]).then_inc(full_ready, 1)

            def low(s, hi, lo, width=SEQ):
                dve.wait_ge(full_ready, s + 1)
                dve.wait_ge(full_hi, s + 1)
                V.tensor_tensor(lo, full[:, s % 2, 0:width], hi.bitcast(F32), ALU.subtract).then_inc(split_ready, 1)

            def norm_rstd(name, width=SEQ):
                dve.wait_ge(root_ready, ROOT_AT[name] + 1)
                V.reciprocal(rstd[:, 0:width], rstd[:, 0:width]).then_inc(rstd_ready, 1)
                dve.wait_ge(rstd_ready, ROOT_AT[name] + 1)

            def norm(name, hi, lo, src=x, width=SEQ):
                norm_rstd(name, width)
                s0 = SPLITS[name]
                for k in range(KT + 1):
                    if k < KT:
                        scaled_full(s0 + k, lambda o: V.scalar_tensor_tensor(
                            o[:, 0:width], src[:, k, 0:width], gain(GAIN_OF[name], k), rstd[:, 0:width],
                            ALU.mult, ALU.mult))
                    if k:
                        low(s0 + k - 1, hi[:, k - 1, 0:width], lo[:, k - 1, 0:width], width)

            def norm_in_place(name, ready, done):
                norm_rstd(name)
                for k in range(KT):
                    V.scalar_tensor_tensor(x[:, k, :], x[:, k, :], gain(GAIN_OF[name], k), rstd[:],
                                           ALU.mult, ALU.mult).then_inc(done, 1)

            X_DONE = [8]

            def residual(names):
                for h, name in enumerate(names):
                    n = G[name]
                    group_done(n)
                    for j in range(4):
                        V.tensor_tensor(x[:, 4 * h + j, :], x[:, 4 * h + j, :], bank(n, j), ALU.add)\
                            .then_inc(x_ready, 1)
                        X_DONE[0] += 1
                        if j == 3:
                            dve.wait_ge(x_ready, X_DONE[0])
                            for b in range(4):
                                dve.sem_inc(set_free[n % 2], 1)

            dve.wait_ge(turned, 1)
            for r in range(6):
                last = V.tensor_copy(vecs[:, r, 0:ROWS[r]], ps[:, r // 4, P * (r % 4):P * (r % 4) + ROWS[r]])
            last.then_inc(turned_read, 1)
            for k in range(KT):
                dve.wait_ge(turned, 2 + k)
                V.tensor_copy(x[:, k, :], ps[:, 2 + k % 4, :]).then_inc(x_ready, 1)
            dve.wait_ge(turned_read, 1)
            norm("mix", h_hi, h_lo)

            group_done(G["kv"])
            for j in range(4):
                V.tensor_copy(kvT[:, j, :], bank(G["kv"], j)).then_inc(set_free[G["kv"] % 2], 1)
            group_done(G["tok"])
            for j in range(4):
                V.tensor_copy(tok[:, j, :], bank(G["tok"], j)[:, 0:TOKW]).then_inc(set_free[G["tok"] % 2], 1)
            dve.wait_ge(gate_loaded, 16)
            dve.wait_ge(set_free[0], 4 * (G["tok"] // 2 + 1))
            V.tensor_tensor(gates[:], tok[:, :, 2 * P:2 * P + 24],
                            gate_b[:].unsqueeze(1).to_broadcast([P, TT, 3 * HEADS]), ALU.add).then_inc(gate_a, 1)
            group_done(G["vb"])
            for j in range(4):
                V.tensor_copy(vb[:, j, :], bank(G["vb"], j)).then_inc(set_free[G["vb"] % 2], 1)
            dve.wait_ge(cmp_pe, 2)
            V.tensor_copy(posT[:].rearrange("p a c -> p (a c)"), ps[:, 4, 0:2 * CMPB]).then_inc(cmp_b, 1)
            dve.wait_ge(cmp_b, 1)

            def blocks(kv):
                tokens = kvT[:, kv, :].rearrange("p (n c) -> p c n", c=16)
                for half in range(2):
                    last = V.tensor_tensor(blk[:, 16 * half:16 * half + 16, 0:NCMP], tokens[:, :, half:half + NCMP],
                                           posT[:, kv, 16 * half:16 * half + 16].unsqueeze(2)
                                           .to_broadcast([P, 16, NCMP]), ALU.add)
                last.then_inc(cmp_blk, 1)

            blocks(0)
            dve.wait_ge(const_ready, 2)
            dve.wait_ge(gate_s, 1)
            g0 = gates[:, 0, :].rearrange("p (h b) -> p h b", b=3)[:, :, 0]
            V.tensor_scalar(g0, g0, row_ok[:, 0:1], None, ALU.mult).then_inc(gate_m, 1)
            dve.wait_ge(cmp_pe, 3)
            blocks(1)
            dve.wait_ge(cmp_pe, 5)
            for h in range(KVH):
                order.mark(V.tensor_copy(kcT[HD * h:HD * h + HD, 0:NCMP], ps[HD * h:HD * h + HD, 4 + h, 0:NCMP]))
            V.tensor_copy(vc[0:NCMP, :, :], ps[0:NCMP, 6:8, 0:HD]).then_inc(cmp_b, 1)

            def nsa_bias(it):
                qt, h = NSA[it]
                b = it % 2
                nk, nw = P * (qt + 1), P * min(3, qt + 1)
                dve.wait_ge(att_s, it + 1)
                if it >= 2:
                    dve.wait_ge(att_t, it - 1)
                order.mark(V.scalar_tensor_tensor(s_buf[:, b, 0:nk], d_slc[:, SEQ - nk:SEQ], SLOPES[h],
                                                  ps[:, 2 * b, 0:nk], ALU.mult, ALU.add))
                order.mark(V.scalar_tensor_tensor(s_buf[:, b, 512:512 + nw], d_win[:, WIN + P - nw:WIN + P],
                                                  SLOPES[h], ps[:, 2 * b + 1, 0:nw], ALU.mult, ALU.add))
                V.scalar_tensor_tensor(s_buf[:, b, 896:896 + NCMP], d_cmp[:, qt, 0:NCMP], SLOPES[h],
                                       ps[:, 2 * b + 1, 384:384 + NCMP], ALU.mult, ALU.add).then_inc(att_m, 1)
                order.wait()
                order.mark(V.tensor_reduce(att_st[:, b, 1:2], s_buf[:, b, 0:nk], AX_X, ALU.max, negate=True))
                order.mark(V.tensor_reduce(att_st[:, b, 2:3], s_buf[:, b, 512:512 + nw], AX_X, ALU.max,
                                           negate=True))
                dve.wait_ge(att_m, it + 1)
                V.tensor_reduce(att_st[:, b, 0:1], s_buf[:, b, 896:896 + NCMP], AX_X, ALU.max, negate=True)\
                    .then_inc(att_n, 1)

            def nsa_scale(it):
                qt, h = NSA[it]
                b = it % 2
                nk, nw = P * (qt + 1), P * min(3, qt + 1)
                dve.wait_ge(att_e, it + 1)
                order(V.reciprocal(att_st[:, b, 6:9], att_st[:, b, 3:6]))
                order(V.tensor_tensor(att_st[:, b, 9:12], att_st[:, b, 6:9], gates[:, qt, 3 * h:3 * h + 3],
                                      ALU.mult))
                for n, (c, w) in enumerate(((896, NCMP), (0, nk), (512, nw))):
                    last = V.tensor_scalar(s_buf[:, b, c:c + w], s_buf[:, b, c:c + w], att_st[:, b, 9 + n:10 + n],
                                           None, ALU.mult)
                last.then_inc(att_p, 1)

            dve.wait_ge(gate_m, 1)
            for it in range(len(NSA) + 3):
                if it < len(NSA):
                    nsa_bias(it)
                if 1 <= it <= len(NSA):
                    nsa_scale(it - 1)
                if it >= 3 and it % 2:
                    pr = (it - 3) // 2
                    qt, i = pr // GRP, pr % GRP
                    dve.wait_ge(att_h, pr + 1)
                    V.tensor_tensor(o_lo[:, i, P * qt:P * qt + P], ps[:, 6 + pr % 2, 0:P],
                                    o_hi[:, i, P * qt:P * qt + P].bitcast(F32), ALU.subtract).then_inc(att_r, 1)

            for pr in range(2):
                v0, x0 = 3 * pr, 6 * pr
                dve.wait_ge(gla_pe, 2 + 3 * pr)
                if pr:
                    dve.wait_ge(gla_o, 8)
                    dve.wait_ge(gla_x, 6)
                b_al = vecs[:, 0, V_BALPHA + pr:V_BALPHA + pr + 1]
                V.tensor_scalar(ebuf[:], ps[:, 1, :], b_al, -FAR, ALU.add, ALU.max).then_inc(gla_v, 1)
                V.tensor_scalar(la[:], ps[:, 1, :], b_al, None, ALU.add).then_inc(gla_lg, 1)
                dve.wait_ge(gla_x, x0 + 2)
                dve.wait_ge(gla_lg, pr + 1)
                order(V.scalar_tensor_tensor(la[:], ebuf[:], -1.0, la[:], ALU.mult, ALU.min))
                V.tensor_tensor_scan(bcum[:], keep[:], la[:], 0.0, ALU.mult, ALU.add).then_inc(gla_v, 1)
                dve.wait_ge(gla_v, v0 + 2)
                b3 = bcum[:].rearrange("p (c i) -> p c i", i=CH)
                V.tensor_tensor(la[:].rearrange("p (c i) -> p c i", i=CH),
                                b3[:, :, CH - 1:CH].to_broadcast([P, NCH, CH]), b3, ALU.subtract).then_inc(gla_v, 1)
                dve.wait_ge(gla_x, x0 + 6)
                V.tensor_tensor(ks_t[:], ks_t[:], qkb[:, 2 + pr, :], ALU.mult).then_inc(gla_ks, 1)
                order.mark(V.tensor_tensor(qd[:], qd[:], qkb[:, pr, :], ALU.mult))
                V.tensor_tensor(kd[:], kd[:], qkb[:, 2 + pr, :], ALU.mult).then_inc(gla_qk, 1)
                order(V.memset(states[:, 0, :], 0.0))
                dve.wait_ge(gla_pe, 4 + 3 * pr)
                for c in range(NCH - 1):
                    for e in range(2):
                        r = slice(CH * e, CH * e + CH)
                        ins = V.scalar_tensor_tensor(
                            states[r, c + 1, :], states[r, c, :], dec[r, c:c + 1],
                            inc_at(c)[r, P * e:P * e + P], ALU.mult, ALU.add)
                        if c < NCH - 2 or e == 0:
                            order.mark(ins)
                        else:
                            ins.then_inc(gla_st, 1)
                    order.wait()
                for e in range(2):
                    head = 2 * pr + e
                    for t in range(TT):
                        u = 4 * head + t
                        dve.wait_ge(gla_sc, u + 1)
                        if u >= 2:
                            dve.wait_ge(gla_o, u - 1)
                        for q in range(2):
                            r = slice(CH * q, CH * q + CH)
                            last = V.tensor_tensor(attT[r, u % 2, CH * q:CH * q + CH],
                                                   ps[r, 2 + u % 2, CH * q:CH * q + CH], caus[r, :], ALU.mult)
                        last.then_inc(gla_at, 1)
                    dve.wait_ge(root_ready, ROOT_AT[f"gla{head}"] + 1)
                    V.reciprocal(rstd[:], rstd[:]).then_inc(rstd_ready, 1)
                    dve.wait_ge(rstd_ready, ROOT_AT[f"gla{head}"] + 1)
                    s = SPLITS["gla"] + head
                    if s >= 2:
                        dve.wait_ge(full_hi, s - 1)
                        dve.wait_ge(split_ready, s - 1)
                    f = full[:, s % 2, :]
                    V.tensor_tensor(f, ps[:, 6, :], rstd[:], ALU.mult).then_inc(gla_rd, 1)
                    dve.wait_ge(gla_rd, head + 1)
                    V.scalar_tensor_tensor(f, f, vecs[:, 0, V_GLAG:V_GLAG + 1], rT[:, head, :], ALU.mult, ALU.mult)\
                        .then_inc(full_ready, 1)
                    low(s, o_hi[:, 4 + head, :], o_lo[:, 4 + head, :])

            for h in range(2):
                for j in range(4):
                    if j == 0:
                        group_done(G[f"bn{h}"])
                        dve.wait_ge(set_free[G[f"mn{h}"] % 2], 4 * (G[f"mn{h}"] // 2 + 1))
                    V.tensor_tensor(gN[:, j, :], gN[:, j, :], bank(G[f"bn{h}"], j), ALU.mult)\
                        .then_inc(set_free[G[f"bn{h}"] % 2], 1)
                group_done(G[f"bg{h}"])
                dve.wait_ge(set_free[G[f"mg{h}"] % 2], 4 * (G[f"mg{h}"] // 2 + 1))
                for j in range(4):
                    V.tensor_tensor(gG[:, j, :], gG[:, j, :], bank(G[f"bg{h}"], j), ALU.mult)\
                        .then_inc(set_free[G[f"bg{h}"] % 2], 1)
                dve.wait_ge(set_free[G[f"bg{h}"] % 2], 4 * (G[f"bg{h}"] // 2 + 1))
                dve.wait_ge(set_free[G[f"bn{h}"] % 2], 4 * (G[f"bn{h}"] // 2 + 1))
                for j in range(4 + 1):
                    s = SPLITS["mx"] + 4 * h + j
                    if j < 4:
                        scaled_full(s, lambda o: V.tensor_tensor(o, gN[:, j, :], gG[:, j, :], ALU.add))
                    if j:
                        low(s - 1, mx_hi[:, 4 * h + j - 1, :], mx_lo[:, 4 * h + j - 1, :])
            residual(("out0", "out1"))

            for k in range(KT):
                dve.wait_ge(turned, 1 + 8 + k + 1)
                V.tensor_copy(memT[:, k, :], ps[:, k % 4, 0:MEM]).then_inc(mem_turned_read, 1)
            norm("mem", m_hi, m_lo, memT, MEM)
            norm("xn", h_hi, h_lo)
            group_done(G["xv"])
            for j in range(4):
                if j < MEM // P:
                    V.tensor_copy(xv[:, j, :], bank(G["xv"], j)).then_inc(set_free[G["xv"] % 2], 1)
                else:
                    dve.sem_inc(set_free[G["xv"] % 2], 1)
            for it in range(XH * TT + 2):
                b = it % 2
                if it < XH * TT:
                    dve.wait_ge(xat_s, it + 1)
                    V.tensor_reduce(x_st[:, b, 0:1], ps[:, b, 0:MEM], AX_X, ALU.max, negate=True).then_inc(xat_m, 1)
                if 1 <= it <= XH * TT:
                    u = it - 1
                    dve.wait_ge(xat_e, u + 1)
                    order(V.reciprocal(x_st[:, u % 2, 2:3], x_st[:, u % 2, 1:2]))
                    V.tensor_scalar(xp[:, u % 2, :], xp[:, u % 2, :], x_st[:, u % 2, 2:3], None, ALU.mult)\
                        .then_inc(xat_p, 1)
                if it >= TT + 1 and (it - 1) % TT == 0:
                    h = (it - 1) // TT - 1
                    dve.wait_ge(xat_h, h + 1)
                    V.tensor_tensor(xo_lo[:, h, :], ps[:, 4 + h % 2, :], xo_hi[:, h, :].bitcast(F32), ALU.subtract)\
                        .then_inc(xat_r, 1)
            residual(("xo0", "xo1"))

            def ffn(tag, name, two):
                norm(name, h_hi, h_lo)
                n0 = G[f"up{tag}_0"]
                row = {1: 1, 2: 2, 3: 4}[tag]
                s0 = SPLITS[f"ffn{tag}"]
                per = 4 if two else 2
                cd = CONV0[tag]
                nl0 = 22 * (tag - 1)

                def taps(dst, src, e, col, r, done, own):
                    V.scalar_tensor_tensor(dst[:, e, 2:SEQ], src[:, 0:SEQ - 2], vec(r, col),
                                           dst[:, e, 2:SEQ], ALU.mult, ALU.add).then_inc(dve_order, 1)
                    dve.wait_ge(dve_order, own)
                    V.scalar_tensor_tensor(dst[:, e, 1:SEQ], src[:, 0:SEQ - 1], vec(r, col + FT),
                                           dst[:, e, 1:SEQ], ALU.mult, ALU.add).then_inc(done, 1)

                base = order.n

                def group(n, c, t, s, nl, own):
                    st = set_free[n % 2]
                    for half in range(1 + two):
                        for e in range(2):
                            u = 2 * half + e
                            dve.wait_ge(conv_a, c + u + 1)
                            taps(cv if half else cu, ps[:, 4 * (n % 2) + u, :], e, t + e, row + half, conv_d,
                                 own + u + 1)
                    for e in range(2):
                        dve.wait_ge(nonlin, nl + e + 1)
                        dve.wait_ge(full_hi, s + e - 1)
                        dve.wait_ge(split_ready, s + e - 1)
                        if two:
                            dve.wait_ge(conv_d, c + 4)
                            V.tensor_tensor(full[:, (s0 + e) % 2, :], cu[:, e, :], cv[:, e, :], ALU.mult)\
                                .then_inc(full_ready, 1)
                        else:
                            V.tensor_tensor(full[:, (s0 + e) % 2, :], cu[:, e, :], ps[:, 4 * (n % 2) + 2 + e, :],
                                            ALU.mult).then_inc(full_ready, 1)
                    dve.wait_ge(full_ready, s + 2)
                    for b in range(4):
                        dve.sem_inc(st, 1)
                    for e in range(2):
                        dve.wait_ge(full_hi, s + e + 1)
                        V.tensor_tensor(f_tile(f_lo, t + e), full[:, (s0 + e) % 2, :],
                                        f_tile(f_hi, t + e).bitcast(F32), ALU.subtract).then_inc(split_ready, 1)

                group(n0, cd, 0, s0, nl0, base)
                with dve.Fori(0, 5) as i:
                    for e in range(2):
                        group(n0 + 1 + e, i * (2 * per) + (cd + per * (1 + e)), i * 4 + 2 * (1 + e),
                              i * 4 + (s0 + 2 * (1 + e)), i * 4 + (nl0 + 2 * (1 + e)),
                              i * (2 * per) + (base + per * (1 + e)))
                order.n = base + 11 * per
                residual((f"down{tag}_0", f"down{tag}_1"))

            ffn(1, "ffn1n", False)

            norm_in_place("fin1", x_ready, x_ready)
            X_DONE[0] += 8
            norm("retn", h_hi, h_lo)
            dve.wait_ge(rope_loaded, 32)
            for h in range(RH):
                nq, ng = G[f"rqk{h}"], G[f"rg{h}"]
                group_done(nq)
                if h:
                    dve.wait_ge(ret_s, TT * h)
                for w in range(2):
                    b0, b1 = bank(nq, 2 * w), bank(nq, 2 * w + 1)
                    order.mark(V.tensor_tensor(rq[:, 2 * w, :], b0, cosT[:], ALU.mult))
                    order.mark(V.tensor_tensor(rq[:, 2 * w + 1, :], b0, sinT[:], ALU.mult))
                    order.mark(V.tensor_tensor(r1[:, 0, :], b1, sinT[:], ALU.mult))
                    V.tensor_tensor(r1[:, 1, :], b1, cosT[:], ALU.mult).then_inc(rope_d, 1)
                    order.wait()
                    dve.wait_ge(rope_d, 2 * h + w + 1)
                    order.mark(V.tensor_tensor(rq[:, 2 * w, :], rq[:, 2 * w, :], r1[:, 0, :], ALU.subtract))
                    order(V.tensor_tensor(rq[:, 2 * w + 1, :], rq[:, 2 * w + 1, :], r1[:, 1, :], ALU.add))
                for b in range(4):
                    dve.sem_inc(set_free[nq % 2], 1)
                dve.wait_ge(dmat_loaded, 16 * (h + 1))
                for j in range(TT):
                    dve.wait_ge(ret_s, TT * h + j + 1)
                    w = SEQ - P * j
                    V.scalar_tensor_tensor(rsc[:, j, 0:w], bank(nq, j)[:, 0:w], 1.0 / 16, dmat[:, 0:w],
                                           ALU.mult, ALU.mult).then_inc(ret_sc, 1)
                dve.wait_ge(root_ready, ROOT_AT[f"ret{h}"] + 1)
                V.reciprocal(rstd[:], rstd[:]).then_inc(rstd_ready, 1)
                dve.wait_ge(rstd_ready, ROOT_AT[f"ret{h}"] + 1)
                for e in range(4 + 1):
                    s = SPLITS["ret"] + 4 * h + e
                    if e < 4:
                        order(V.tensor_tensor(ro[:, e, :], ro[:, e, :], rstd[:], ALU.mult))
                        dve.wait_ge(set_free[ng % 2], 4 * (ng // 2) + e + 1)
                        scaled_full(s, lambda o: V.tensor_tensor(o, ro[:, e, :], r1[:, e % 2, :], ALU.mult))
                    if e:
                        low(s - 1, y_hi[:, 4 * h + e - 1, :], y_lo[:, 4 * h + e - 1, :])
            residual(("ro0", "ro1"))
            ffn(2, "ffn2n", True)

            norm("sbn", h_hi, h_lo)
            dve.wait_ge(const_ready, 3)
            for half in range(2):
                n = G[f"sk{half}"]
                group_done(n)
                for j in range(4):
                    V.tensor_copy(skT[:, j, :], bank(n, j)).then_inc(set_free[n % 2], 1)

                def bounded(it):
                    pair, j, e = SB[it]
                    g = len(SB) * half + it
                    w = SEQ - P * j
                    dve.wait_ge(st_z, g + 1)
                    V.tensor_scalar(s_ez[:, e, 0:w], ps[:, it % 2, 0:w], FAR, None, ALU.min)\
                        .then_inc(st_min, 1)

                def softplus(it):
                    pair, j, e = SB[it]
                    g = len(SB) * half + it
                    w = SEQ - P * j
                    dve.wait_ge(st_l, g + 1)
                    if it >= 2:
                        dve.wait_ge(st_acc, g - 1)
                        dve.wait_ge(st_up, updates(half, it - 2))
                        order.wait()
                    order(V.tensor_tensor(s_sp[:, e, 0:w], ps[:, it % 2, 0:w], s_ez[:, e, 0:w], ALU.max))
                    V.tensor_tensor(s_sp[:, e, 0:P], s_sp[:, e, 0:P], strict[:], ALU.mult).then_inc(st_sp, 1)

                def update(it):
                    pair, j, e = SB[it]
                    if j == 0:
                        return
                    g = len(SB) * half + it
                    dve.wait_ge(st_acc, g + 1)
                    dve.wait_ge(st_sp, g + 1)
                    if j < TT - 1:
                        order.mark(V.tensor_tensor(s_sum[:, e, P * (j + 1):SEQ], s_sum[:, e, P * (j + 1):SEQ],
                                                   s_sp[:, e, P:SEQ - P * j], ALU.add))
                    V.tensor_copy(s_sum[:, e, P * j:P * (j + 1)], s_sp[:, e, 0:P]).then_inc(st_up, 1)

                def low_part(pair):
                    i = 4 * half + pair
                    dve.wait_ge(sb_h, i + 1)
                    V.tensor_tensor(so_lo[:, i, :], ps[:, 4 + pair % 2, :], so_hi[:, i, :].bitcast(F32),
                                    ALU.subtract).then_inc(sb_r, 1)

                for it in range(len(SB) + 3):
                    if it < len(SB):
                        bounded(it)
                    if 1 <= it <= len(SB):
                        softplus(it - 1)
                    if 2 <= it < len(SB) + 2:
                        update(it - 2)
                    if it >= 3 and (it - 2) % 8 == 1 and it > 8:
                        low_part((it - 2) // 8 - 1)
                low_part(3)
            residual(("so0", "so1"))
            ffn(3, "ffn3n", True)
            norm_in_place("fin", x_ready, fin_ready)


def shape_constants():
    pos = np.arange(SEQ, dtype=np.float32)
    inv = (np.float32(10000.0) ** (-np.arange(0, 256, 2, dtype=np.float32) / np.float32(256))).astype(np.float32)
    ang = inv[:, None] * pos[None, :]
    key, query = np.arange(P)[:, None], np.arange(SEQ)[None, :]
    decay = np.stack([np.where(query >= key, np.exp(np.maximum(query - key, 0) * np.log(g)), 0.0)
                      for g in RET_DECAY]).astype(np.float32)
    return {"rope_cos": np.cos(ang).astype(np.float32), "rope_sin": np.sin(ang).astype(np.float32),
            "ret_decay": decay}


def kernel(**inputs):
    import concourse.bacc as bacc
    from concourse.bass_utils import run_bass_kernel_spmd

    nc = bacc.Bacc("TRN2", target_bir_lowering=False, num_devices=1)
    arrays, aps = {}, {}
    for name, value in {**inputs, **shape_constants()}.items():
        v = np.ascontiguousarray(value)
        arrays[f"in_{name}"] = v
        aps[name] = nc.dram_tensor(f"in_{name}", v.shape, mybir.dt.from_np(v.dtype), kind="ExternalInput").ap()
    out = nc.dram_tensor("out_x", (1, SEQ, D), F32, kind="ExternalOutput").ap()
    build(nc, aps, out)
    result = run_bass_kernel_spmd(nc, [arrays], core_ids=[0])
    return result.results[0]["out_x"]
```

```python
from contextlib import ExitStack

import numpy as np

import concourse.bass as bass
from concourse import mybir

ALU = mybir.AluOpType
ACT = mybir.ActivationFunctionType
F32 = mybir.dt.float32
F32R = mybir.dt.float32r
AX_X = mybir.AxisListType.X

P = 128
SEQ = 512
D = 1024
MEM = 256
KT = D // P
TT = SEQ // P
FFN = 2816
FT = FFN // P
HEADS = 8
KVH = 2
GRP = HEADS // KVH
HD = 64
NCMP = SEQ // 16 - 1
CMPB = 32
WIN = 256
GH = 4
CH = 64
NCH = SEQ // CH
XH = 4
RH = 4
SH = 16
EPS = 1e-6
MASKED = -1e30
FAR = 40.0

C_Q, C_KV, C_GATE, C_QB = 0, 512, 1280, 1304
C_VB, C_RB, C_AL, C_MERGE = C_QB + 512, C_QB + 1024, C_QB + 1536, C_QB + 1552
TOKW = 2 * P + 3 * HEADS + 16

RING = 4
RAW_RING = 4


class Chain:

    def __init__(self, eng, sem):
        self.eng, self.sem, self.n, self.i, self.per, self.used = eng, sem, 0, None, 0, 0

    def value(self):
        if self.i is None:
            return self.n
        return self.i * self.per + (self.n + self.used)

    def mark(self, ins):
        if self.i is None:
            self.n += 1
        else:
            self.used += 1
        ins.then_inc(self.sem, 1)
        return self.value()

    def wait(self):
        self.eng.wait_ge(self.sem, self.value())

    def __call__(self, ins):
        self.mark(ins)
        self.wait()

    def loop(self, count, per):
        with self.eng.Fori(0, count) as i:
            self.i, self.per, self.used = i, per, 0
            yield i
            assert self.used == per, (self.used, per)
        self.n += count * per
        self.i = None


NSA = [(qt, h) for qt in range(TT) for h in range(HEADS)]
NSA_DEEP = 3
SLOPES = [2.0 ** -(h + 1) for h in range(HEADS)]
SH_D = 64
SB_BANK = (0, 1, 2, 3, 6, 7)
SB = [(pair, j, e) for pair in range(4) for j in reversed(range(TT)) for e in range(2)]
GAIN_ROWS = 83
N_GAIN_LOADS = 12
N_CONV_LOADS = 5 * 4
RET_DECAY = [1.0 - 2.0 ** (-5 - h) for h in range(RH)]

V_GAIN, V_BALPHA, V_GLAG = 0, 80, 82
NORMS = ("ln_mix_g", "ln_mem_g", "ln_x_g", "ln_ffn_g", "ln_final_g",
         "ret_norm_2", "ffn_norm_2a", "sb_norm_2", "ffn_norm_2b", "final_norm_2")

GROUPS = ([("q", 4), ("kv", 4), ("qkb", 4), ("vb", 4), ("tok", 4), ("rb", 4)]
          + [(n + str(h), s) for h in range(2) for n, s in (("mn", 4), ("mg", 4), ("bn", 2), ("bg", 2))]
          + [("out0", 4), ("out1", 4), ("xk", 4), ("xv", 4), ("xq", 4), ("xo0", 2), ("xo1", 2)]
          + [(f"up1_{n}", 4) for n in range(11)] + [("down1_0", 11), ("down1_1", 11)]
          + [(f"{n}{h}", 4) for h in range(RH) for n in ("rqk", "rv", "rg")]
          + [("ro0", 8), ("ro1", 8)]
          + [(f"up2_{n}", 4) for n in range(11)] + [("down2_0", 11), ("down2_1", 11)]
          + [(f"{n}{h}", 4) for h in range(2) for n in ("sq", "sk", "sv")]
          + [("so0", 4), ("so1", 4)]
          + [(f"up3_{n}", 4) for n in range(11)] + [("down3_0", 11), ("down3_1", 11)])
GIDX = {n: i for i, (n, _) in enumerate(GROUPS)}
SLOT0 = [0]
for _n, _s in GROUPS:
    SLOT0.append(SLOT0[-1] + _s)
N_SLOTS = SLOT0[-1]
FIRST_PIECED = 20


def build(nc, a, out):
    with ExitStack() as ctx:
        def sb(name, shape, dt=F32, stack=ctx):
            return stack.enter_context(nc.sbuf_tensor(name, shape, dt))

        def sem(name):
            return ctx.enter_context(nc.semaphore(name))

        ps = ctx.enter_context(nc.psum_tensor("ps", [P, 8, 512], F32))
        x = sb("x", [P, KT, SEQ])
        h_hi = sb("h_hi", [P, KT, SEQ], F32R)
        h_lo = sb("h_lo", [P, KT, SEQ], F32R)
        w_raw = sb("w_raw", [P, RAW_RING, 2, 512])
        w_hi = sb("w_hi", [P, RING, 2, 512], F32R)
        w_lo = sb("w_lo", [P, RING, 2, 512], F32R)
        ident = sb("ident", [P, P])
        mean = sb("mean", [P, P])
        vecs = sb("vecs", [P, 6, 4 * FT])
        rstd = sb("rstd", [P, SEQ])
        eps = sb("eps", [P, 1])
        zero = sb("zero", [P, 1])
        sq = sb("sq", [P, 2, SEQ])
        full = sb("full", [P, 2, SEQ])

        with ExitStack() as m:
            o_hi = sb("o_hi", [P, 8, SEQ], F32R, m)
            o_lo = sb("o_lo", [P, 8, SEQ], F32R, m)
            with ExitStack() as m1:
                tok = sb("tok", [P, TT, TOKW], F32, m1)
                gates = sb("gates", [P, TT, 3 * HEADS], F32, m1)
                gate_b = sb("gate_b", [P, 3 * HEADS], F32, m1)
                qkb = sb("qkb", [P, 4, SEQ], F32, m1)
                vb = sb("vb", [P, TT, 512], F32, m1)
                d_slc = sb("d_slc", [P, SEQ], F32, m1)
                d_win = sb("d_win", [P, WIN + P], F32, m1)
                d_cmp = sb("d_cmp", [P, TT, 32], F32, m1)
                row_ok = sb("row_ok", [P, 1], F32, m1)
                keep = sb("keep", [P, SEQ], F32, m1)
                attT = sb("attT", [P, 2, P], F32, m1)
                caus = sb("caus", [P, CH], F32, m1)
                with ExitStack() as m2:
                    qT = sb("qT", [P, 4, SEQ], F32, m2)
                    kvT = sb("kvT", [P, 4, SEQ], F32, m2)
                    kcT = sb("kcT", [P, 32], F32, m2)
                    vc = sb("vc", [32, KVH, HD], F32, m2)
                    s_buf = sb("s_buf", [P, NSA_DEEP, 928], F32, m2)
                    pT_buf = sb("pT_buf", [P, 2, 8, P], F32, m2)
                    att_st = sb("att_st", [P, NSA_DEEP, 16], F32, m2)
                with ExitStack() as m2:
                    rT = sb("rT", [P, GH, SEQ], F32, m2)
                    alT = sb("alT", [16, SEQ], F32, m2)
                    wal = sb("wal", [16, 256], F32, m2)
                    la = sb("la", [P, SEQ], F32, m2)
                    bcum = sb("bcum", [P, SEQ], F32, m2)
                    ebuf = sb("ebuf", [P, SEQ], F32, m2)
                    ks_t = sb("ks_t", [P, SEQ], F32, m2)
                    ks_tok = sb("ks_tok", [P, TT, P], F32, m2)
                    kd = sb("kd", [P, SEQ], F32, m2)
                    qd = sb("qd", [P, SEQ], F32, m2)
                    dec = sb("dec", [P, NCH], F32, m2)
                    states = sb("states", [P, NCH, P], F32, m2)
            with ExitStack() as m1:
                mx_hi = sb("mx_hi", [P, KT, SEQ], F32R, m1)
                mx_lo = sb("mx_lo", [P, KT, SEQ], F32R, m1)
                gN = sb("gN", [P, 4, SEQ], F32, m1)
                gG = sb("gG", [P, 4, SEQ], F32, m1)
        with ExitStack() as m:
            w1c = sb("w1c", [P, 2, CMPB // 2, P], F32, m)
            w2k = sb("w2k", [P, P], F32, m)
            w2v = sb("w2v", [P, HD], F32, m)
            pos = sb("pos", [CMPB, 2, P], F32, m)
            posT = sb("posT", [P, 2, CMPB], F32, m)
            blk = sb("blk", [P, 2, CMPB // 2, KVH, NCMP], F32, m)
            hid = sb("hid", [P, 2, KVH, 32], F32, m)
        with ExitStack() as m:
            gain_rows = sb("gain_rows", [P, P], F32, m)
            x_tok = sb("x_tok", [P, TT, D], F32, m)
        with ExitStack() as m:
            mem_tok = sb("mem_tok", [P, MEM // P, D], F32, m)
            memT = sb("memT", [P, KT, MEM], F32, m)
            m_hi = sb("m_hi", [P, KT, MEM], F32R, m)
            m_lo = sb("m_lo", [P, KT, MEM], F32R, m)
            xkT = sb("xkT", [P, XH, MEM], F32, m)
            xv = sb("xv", [P, MEM // P, 512], F32, m)
            xqT = sb("xqT", [P, XH, SEQ], F32, m)
            xo_hi = sb("xo_hi", [P, XH, SEQ], F32R, m)
            xo_lo = sb("xo_lo", [P, XH, SEQ], F32R, m)
            xp = sb("xp", [P, 2, MEM], F32, m)
            xpT = sb("xpT", [P, 2, 2, P], F32, m)
            x_st = sb("x_st", [P, 2, 4], F32, m)
            conv_rows = sb("conv_rows", [P, 5, P], F32, m)
        with ExitStack() as m:
            f_hi = sb("f_hi", [P, FT, SEQ], F32R, m)
            f_lo = sb("f_lo", [P, FT, SEQ], F32R, m)
            cu = sb("cu", [P, 2, SEQ], F32, m)
            cv = sb("cv", [P, 2, SEQ], F32, m)
        with ExitStack() as m:
            y_hi = sb("y_hi", [P, 16, SEQ], F32R, m)
            y_lo = sb("y_lo", [P, 16, SEQ], F32R, m)
            rq = sb("rq", [P, 4, SEQ], F32, m)
            rv = sb("rv", [P, TT, 512], F32, m)
            cosT = sb("cosT", [P, SEQ], F32, m)
            sinT = sb("sinT", [P, SEQ], F32, m)
            dmat = sb("dmat", [P, SEQ], F32, m)
            r1 = sb("r1", [P, 2, SEQ], F32, m)
            with ExitStack() as m1:
                rsc = sb("rsc", [P, TT, SEQ], F32, m1)
            with ExitStack() as m1:
                ro = sb("ro", [P, 4, SEQ], F32, m1)
        with ExitStack() as m:
            so_hi = sb("so_hi", [P, 8, SEQ], F32R, m)
            so_lo = sb("so_lo", [P, 8, SEQ], F32R, m)
            sqT = sb("sqT", [P, 4, SEQ], F32, m)
            skT = sb("skT", [P, 4, SEQ], F32, m)
            sv = sb("sv", [P, TT, 512], F32, m)
            s_ez = sb("s_ez", [P, 4, SEQ], F32, m)
            s_sp = sb("s_sp", [P, 4, SEQ], F32, m)
            s_sum = sb("s_sum", [P, 2, SEQ], F32, m)
            s_a = sb("s_a", [P, 4, SEQ], F32, m)
            strict = sb("strict", [P, P], F32, m)
            neg_tri = sb("neg_tri", [P, P], F32, m)
            neg_one = sb("neg_one", [P, P], F32, m)
            unseen_f = sb("unseen_f", [P, P], F32, m)
            unseen = sb("unseen", [P, P], F32R, m)
            ident_r = sb("ident_r", [P, P], F32R, m)
        with ExitStack() as m:
            o_tok = sb("o_tok", [P, TT, D], F32, m)

        raw_loaded = [sem(f"raw_loaded{j}") for j in range(RAW_RING)]
        raw_free = sem("raw_free")
        hi_written = sem("hi_written")
        slot_used = sem("slot_used")
        bank_done = sem("bank_done")
        set_free = [sem("set_free0"), sem("set_free1")]
        in_loaded = sem("in_loaded")
        rows_loaded = sem("rows_loaded")
        conv_loaded = sem("conv_loaded")
        conv_turned = sem("conv_turned")
        conv_read = sem("conv_read")
        gate_loaded = sem("gate_loaded")
        wal_loaded = sem("wal_loaded")
        cw_loaded = sem("cw_loaded")
        cw1_loaded = sem("cw1_loaded")
        cw2_loaded = sem("cw2_loaded")
        mem_loaded = sem("mem_loaded")
        rope_loaded = sem("rope_loaded")
        dmat_loaded = sem("dmat_loaded")
        const_ready = sem("const_ready")
        pool_order = sem("pool_order")
        act_order = sem("act_order")
        dve_order = sem("dve_order")
        turned = sem("turned")
        turned_read = sem("turned_read")
        mem_turned_read = sem("mem_turned_read")
        x_ready = sem("x_ready")
        fin_ready = sem("fin_ready")
        sq_ready = sem("sq_ready")
        sq_used = sem("sq_used")
        root_ready = sem("root_ready")
        rstd_ready = sem("rstd_ready")
        full_ready = sem("full_ready")
        full_hi = sem("full_hi")
        split_ready = sem("split_ready")
        gate_a = sem("gate_a")
        gate_s = sem("gate_s")
        gate_m = sem("gate_m")
        cmp_pe = sem("cmp_pe")
        cmp_blk = sem("cmp_blk")
        cmp_a = sem("cmp_a")
        cmp_b = sem("cmp_b")
        att_s = sem("att_s")
        att_m = sem("att_m")
        att_n = sem("att_n")
        att_e = sem("att_e")
        att_p = sem("att_p")
        att_t = sem("att_t")
        att_c = sem("att_c")
        att_o = sem("att_o")
        att_h = sem("att_h")
        att_r = sem("att_r")
        gla_pe = sem("gla_pe")
        gla_al = sem("gla_al")
        gla_lg = sem("gla_lg")
        gla_x = sem("gla_x")
        gla_v = sem("gla_v")
        gla_ks = sem("gla_ks")
        gla_kt = sem("gla_kt")
        gla_qk = sem("gla_qk")
        gla_st = sem("gla_st")
        gla_sc = sem("gla_sc")
        gla_at = sem("gla_at")
        gla_o = sem("gla_o")
        gla_sq = sem("gla_sq")
        gla_sum = sem("gla_sum")
        gla_rd = sem("gla_rd")
        merged = sem("merged")
        sig_n = sem("sig_n")
        sig_g = sem("sig_g")
        xat_s = sem("xat_s")
        xat_m = sem("xat_m")
        xat_e = sem("xat_e")
        xat_p = sem("xat_p")
        xat_t = sem("xat_t")
        xat_c = sem("xat_c")
        xat_o = sem("xat_o")
        xat_h = sem("xat_h")
        xat_r = sem("xat_r")
        conv_a = sem("conv_a")
        conv_d = sem("conv_d")
        nonlin = sem("nonlin")
        rope_d = sem("rope_d")
        ret_s = sem("ret_s")
        ret_sc = sem("ret_sc")
        ret_o = sem("ret_o")
        ret_cp = sem("ret_cp")
        ret_q = sem("ret_q")
        ret_m = sem("ret_m")
        ret_si = sem("ret_si")
        st_z = sem("st_z")
        st_min = sem("st_min")
        st_l = sem("st_l")
        st_sp = sem("st_sp")
        st_acc = sem("st_acc")
        st_up = sem("st_up")
        st_ex = sem("st_ex")
        st_o = sem("st_o")
        sb_h = sem("sb_h")
        sb_r = sem("sb_r")
        stored = sem("stored")

        block = ctx.enter_context(nc.Block())

        def gain(n, k):
            return vecs[:, 0, 8 * n + k:8 * n + k + 1]

        def bank(n, j):
            return ps[:, 4 * (n % 2) + j, :]

        def vec(r, col):
            return vecs[:, r, col:col + 1] if isinstance(col, int) else vecs[:, r, bass.ds(col, 1)]

        def f_tile(f, t):
            return f[:, t, :] if isinstance(t, int) else f[:, bass.ds(t, 1), :].rearrange("p a n -> p (a n)")

        def inc_at(c):
            u = c // 2
            return ps[:, 2 + 2 * (c % 2) + u // 2, 256 * (u % 2):256 * (u % 2) + 256]

        def sb_bank(it):
            return ps[:, SB_BANK[it % len(SB_BANK)], :]

        def updates(half, it):
            pair, j, e = SB[it]
            return 24 * half + 6 * pair + (2 * (TT - 1 - j) + e + 1 if j else 6)

        CONV0 = {1: 0, 2: 2 * 11, 3: 6 * 11}

        SPLITS = {}
        n_split = 0
        for what, n in (("mix", 8), ("gla", 4), ("mx", 8), ("mem", 8), ("xn", 8), ("ffn1n", 8), ("ffn1", FT), ("retn", 8), ("ret", 16),
                        ("ffn2n", 8), ("ffn2", FT), ("sbn", 8), ("ffn3n", 8), ("ffn3", FT)):
            SPLITS[what] = n_split
            n_split += n

        NORM_ORDER = ["mix", "mem", "xn", "ffn1n", "fin1", "retn", "ffn2n", "sbn", "ffn3n", "fin"]
        NORM_AT = {n: i for i, n in enumerate(NORM_ORDER)}
        GAIN_OF = {"mix": 0, "mem": 1, "xn": 2, "ffn1n": 3, "fin1": 4, "retn": 5, "ffn2n": 6,
                   "sbn": 7, "ffn3n": 8, "fin": 9}
        ROOTS = ["mix", "gla0", "gla1", "gla2", "gla3", "mem", "xn", "ffn1n", "fin1", "retn",
                 "ret0", "ret1", "ret2", "ret3", "ffn2n", "sbn", "ffn3n", "fin"]
        ROOT_AT = {n: i for i, n in enumerate(ROOTS)}
        X_AT = {"mix": 0, "xn": 8, "ffn1n": 16, "fin1": 24, "retn": 32, "ffn2n": 40, "sbn": 48,
                "ffn3n": 56, "fin": 64}
        NORM_BANK = {"mix": 7, "mem": 3, "xn": 7, "retn": 7}
        for name, first in (("ffn1n", "xo0"), ("fin1", "down1_0"), ("ffn2n", "ro0"), ("sbn", "down2_0"),
                            ("ffn3n", "so0"), ("fin", "down3_0")):
            NORM_BANK[name] = 4 * (GIDX[first] % 2) + 3

        @block.sync
        def _(sp):
            x2 = a["x"][0].rearrange("(t p) d -> p t d", p=P)
            for t in range(TT):
                sp.dma_start(x_tok[:, t, :], x2[:, t, :]).then_inc(in_loaded, 16)

            w_in = a["w_in"][0]
            w4 = w_in.rearrange("(k p) n -> p k n", p=P)
            for g in range(FIRST_PIECED):
                if g >= RAW_RING:
                    sp.wait_ge(raw_free, g - RAW_RING + 1)
                k0, j = 2 * (g % 4), g % RAW_RING
                if g < 4:
                    for k in range(2):
                        src = w4[:, k0 + k, C_Q:C_Q + 512].rearrange("p (a i d) -> p i a d", a=2, i=4)
                        for b in range(2):
                            dst = w_raw[:, j, k, :].rearrange("p (i a d) -> p i a d", a=2, i=4)
                            sp.dma_start(dst[:, :, b, :], src[:, :, b, :]).then_inc(raw_loaded[j], 16)
                elif g < 8:
                    for dst0, c0, n in ((0, C_KV, 384), (384, C_KV + 512, 128)):
                        for k in range(2):
                            sp.dma_start(w_raw[:, j, k, dst0:dst0 + n], w4[:, k0 + k, c0:c0 + n])\
                                .then_inc(raw_loaded[j], 16)
                elif g < 16:
                    for c0 in (0, 256):
                        for k in range(2):
                            c = (C_QB if g < 12 else C_VB) + c0
                            sp.dma_start(w_raw[:, j, k, c0:c0 + 256], w4[:, k0 + k, c:c + 256])\
                                .then_inc(raw_loaded[j], 16)
                else:
                    for dst0, c0, n in ((0, C_KV + 384, 128), (128, C_KV + 640, 128),
                                        (256, C_GATE, 24), (280, C_AL, 16)):
                        sp.dma_start(w_raw[:, j, :, dst0:dst0 + n], w4[:, k0:k0 + 2, c0:c0 + n])\
                            .then_inc(raw_loaded[j], 16)

            def load(g, first, src):
                j = g % RAW_RING
                sp.wait_ge(raw_free, first - RAW_RING + 1)
                for kk in range(2):
                    dst = w_raw[:, j, kk, :]
                    piece = src(kk)
                    if len(piece.shape) == 3:
                        dst = dst.rearrange("p (a n) -> p a n", a=2)
                    sp.dma_start(dst, piece).then_inc(raw_loaded[j], 16)

            def square(g, w, c0, nk=KT):
                wk = w.rearrange("(k p) n -> p k n", p=P)
                for k0 in range(0, nk, 2):
                    load(g, g, lambda kk: wk[:, k0 + kk, c0:c0 + 512])
                    g += 1
                return g

            def squares(g, w, c0, count):
                wk = w.rearrange("(k p) n -> p k n", p=P)
                with sp.Fori(0, count) as i:
                    for k in range(4):
                        load(g + k, i * 4 + (g + k),
                             lambda kk: wk[:, 2 * k + kk, bass.ds(i * 512 + c0, 512)])
                return g + 4 * count

            g = FIRST_PIECED
            g = square(g, w_in, C_RB)
            for h in range(2):
                g = square(g, w_in, C_MERGE + 512 * h)
                g = square(g, w_in, C_MERGE + D + 512 * h)
                g = square(g, a["w_branch_nsa"][0], 512 * h, 4)
                g = square(g, a["w_branch_gla"][0], 512 * h, 4)
            g = squares(g, a["w_out"][0], 0, 2)
            g = squares(g, a["w_xkv"][0], 0, 2)
            g = square(g, a["w_xq"][0], 0)
            sp.wait_ge(full_ready, SPLITS["mx"] + 8)
            convs = [(a["conv_w"][0], a["conv_b"][0])]
            convs += [(a["ffn_conv_w_2"][l][:, FFN * b:FFN * b + FFN], a["ffn_conv_b_2"][l][FFN * b:FFN * b + FFN])
                      for l in range(2) for b in range(2)]
            for r, (w, bias) in enumerate(convs):
                for t in range(3):
                    sp.dma_start(conv_rows[FT * t:FT * t + FT, r, :], w[t].rearrange("(k p) -> k p", p=P))\
                        .then_inc(conv_loaded, 16)
                sp.dma_start(conv_rows[3 * FT:4 * FT, r, :], bias.rearrange("(k p) -> k p", p=P))\
                    .then_inc(conv_loaded, 16)
            for h in range(2):
                g = square(g, a["w_xo"][0], 512 * h, 4)

            def ffn(g, up, down):
                up4 = up.rearrange("(k p) (a n) -> p k a n", p=P, a=2)
                with sp.Fori(0, FT // 2) as i:
                    for k in range(4):
                        load(g + k, i * 4 + (g + k),
                             lambda kk: up4[:, 2 * k + kk, :, bass.ds(i * 256, 256)])
                g += 2 * FT
                for h in range(2):
                    g = square(g, down, 512 * h, FT)
                return g

            g = ffn(g, a["w_up"][0], a["w_down"][0])
            assert g == SLOT0[GIDX["rqk0"]]
            w = a["ret_w_in_2"][0]
            wqk = w[:, 0:2 * D].rearrange("(k p) (a n) -> p k a n", p=P, a=2)
            wk = w.rearrange("(k p) n -> p k n", p=P)
            with sp.Fori(0, RH) as i:
                for k in range(4):
                    load(g + k, i * 12 + (g + k),
                         lambda kk: wqk[:, 2 * k + kk, :, bass.ds(i * 256, 256)])
                for b in range(2):
                    for k in range(4):
                        g2 = g + 4 + 4 * b + k
                        load(g2, i * 12 + g2,
                             lambda kk: wk[:, 2 * k + kk, bass.ds(i * 512 + (2 * D + 2 * D * b), 512)])
            g += 12 * RH
            for h in range(2):
                g = square(g, a["ret_w_out_2"][0], 512 * h, 16)
            g = ffn(g, a["ffn_w_up_2"][0], a["ffn_w_down_2"][0])
            wk2 = a["sb_w_in_2"][0].rearrange("(k p) n -> p k n", p=P)
            with sp.Fori(0, 2) as i:
                for b in range(3):
                    for k in range(4):
                        g2 = g + 4 * b + k
                        load(g2, i * 12 + g2,
                             lambda kk: wk2[:, 2 * k + kk, bass.ds(i * 512 + D * b, 512)])
            g += 24
            g = squares(g, a["sb_w_out_2"][0], 0, 2)
            g = ffn(g, a["ffn_w_up_2"][1], a["ffn_w_down_2"][1])
            assert g == N_SLOTS
            out2 = out[0].rearrange("(t p) d -> p t d", p=P)
            for t in range(TT):
                sp.wait_ge(turned_read, 2 * t + 3)
                sp.dma_start(out2[:, t, :], o_tok[:, t, :]).then_inc(stored, 16)
            sp.wait_ge(stored, 16 * TT)

        @block.gpsimd
        def _(pool):
            order = Chain(pool, pool_order)
            order.mark(nc.gpsimd.memset(ident[:], 0.0))
            order.mark(nc.gpsimd.memset(eps[:], EPS))
            order.mark(nc.gpsimd.memset(zero[:], 0.0))
            order(nc.gpsimd.memset(mean[:], 1.0 / D))
            order(nc.gpsimd.affine_select(out=ident[:], in_=ident[:], compare_op=ALU.not_equal, fill=1.0,
                                          base=0, pattern=[[-1, P]], channel_multiplier=1))
            pool.sem_inc(const_ready, 1)

            def split(j, r, first, loaded):
                pool.wait_ge(raw_loaded[r], loaded)
                if not isinstance(first, int) or first >= RING:
                    pool.wait_ge(slot_used, first - RING + 1)
                nc.gpsimd.tensor_tensor(w_hi[:, j], w_raw[:, r], zero[:].unsqueeze(1).to_broadcast([P, 2, 512]),
                                        ALU.add).then_inc(hi_written, 1)
                pool.wait_ge(hi_written, first + 1)
                nc.gpsimd.tensor_tensor(w_lo[:, j], w_raw[:, r], w_hi[:, j].bitcast(F32), ALU.subtract)\
                    .then_inc(raw_free, 1)

            def split_tok(j, r, first, loaded):
                pool.wait_ge(raw_loaded[r], loaded)
                pool.wait_ge(slot_used, first - RING + 1)
                nc.gpsimd.tensor_tensor(w_hi[:, j, :, 0:TOKW], w_raw[:, r, :, 0:TOKW],
                                        zero[:].unsqueeze(1).to_broadcast([P, 2, TOKW]),
                                        ALU.add).then_inc(hi_written, 1)
                pool.wait_ge(hi_written, first + 1)
                nc.gpsimd.tensor_tensor(w_lo[:, j, :, 0:TOKW], w_raw[:, r, :, 0:TOKW],
                                        w_hi[:, j, :, 0:TOKW].bitcast(F32), ALU.subtract).then_inc(raw_free, 1)

            for g in range(4):
                split(g % RING, g % RAW_RING, g, 64 * (g // RAW_RING + 1))
            order.mark(nc.gpsimd.iota(d_slc[:], pattern=[[1, SEQ]], base=-(SEQ - P), channel_multiplier=-1,
                                      allow_small_or_imprecise_dtypes=True))
            order.mark(nc.gpsimd.iota(d_win[:], pattern=[[1, WIN + P]], base=-WIN, channel_multiplier=-1,
                                      allow_small_or_imprecise_dtypes=True))
            order.mark(nc.gpsimd.iota(d_cmp[:], pattern=[[-P, TT], [16, 32]], base=CMPB - 1, channel_multiplier=-1,
                                      allow_small_or_imprecise_dtypes=True))
            order.mark(nc.gpsimd.memset(row_ok[:], 1.0))
            order(nc.gpsimd.memset(keep[:], 1.0))
            order.mark(nc.gpsimd.affine_select(out=d_slc[:], in_=d_slc[:], compare_op=ALU.is_ge, fill=MASKED,
                                               base=SEQ - P, pattern=[[-1, SEQ]], channel_multiplier=1))
            order.mark(nc.gpsimd.affine_select(out=d_win[:], in_=d_win[:], compare_op=ALU.is_ge, fill=MASKED,
                                               base=WIN, pattern=[[-1, WIN + P]], channel_multiplier=1))
            order.mark(nc.gpsimd.affine_select(out=d_cmp[:], in_=d_cmp[:], compare_op=ALU.is_ge, fill=MASKED,
                                               base=-(CMPB - 1), pattern=[[P, TT], [-16, 32]],
                                               channel_multiplier=1))
            order(nc.gpsimd.affine_select(out=row_ok[:], in_=row_ok[:], compare_op=ALU.is_ge, fill=0.0,
                                          base=-(CMPB - 1), pattern=[[0, 1]], channel_multiplier=1))
            order.mark(nc.gpsimd.affine_select(out=d_win[:], in_=d_win[:], compare_op=ALU.is_ge, fill=MASKED,
                                               base=-1, pattern=[[1, WIN + P]], channel_multiplier=-1))
            order.mark(nc.gpsimd.affine_select(out=keep[:], in_=keep[:], compare_op=ALU.not_equal, fill=0.0,
                                               base=0, pattern=[[0, NCH], [1, CH]], channel_multiplier=0))
            order(nc.gpsimd.memset(attT[:], 0.0))
            for e in range(2):
                order.mark(nc.gpsimd.memset(caus[64 * e:64 * e + 64, :], 1.0))
            order.wait()
            for e in range(2):
                order.mark(nc.gpsimd.affine_select(out=caus[64 * e:64 * e + 64, :], in_=caus[64 * e:64 * e + 64, :],
                                                   compare_op=ALU.is_ge, fill=0.0, base=0, pattern=[[1, CH]],
                                                   channel_multiplier=-1))
            order.wait()
            pool.sem_inc(const_ready, 1)
            for g in range(4, 16):
                split(g % RING, g % RAW_RING, g, 64 * (g // RAW_RING + 1))
            for g in range(16, FIRST_PIECED):
                split_tok(g % RING, g % RAW_RING, g, 64 * (g // RAW_RING + 1))
            base = 64 * (FIRST_PIECED // RAW_RING)
            rest = SLOT0[GIDX["sk0"]] - FIRST_PIECED
            turns = rest // RING

            def rounds(g0, turns, base):
                with pool.Fori(0, turns) as i:
                    for j in range(RING):
                        split((g0 + j) % RING, (g0 + j) % RAW_RING, i * RING + (g0 + j), i * 32 + (base + 32))
                return g0 + turns * RING, base + 32 * turns

            g, base = rounds(FIRST_PIECED, turns, base)
            order.mark(nc.gpsimd.memset(strict[:], 1.0))
            order.mark(nc.gpsimd.memset(neg_tri[:], -1.0))
            order.mark(nc.gpsimd.memset(unseen_f[:], 0.0))
            order.mark(nc.gpsimd.tensor_copy(ident_r[:], ident[:]))
            order(nc.gpsimd.memset(neg_one[:], -1.0))
            order.mark(nc.gpsimd.affine_select(out=unseen_f[:], in_=unseen_f[:], compare_op=ALU.is_gt,
                                               fill=MASKED, base=0, pattern=[[1, P]], channel_multiplier=-1))
            order.mark(nc.gpsimd.affine_select(out=strict[:], in_=strict[:], compare_op=ALU.is_gt, fill=0.0,
                                               base=0, pattern=[[1, P]], channel_multiplier=-1))
            order(nc.gpsimd.affine_select(out=neg_tri[:], in_=neg_tri[:], compare_op=ALU.is_ge, fill=0.0,
                                          base=0, pattern=[[-1, P]], channel_multiplier=1))
            order(nc.gpsimd.tensor_copy(unseen[:], unseen_f[:]))
            pool.sem_inc(const_ready, 1)
            left = N_SLOTS - g
            g, base = rounds(g, left // RING, base)
            for n in range(N_SLOTS - g):
                split(g % RING, g % RAW_RING, g, base + 32)
                g += 1
            assert g == N_SLOTS

        @block.tensor
        def _(pe):
            def mm(o, l, r, start, stop):
                return nc.tensor.matmul(o, l, r, start=start, stop=stop, skip_group_check=True)

            def three(o, w, xx, start, stop):
                mm(o, w[0], xx[0], start, False)
                mm(o, w[0], xx[1], False, False)
                return mm(o, w[1], xx[0], False, stop)

            def bank_free(n):
                if n >= 2:
                    pe.wait_ge(set_free[n % 2], 4 * (n // 2))

            def evacuated(n):
                pe.wait_ge(set_free[n % 2], 4 * (n // 2 + 1))

            def by_feature(n, act_hi, act_lo, width=SEQ, ready=None, g0=None, first=0, k0=0, i4=0,
                           hook=None, slots=None, adds=False):
                g0 = SLOT0[n] if g0 is None else g0
                slots = GROUPS[n][1] if slots is None else slots
                for sl in range(slots):
                    g = g0 + sl
                    pe.wait_ge(raw_free, i4 + (g + 1))
                    for kk in range(2):
                        k = k0 + 2 * sl + kk
                        if ready is not None:
                            pe.wait_ge(split_ready, ready + 2 * sl + kk + 1)
                        for j in range(4):
                            last_mm = three(ps[:, 4 * (n % 2) + j, 0:width],
                                            [w[:, g % RING, kk, P * j:P * j + P] for w in (w_hi, w_lo)],
                                            [t[:, k, 0:width] for t in (act_hi, act_lo)],
                                            first + sl + kk == 0, sl == slots - 1 and kk == 1)
                            if adds and sl == slots - 1 and kk == 1 and j < 3:
                                last_mm.then_inc(bank_done, 1)
                    last_mm.then_inc(slot_used, 1)
                    if hook and sl in hook:
                        hook[sl]()

            def by_token(n, act_hi, act_lo, tiles=TT, width=512, i4=0, ready=None):
                g0 = SLOT0[n]
                for sl in range(GROUPS[n][1]):
                    g = g0 + sl
                    pe.wait_ge(raw_free, i4 + (g + 1))
                    for kk in range(2):
                        k = 2 * sl + kk
                        if ready is not None:
                            pe.wait_ge(split_ready, ready + k + 1)
                        for j in range(tiles):
                            last_mm = three(ps[:, 4 * (n % 2) + j, 0:width],
                                            [t[:, k, P * j:P * j + P] for t in (act_hi, act_lo)],
                                            [w[:, g % RING, kk, 0:width] for w in (w_hi, w_lo)],
                                            k == 0, k == KT - 1)
                    last_mm.then_inc(slot_used, 1)


            def norm_part(name, k, width=SEQ):
                pe.wait_ge(sq_ready, 8 * NORM_AT[name] + k + 1)
                mm(ps[:, NORM_BANK[name], 0:width], mean[:], sq[:, k % 2, 0:width], k == 0, k == KT - 1)\
                    .then_inc(sq_used, 1)

            def norm_sum(name, width=SEQ):
                for k in range(KT):
                    norm_part(name, k, width)

            def last_half(n, act_hi, act_lo, name, ready=None):
                def first_tiles():
                    evacuated(n - 1)
                    for k in range(4):
                        norm_part(name, k)

                assert NORM_BANK[name] // 4 == (n - 1) % 2, name
                by_feature(n, act_hi, act_lo, ready=ready, hook={min(1, GROUPS[n][1] - 1): first_tiles}
                           if GROUPS[n][1] > 2 else {0: first_tiles}, adds=True)
                for k in range(4, KT):
                    norm_part(name, k)
                norm_read(name)
                evacuated(n)

            def norm_read(name):
                pe.wait_ge(root_ready, ROOT_AT[name] + 1)

            pe.wait_ge(const_ready, 1)
            pe.wait_ge(in_loaded, 16 * TT)
            for k in range(KT):
                b = 2 + k % 4
                if k >= 4:
                    pe.wait_ge(x_ready, k - 3)
                for t in range(TT):
                    last = nc.tensor.transpose(ps[:, b, P * t:P * t + P], x_tok[:, t, P * k:P * k + P], ident[:])
                last.then_inc(turned, 1)
                if k >= 2:
                    norm_part("mix", k - 2)
            norm_part("mix", KT - 2)
            norm_part("mix", KT - 1)
            pe.wait_ge(rows_loaded, 16 * N_GAIN_LOADS)
            nc.tensor.transpose(ps[:, 0, 0:GAIN_ROWS], gain_rows[0:GAIN_ROWS, :], ident[0:GAIN_ROWS, 0:GAIN_ROWS])\
                .then_inc(turned, 1)
            pe.wait_ge(turned_read, 1)
            norm_read("mix")

            G = GIDX
            h_ = (h_hi, h_lo)
            by_feature(G["q"], *h_, ready=SPLITS["mix"])
            by_feature(G["kv"], *h_)
            bank_free(G["qkb"])
            pe.wait_ge(cw_loaded, 16 * 4)
            for kv in range(2):
                nc.tensor.transpose(ps[:, 0, CMPB * kv:CMPB * kv + CMPB], pos[0:CMPB, kv, :],
                                    ident[0:CMPB, 0:CMPB]).then_inc(cmp_pe, 1)
            pe.wait_ge(cmp_b, 1)
            by_feature(G["qkb"], *h_)

            bank_free(G["vb"])
            pe.wait_ge(cw1_loaded, 32)
            pe.wait_ge(cmp_blk, 2)
            for kv in range(2):
                for c in range(CMPB // 2):
                    last = mm(ps[:, 4 + kv, 0:KVH * NCMP], w1c[:, kv, c, :],
                              blk[:, kv, c].rearrange("p h n -> p (h n)"), c == 0, c == CMPB // 2 - 1)
                last.then_inc(cmp_pe, 1)
            pe.wait_ge(cmp_a, 2)
            by_token(G["vb"], *h_)
            bank_free(G["tok"])
            pe.wait_ge(cw2_loaded, 48)
            for h in range(KVH):
                mm(ps[:, h, 0:NCMP], w2k[:], hid[:, 0, h, 0:NCMP], True, True)
                last = mm(ps[0:NCMP, 2 + h, 0:HD], hid[:, 1, h, 0:NCMP], w2v[:], True, True)
            last.then_inc(cmp_pe, 1)
            pe.wait_ge(cmp_b, 2)
            by_token(G["tok"], *h_, width=TOKW)
            evacuated(G["vb"])
            evacuated(G["tok"])

            def nsa_scores(it):
                qt, h = NSA[it]
                r = slice(HD * (h // GRP), HD * (h // GRP) + HD)
                q = qT[r, h % GRP, P * qt:P * qt + P]
                b = 2 * (it % 2)
                if it >= 2:
                    pe.wait_ge(att_m, it - 1)
                mm(ps[:, b, 0:P * (qt + 1)], q, kvT[r, 2, 0:P * (qt + 1)], True, True)
                w0 = P * max(0, qt - 2)
                mm(ps[:, b + 1, 0:P * (qt + 1) - w0], q, kvT[r, 3, w0:P * (qt + 1)], True, True)
                mm(ps[:, b + 1, 384:384 + NCMP], q, kcT[r, 0:NCMP], True, True).then_inc(att_s, 1)

            def nsa_blocks(qt):
                return ([(P * t, P, tok[:, t, 0:P]) for t in range(qt + 1)]
                        + [(512 + P * n, P, tok[:, t, P:2 * P])
                           for n, t in enumerate(range(max(0, qt - 2), qt + 1))]
                        + [(896, NCMP, None)])

            def nsa_turn(it):
                qt, h = NSA[it]
                pe.wait_ge(att_p, it + 1)
                if it >= 1:
                    pe.wait_ge(att_c, it)
                for n, (col, rows, _) in enumerate(nsa_blocks(qt)):
                    last = nc.tensor.transpose(ps[0:rows, 4 + n // 4, P * (n % 4):P * (n % 4) + P],
                                               s_buf[:, it % NSA_DEEP, col:col + rows], ident[:])
                last.then_inc(att_t, 1)

            def nsa_out(it):
                qt, h = NSA[it]
                pe.wait_ge(att_c, it + 1)
                pr = it // 2
                if pr >= 2:
                    pe.wait_ge(att_r, pr - 1)
                kvh = h // GRP
                o = ps[HD * (h % 2):HD * (h % 2) + HD, 6 + pr % 2, 0:P]
                blocks = nsa_blocks(qt)
                for n, (_, rows, v) in enumerate(blocks):
                    v = vc[0:NCMP, kvh, :] if v is None else v[:, HD * kvh:HD * kvh + HD]
                    last = mm(o, v, pT_buf[0:rows, it % 2, n, :], n == 0, n == len(blocks) - 1)
                last.then_inc(att_o, 1)

            for it in range(len(NSA) + 3):
                if it < len(NSA):
                    nsa_scores(it)
                if it >= 3:
                    nsa_out(it - 3)
                if 2 <= it < len(NSA) + 2:
                    nsa_turn(it - 2)
            pe.wait_ge(att_r, 16)
            by_feature(G["rb"], *h_)
            for t in range(TT):
                last = nc.tensor.transpose(ps[0:16, 0, P * t:P * t + P], tok[:, t, TOKW - 16:TOKW], ident[:])
            last.then_inc(gla_pe, 1)
            pe.wait_ge(gla_al, 1)
            pe.wait_ge(wal_loaded, 16)
            for pr in range(2):
                if pr:
                    pe.wait_ge(gla_lg, 1)
                mm(ps[:, 1, :], wal[:, P * pr:P * pr + P], alT[:], True, True).then_inc(gla_pe, 1)
                pe.wait_ge(gla_ks, pr + 1)
                for t in range(TT):
                    last = nc.tensor.transpose(ps[:, 0, P * t:P * t + P], ks_t[:, P * t:P * t + P], ident[:])
                last.then_inc(gla_pe, 1)
                pe.wait_ge(gla_kt, pr + 1)
                evacuated(G["rb"])
                for c in range(NCH - 1):
                    r = slice(CH * (c % 2), CH * (c % 2) + CH)
                    last = mm(inc_at(c), ks_tok[r, c // 2, :],
                              vb[r, c // 2, 256 * pr:256 * pr + 256], True, True)
                last.then_inc(gla_pe, 1)
                pe.wait_ge(gla_qk, pr + 1)
                pe.wait_ge(gla_st, pr + 1)
                for e in range(2):
                    head = 2 * pr + e
                    r = slice(CH * e, CH * e + CH)
                    evacuated(G["rb"])
                    if head:
                        pe.wait_ge(gla_rd, head)
                    for t in range(TT):
                        u = 4 * head + t
                        if u >= 2:
                            pe.wait_ge(gla_at, u - 1)
                        for q in range(2):
                            s = slice(P * t + CH * q, P * t + CH * q + CH)
                            last = mm(ps[CH * q:CH * q + CH, 2 + u % 2, CH * q:CH * q + CH], kd[r, s], qd[r, s],
                                      True, True)
                        last.then_inc(gla_sc, 1)
                        pe.wait_ge(gla_at, u + 1)
                        mm(ps[:, 6, P * t:P * t + P], vb[:, t, P * head:P * head + P], attT[:, u % 2, :],
                           True, False)
                        for c in (2 * t, 2 * t + 1):
                            if c:
                                last = mm(ps[:, 6, CH * c:CH * c + CH], states[r, c, :],
                                          qd[r, CH * c:CH * c + CH], False, True)
                        last.then_inc(gla_o, 1)
                    pe.wait_ge(gla_sq, head + 1)
                    mm(ps[:, 7, :], mean[:], sq[:, 0, :], True, True).then_inc(gla_sum, 1)
            pe.wait_ge(gla_rd, GH)

            for h in range(2):
                bank_free(G[f"mn{h}"])
                by_feature(G[f"mn{h}"], *h_)
                bank_free(G[f"mg{h}"])
                by_feature(G[f"mg{h}"], *h_)
                pe.wait_ge(split_ready, SPLITS["gla"] + 4)
                pe.wait_ge(att_r, 16)
                bank_free(G[f"bn{h}"])
                by_feature(G[f"bn{h}"], o_hi, o_lo)
                bank_free(G[f"bg{h}"])
                by_feature(G[f"bg{h}"], o_hi, o_lo, k0=4)
            bank_free(G["out0"])
            by_feature(G["out0"], mx_hi, mx_lo, ready=SPLITS["mx"], adds=True)
            bank_free(G["out1"])
            pe.wait_ge(mem_loaded, 16)
            for k in range(KT):
                if k >= 4:
                    pe.wait_ge(mem_turned_read, k - 3)
                for t in range(MEM // P):
                    last = nc.tensor.transpose(ps[:, 4 + k % 4, P * t:P * t + P], mem_tok[:, t, P * k:P * k + P],
                                               ident[:])
                last.then_inc(turned, 1)
            pe.wait_ge(mem_turned_read, 8)

            def memory_squares():
                evacuated(G["out0"])
                norm_sum("mem", MEM)

            by_feature(G["out1"], mx_hi, mx_lo, hook={0: memory_squares}, adds=True)

            norm_read("mem")
            by_feature(G["xk"], m_hi, m_lo, width=MEM, ready=SPLITS["mem"])
            evacuated(G["out1"])
            norm_sum("xn")
            by_token(G["xv"], m_hi, m_lo, tiles=MEM // P)
            norm_read("xn")
            bank_free(G["xq"])
            by_feature(G["xq"], *h_, ready=SPLITS["xn"])
            evacuated(G["xk"])
            evacuated(G["xv"])
            evacuated(G["xq"])

            def x_scores(it):
                h, qt = it // TT, it % TT
                if it >= 2:
                    pe.wait_ge(xat_e, it - 1)
                mm(ps[:, it % 2, 0:MEM], xqT[:, h, P * qt:P * qt + P], xkT[:, h, :], True, True)\
                    .then_inc(xat_s, 1)

            def x_turn(it):
                pe.wait_ge(xat_p, it + 1)
                if it >= 2:
                    pe.wait_ge(xat_c, it - 1)
                for t in range(MEM // P):
                    last = nc.tensor.transpose(ps[:, 2 + it % 2, P * t:P * t + P], xp[:, it % 2, P * t:P * t + P],
                                               ident[:])
                last.then_inc(xat_t, 1)

            def x_out(it):
                h, qt = it // TT, it % TT
                pe.wait_ge(xat_c, it + 1)
                if h >= 2 and qt == 0:
                    pe.wait_ge(xat_r, h - 1)
                for t in range(MEM // P):
                    last = mm(ps[:, 4 + h % 2, P * qt:P * qt + P], xv[:, t, P * h:P * h + P], xpT[:, it % 2, t, :],
                              t == 0, t == 1)
                last.then_inc(xat_o, 1)

            for it in range(XH * TT + 2):
                if it < XH * TT:
                    x_scores(it)
                if it >= 2:
                    x_out(it - 2)
                if 1 <= it <= XH * TT:
                    x_turn(it - 1)
            pe.wait_ge(conv_loaded, 16 * N_CONV_LOADS)
            for r in range(5):
                last = nc.tensor.transpose(ps[:, r // 4, 4 * FT * (r % 4):4 * FT * (r % 4 + 1)],
                                           conv_rows[0:4 * FT, r, :], ident[0:4 * FT, 0:4 * FT])
            last.then_inc(conv_turned, 1)
            pe.wait_ge(xat_r, XH)
            by_feature(G["xo0"], xo_hi, xo_lo, adds=True)
            bank_free(G["xo1"])
            pe.wait_ge(conv_read, 1)
            last_half(G["xo1"], xo_hi, xo_lo, "ffn1n")

            def ffn(tag, name, then):
                n0 = G[f"up{tag}_0"]
                by_feature(n0, *h_, ready=SPLITS[name])
                with pe.Fori(0, 5) as i:
                    for e in range(2):
                        n = n0 + 1 + e
                        pe.wait_ge(set_free[n % 2], i * 4 + 4 * (n // 2))
                        by_feature(n, *h_, i4=i * 8)
                bank_free(G[f"down{tag}_0"])
                by_feature(G[f"down{tag}_0"], f_hi, f_lo, ready=SPLITS[f"ffn{tag}"], adds=True)
                bank_free(G[f"down{tag}_1"])
                last_half(G[f"down{tag}_1"], f_hi, f_lo, then)

            ffn(1, "ffn1n", "fin1")

            norm_sum("retn")
            norm_read("retn")
            for h in range(RH):
                nq, nv, ng = G[f"rqk{h}"], G[f"rv{h}"], G[f"rg{h}"]
                sa, sc = 4 * (nq % 2), 4 * (nv % 2)
                bank_free(nq)
                if h:
                    pe.wait_ge(root_ready, ROOT_AT[f"ret{h}"])
                by_feature(nq, *h_, ready=SPLITS["retn"] if h == 0 else None)
                bank_free(nv)
                by_token(nv, *h_)
                evacuated(nq)
                for j in range(TT):
                    for kk in range(2):
                        last = mm(ps[:, sa + j, 0:SEQ - P * j], rq[:, 2 + kk, P * j:P * j + P],
                                  rq[:, kk, P * j:SEQ], kk == 0, kk == 1)
                    last.then_inc(ret_s, 1)
                evacuated(nv)
                pe.wait_ge(ret_sc, TT * (h + 1))
                for e in range(4):
                    for j in range(TT):
                        last = mm(ps[:, sc + e, P * j:SEQ], rv[:, j, P * e:P * e + P], rsc[:, j, 0:SEQ - P * j],
                                  j == 0, j == TT - 1)
                    last.then_inc(ret_o, 1)

                def mean_squares():
                    pe.wait_ge(ret_cp, 4 * (h + 1))
                    for e in range(4):
                        pe.wait_ge(ret_q, 4 * h + e + 1)
                        mm(ps[:, sc, :], mean[:], sq[:, e % 2, :], e == 0, e == 3).then_inc(ret_m, 1)

                by_feature(ng, *h_, hook={1: mean_squares})
            bank_free(G["ro0"])
            pe.wait_ge(root_ready, ROOT_AT["ret3"] + 1)
            by_feature(G["ro0"], y_hi, y_lo, ready=SPLITS["ret"], adds=True)
            bank_free(G["ro1"])
            last_half(G["ro1"], y_hi, y_lo, "ffn2n")
            ffn(2, "ffn2n", "sbn")

            pe.wait_ge(const_ready, 3)
            for half in range(2):
                if half:
                    pe.wait_ge(sb_r, 4)
                for name in ("sq", "sk"):
                    n = G[f"{name}{half}"]
                    bank_free(n)
                    by_feature(n, *h_, ready=SPLITS["sbn"] if (name, half) == ("sq", 0) else None)
                n = G[f"sv{half}"]
                bank_free(n)
                by_token(n, *h_)
                for name in ("sq", "sk", "sv"):
                    evacuated(G[f"{name}{half}"])

                def z(it):
                    g = len(SB) * half + it
                    pair, j, e = SB[it]
                    r = slice(SH_D * e, SH_D * e + SH_D)
                    if it >= len(SB_BANK):
                        pe.wait_ge(st_ex, g - len(SB_BANK) + 1)
                    mm(sb_bank(it)[:, 0:SEQ - P * j], skT[r, pair, P * j:P * j + P], sqT[r, pair, P * j:SEQ],
                       True, True).then_inc(st_z, 1)

                def weights(it):
                    g = len(SB) * half + it
                    pair, j, e = SB[it]
                    pe.wait_ge(st_sp, g + 1)
                    o = sb_bank(it)
                    mm(o[:, 0:SEQ - P * j], neg_tri[:], s_sp[:, it % 4, 0:SEQ - P * j], False, False)
                    last = mm(o[:, 0:P], ident_r[:], unseen[:], False, j == TT - 1)
                    if j < TT - 1:
                        pe.wait_ge(st_up, updates(half, it - 2))
                        last = mm(o[:, P:SEQ - P * j], neg_one[:], s_sum[:, e, P * (j + 1):SEQ], False, True)
                    last.then_inc(st_acc, 1)

                def pv(it):
                    g = len(SB) * half + it
                    pair, j, e = SB[it]
                    pe.wait_ge(st_ex, g + 1)
                    if pair >= 2 and j == TT - 1 and e == 0:
                        pe.wait_ge(sb_r, 4 * half + pair - 1)
                    head = 2 * pair + e
                    mm(ps[SH_D * e:SH_D * e + SH_D, 4 + pair % 2, P * j:SEQ], sv[:, j, SH_D * head:SH_D * head + SH_D],
                       s_a[:, it % 4, 0:SEQ - P * j], j == TT - 1, j == 0).then_inc(st_o, 1)

                for it in range(len(SB) + 4):
                    if it < len(SB):
                        z(it)
                    if 2 <= it < len(SB) + 2:
                        weights(it - 2)
                    if 4 <= it:
                        pv(it - 4)
            pe.wait_ge(sb_r, 8)
            by_feature(G["so0"], so_hi, so_lo, adds=True)
            last_half(G["so1"], so_hi, so_lo, "ffn3n")
            ffn(3, "ffn3n", "fin")
            for t in range(TT):
                for b in range(2):
                    u = 2 * t + b
                    if u >= 4:
                        pe.wait_ge(turned_read, u - 2)
                    for k in range(4):
                        if t == 0:
                            pe.wait_ge(fin_ready, 4 * b + k + 1)
                        last = nc.tensor.transpose(ps[:, u % 4, P * k:P * k + P],
                                                   x[:, 4 * b + k, P * t:P * t + P], ident[:])
                    last.then_inc(turned, 1)

        @block.scalar
        def _(act):
            order = Chain(act, act_order)
            G = GIDX

            def group_done(n):
                act.wait_ge(slot_used, SLOT0[n + 1])

            gains = (a["ln_mix_g"][0], a["ln_mem_g"][0], a["ln_x_g"][0], a["ln_ffn_g"][0], a["ln_final_g"],
                     a["ret_norm_2"][0], a["ffn_norm_2"][0], a["sb_norm_2"][0], a["ffn_norm_2"][1],
                     a["final_norm_2"])
            loads = [(gain_rows[8 * i:8 * i + 8, :], src.rearrange("(k p) -> k p", p=P))
                     for i, src in enumerate(gains)]
            loads += [(gain_rows[80:82, :], a["gla_b_alpha"][0].rearrange("(k p) -> k p", p=P)),
                      (gain_rows[82:83, :], a["gla_norm_g"][0:1, :])]
            assert len(loads) == N_GAIN_LOADS
            for dst, src in loads:
                act.dma_start(dst, src).then_inc(rows_loaded, 16)
            act.dma_start(gate_b[:], a["nsa_gate_b"][0].partition_broadcast(P)).then_inc(gate_loaded, 16)
            def squares(name, src=x, width=SEQ, ready=x_ready):
                g0 = 8 * NORM_AT[name]
                act.preload_act_table_set("natural_log_exp_and_others")
                for k in range(KT):
                    g = g0 + k
                    act.wait_ge(ready, X_AT.get(name, 0) + k + 1)
                    if g >= 2:
                        act.wait_ge(sq_used, g - 1)
                    nc.scalar.activation(sq[:, g % 2, 0:width], src[:, k, 0:width], ACT.Square).then_inc(sq_ready, 1)

            def inverse_root(name, src, scale=1.0, width=SEQ):
                nc.scalar.activation(rstd[:, 0:width], src[:, 0:width], ACT.Ln, bias=eps[:, 0:1], scale=scale)\
                    .then_inc(root_ready, 1)
                act.wait_ge(root_ready, ROOT_AT[name] + 1)
                nc.scalar.activation(rstd[:, 0:width], rstd[:, 0:width], ACT.Exp, scale=-0.5)\
                    .then_inc(rstd_ready, 1)

            def norm_root(name, width=SEQ):
                act.wait_ge(sq_used, 8 * NORM_AT[name] + 8)
                inverse_root(name, ps[:, NORM_BANK[name], :], 1.0, width)

            def high(s, dst, width=SEQ, ready=None):
                act.wait_ge(full_ready, (s if ready is None else ready) + 1)
                nc.scalar.activation(dst, full[:, s % 2, 0:width], ACT.Copy).then_inc(full_hi, 1)

            def highs(name, dst, width=SEQ, n=KT):
                for k in range(n):
                    high(SPLITS[name] + k, dst[:, k, 0:width], width)

            squares("mix")
            norm_root("mix")
            act.wait_ge(turned, KT + 1)
            for kv, name in enumerate(("cmp_pos_k", "cmp_pos_v")):
                for h in range(KVH):
                    act.dma_start(pos[:, kv, HD * h:HD * h + HD], a[name][0]).then_inc(cw_loaded, 16)

            for kv, name in enumerate(("cmp_w1_k", "cmp_w1_v")):
                act.dma_start(w1c[:, kv], a[name][0].rearrange("(c p) n -> p c n", p=P)).then_inc(cw1_loaded, 16)
            for h in range(KVH):
                act.dma_start(w2k[:, HD * h:HD * h + HD], a["cmp_w2_k"][0]).then_inc(cw2_loaded, 16)
            act.dma_start(w2v[:], a["cmp_w2_v"][0]).then_inc(cw2_loaded, 16)

            highs("mix", h_hi)
            group_done(G["q"])
            for j in range(4):
                nc.scalar.activation(qT[:, j, :], bank(G["q"], j), ACT.Copy, scale=HD ** -0.5)\
                    .then_inc(set_free[G["q"] % 2], 1)
            group_done(G["qkb"])
            for j in range(4):
                nc.scalar.activation(qkb[:, j, :], bank(G["qkb"], j), ACT.Copy, scale=CH ** -0.5 if j < 2 else 1.0)\
                    .then_inc(set_free[G["qkb"] % 2], 1)
            for kv in range(2):
                act.wait_ge(cmp_pe, 3 + kv)
                nc.scalar.activation(hid[:, kv, :, 0:NCMP],
                                     ps[:, 4 + kv, 0:KVH * NCMP].rearrange("p (h n) -> p h n", h=KVH),
                                     ACT.Gelu_apprx_tanh).then_inc(cmp_a, 1)
            act.wait_ge(gate_a, 1)
            nc.scalar.activation(gates[:], gates[:], ACT.Sigmoid).then_inc(gate_s, 1)

            def nsa_parts(qt):
                return ((896, NCMP), (0, P * (qt + 1)), (512, P * min(3, qt + 1)))

            def nsa_exp(it):
                qt, b = NSA[it][0], it % NSA_DEEP
                act.wait_ge(att_n, it + 1)
                for n, (c, w) in enumerate(nsa_parts(qt)):
                    last = nc.scalar.activation(s_buf[:, b, c:c + w], s_buf[:, b, c:c + w], ACT.Exp,
                                                bias=att_st[:, b, n:n + 1], accum_out=att_st[:, b, 3 + n:4 + n])
                last.then_inc(att_e, 1)

            def nsa_copy(it):
                qt, b = NSA[it][0], it % 2
                nb = qt + 1 + min(3, qt + 1)
                act.wait_ge(att_t, it + 1)
                if it >= 2:
                    act.wait_ge(att_o, it - 1)
                src = ps[:, 4:6, :].rearrange("p a (b c) -> p (a b) c", c=P)
                nc.scalar.activation(pT_buf[:, b, 0:nb, :], src[:, 0:nb, :], ACT.Copy)
                nc.scalar.activation(pT_buf[0:NCMP, b, nb, :], src[0:NCMP, nb, :], ACT.Copy).then_inc(att_c, 1)

            for it in range(len(NSA) + 4):
                if it < len(NSA):
                    nsa_exp(it)
                if 2 <= it < len(NSA) + 2:
                    nsa_copy(it - 2)
                if it >= 5 and it % 2:
                    pr = (it - 5) // 2
                    qt, i = pr // GRP, pr % GRP
                    act.wait_ge(att_o, 2 * pr + 2)
                    nc.scalar.activation(o_hi[:, i, P * qt:P * qt + P], ps[:, 6 + pr % 2, 0:P], ACT.Copy)\
                        .then_inc(att_h, 1)

            group_done(G["rb"])
            for j in range(4):
                nc.scalar.activation(rT[:, j, :], bank(G["rb"], j), ACT.Silu).then_inc(set_free[G["rb"] % 2], 1)
            act.preload_act_table_set("natural_log_exp_and_others")
            act.wait_ge(gla_pe, 1)
            act.dma_start(wal[:], a["gla_w_alpha2"][0]).then_inc(wal_loaded, 16)
            nc.scalar.activation(alT[:], ps[0:16, 0, :], ACT.Copy).then_inc(gla_al, 1)
            for pr in range(2):
                x0 = 6 * pr
                act.wait_ge(gla_v, 3 * pr + 1)
                nc.scalar.activation(ebuf[:], ebuf[:], ACT.Exp, scale=-1.0).then_inc(gla_x, 1)
                act.wait_ge(gla_x, x0 + 1)
                nc.scalar.activation(ebuf[:], ebuf[:], ACT.Ln, bias=1.0).then_inc(gla_x, 1)
                act.wait_ge(gla_v, 3 * pr + 2)
                act.wait_ge(gla_x, x0 + 2)
                nc.scalar.activation(dec[:], bcum[:].rearrange("p (c i) -> p c i", i=CH)[:, :, CH - 1], ACT.Exp,
                                     scale=1.0 / 16).then_inc(gla_x, 1)
                nc.scalar.activation(qd[:], bcum[:], ACT.Exp, scale=1.0 / 16).then_inc(gla_x, 1)
                nc.scalar.activation(kd[:], bcum[:], ACT.Exp, scale=-1.0 / 16).then_inc(gla_x, 1)
                act.wait_ge(gla_v, 3 * pr + 3)
                nc.scalar.activation(ks_t[:], la[:], ACT.Exp, scale=1.0 / 16).then_inc(gla_x, 1)
                act.wait_ge(gla_pe, 3 + 3 * pr)
                nc.scalar.activation(ks_tok[:].rearrange("p t f -> p (t f)"), ps[:, 0, :], ACT.Copy)\
                    .then_inc(gla_kt, 1)
                for e in range(2):
                    head = 2 * pr + e
                    act.wait_ge(gla_o, 4 * head + 4)
                    if head:
                        act.wait_ge(gla_sum, head)
                    nc.scalar.activation(sq[:, 0, :], ps[:, 6, :], ACT.Square).then_inc(gla_sq, 1)
                    act.wait_ge(gla_sum, head + 1)
                    inverse_root(f"gla{head}", ps[:, 7, :], float(D) / P)
                    high(SPLITS["gla"] + head, o_hi[:, 4 + head, :])

            for h in range(2):
                for name, dst, s in ((f"mn{h}", gN, sig_n), (f"mg{h}", gG, sig_g)):
                    n = G[name]
                    group_done(n)
                    if h:
                        act.wait_ge(full_ready, SPLITS["mx"] + 4)
                    for j in range(4):
                        nc.scalar.activation(dst[:, j, :], bank(n, j), ACT.Sigmoid).then_inc(set_free[n % 2], 1)
                for j in range(4):
                    high(SPLITS["mx"] + 4 * h + j, mx_hi[:, 4 * h + j, :])
            act.wait_ge(slot_used, SLOT0[G["bg1"] + 1])
            act.dma_start(mem_tok[:], a["mem"][0].rearrange("(t p) d -> p t d", p=P)).then_inc(mem_loaded, 16)

            squares("mem", memT, MEM, mem_turned_read)
            norm_root("mem", MEM)
            highs("mem", m_hi, MEM)
            squares("xn")
            group_done(G["xk"])
            for j in range(4):
                nc.scalar.activation(xkT[:, j, :], ps[:, 4 * (G["xk"] % 2) + j, 0:MEM], ACT.Copy)\
                    .then_inc(set_free[G["xk"] % 2], 1)
            norm_root("xn")
            highs("xn", h_hi)
            group_done(G["xq"])
            for j in range(4):
                nc.scalar.activation(xqT[:, j, :], bank(G["xq"], j), ACT.Copy, scale=P ** -0.5)\
                    .then_inc(set_free[G["xq"] % 2], 1)
            for it in range(XH * TT + 2):
                b = it % 2
                if it < XH * TT:
                    act.wait_ge(xat_m, it + 1)
                    if it >= 2:
                        act.wait_ge(xat_t, it - 1)
                    nc.scalar.activation(xp[:, b, :], ps[:, b, 0:MEM], ACT.Exp, bias=x_st[:, b, 0:1],
                                         accum_out=x_st[:, b, 1:2]).then_inc(xat_e, 1)
                if 1 <= it <= XH * TT:
                    u = it - 1
                    act.wait_ge(xat_t, u + 1)
                    if u >= 2:
                        act.wait_ge(xat_o, u - 1)
                    nc.scalar.activation(xpT[:, u % 2].rearrange("p t q -> p (t q)"), ps[:, 2 + u % 2, 0:MEM],
                                         ACT.Copy).then_inc(xat_c, 1)
                if it >= TT + 1 and (it - 1) % TT == 0:
                    h = (it - 1) // TT - 1
                    act.wait_ge(xat_o, TT * (h + 1))
                    nc.scalar.activation(xo_hi[:, h, :], ps[:, 4 + h % 2, :], ACT.Copy).then_inc(xat_h, 1)

            def ffn(tag, name, func, two):
                squares(name)
                norm_root(name)
                highs(name, h_hi)
                n0 = G[f"up{tag}_0"]
                row = {1: 1, 2: 2, 3: 4}[tag]

                def group(n, i, c0, g, t, s, nl):
                    act.wait_ge(slot_used, SLOT0[n + 1] + g)
                    per = 4 if two else 2
                    for half in range(1 + two):
                        for e in range(2):
                            col = t + e
                            act.wait_ge(full_ready, s + e - 1)
                            nc.scalar.activation((cv if half else cu)[:, e, :],
                                                 ps[:, 4 * (n % 2) + 2 * half + e, :], ACT.Identity,
                                                 bias=vec(row + half, col + 3 * FT),
                                                 scale=vec(row + half, col + 2 * FT)).then_inc(conv_a, 1)
                    for e in range(2):
                        act.wait_ge(conv_d, c0 + per * 0 + e + 1)
                        nc.scalar.activation(cu[:, e, :], cu[:, e, :], func).then_inc(nonlin, 1)
                    for e in range(2):
                        act.wait_ge(full_ready, s + e + 1)
                        nc.scalar.activation(f_tile(f_hi, t + e), full[:, (s0 + e) % 2, :], ACT.Copy)\
                            .then_inc(full_hi, 1)

                s0 = SPLITS[f"ffn{tag}"]
                per = 4 if two else 2
                cd = CONV0[tag]
                group(n0, None, cd, 0, 0, s0, 0)
                with act.Fori(0, 5) as i:
                    for e in range(2):
                        group(n0 + 1 + e, i, i * (2 * per) + (cd + per * (1 + e)), i * 8, i * 4 + 2 * (1 + e),
                              i * 4 + (s0 + 2 * (1 + e)), 0)

            ffn(1, "ffn1n", ACT.Gelu_apprx_tanh, False)

            squares("fin1")
            norm_root("fin1")
            act.wait_ge(slot_used, SLOT0[G["rqk0"]])
            act.dma_start(cosT[:], a["rope_cos"]).then_inc(rope_loaded, 16)
            act.dma_start(sinT[:], a["rope_sin"]).then_inc(rope_loaded, 16)
            act.dma_start(dmat[:], a["ret_decay"][0]).then_inc(dmat_loaded, 16)
            squares("retn")
            norm_root("retn")
            highs("retn", h_hi)
            for h in range(RH):
                nv, ng = G[f"rv{h}"], G[f"rg{h}"]
                group_done(nv)
                if h:
                    act.wait_ge(ret_o, 4 * h)
                for t in range(TT):
                    nc.scalar.activation(rv[:, t, :], bank(nv, t), ACT.Copy).then_inc(set_free[nv % 2], 1)
                act.wait_ge(ret_o, 4 * h + 4)
                if h < RH - 1:
                    act.wait_ge(ret_sc, TT * (h + 1))
                    act.dma_start(dmat[:], a["ret_decay"][h + 1]).then_inc(dmat_loaded, 16)
                act.preload_act_table_set("natural_log_exp_and_others")
                for e in range(4):
                    nc.scalar.activation(ro[:, e, :], bank(nv, e), ACT.Copy).then_inc(ret_cp, 1)
                for e in range(4):
                    act.wait_ge(ret_cp, 4 * h + e + 1)
                    if 4 * h + e >= 2:
                        act.wait_ge(ret_m, 4 * h + e - 1)
                    nc.scalar.activation(sq[:, e % 2, :], ro[:, e, :], ACT.Square).then_inc(ret_q, 1)
                act.wait_ge(ret_m, 4 * h + 4)
                inverse_root(f"ret{h}", bank(nv, 0), 2.0)
                group_done(ng)
                for e in range(4):
                    s = SPLITS["ret"] + 4 * h + e
                    act.wait_ge(full_ready, s - 1)
                    nc.scalar.activation(r1[:, e % 2, :], bank(ng, e), ACT.Silu).then_inc(set_free[ng % 2], 1)
                    if e:
                        high(s - 1, y_hi[:, 4 * h + e - 1, :])
                high(SPLITS["ret"] + 4 * h + 3, y_hi[:, 4 * h + 3, :])
            ffn(2, "ffn2n", ACT.Silu, True)

            squares("sbn")
            norm_root("sbn")
            highs("sbn", h_hi)
            for half in range(2):
                n = G[f"sq{half}"]
                group_done(n)
                for j in range(4):
                    nc.scalar.activation(sqT[:, j, :], bank(n, j), ACT.Copy, scale=SH_D ** -0.5)\
                        .then_inc(set_free[n % 2], 1)
                n = G[f"sv{half}"]
                group_done(n)
                for j in range(4):
                    nc.scalar.activation(sv[:, j, :], bank(n, j), ACT.Copy).then_inc(set_free[n % 2], 1)
                act.preload_act_table_set("natural_log_exp_and_others")
                for it in range(len(SB) + 3):
                    if it < len(SB):
                        pair, j, e = SB[it]
                        g = len(SB) * half + it
                        ez = s_ez[:, it % 4, 0:SEQ - P * j]
                        act.wait_ge(st_min, g + 1)
                        nc.scalar.activation(ez, ez, ACT.Exp).then_inc(act_order, 1)
                        act.wait_ge(act_order, g + 1)
                        nc.scalar.activation(ez, ez, ACT.Ln, bias=1.0).then_inc(st_l, 1)
                    if it >= 3:
                        u = it - 3
                        pair, j, e = SB[u]
                        w = SEQ - P * j
                        act.wait_ge(st_acc, len(SB) * half + u + 1)
                        if u >= 4:
                            act.wait_ge(st_o, len(SB) * half + u - 3)
                        nc.scalar.activation(s_a[:, u % 4, 0:w], sb_bank(u)[:, 0:w], ACT.Exp).then_inc(st_ex, 1)
                    if it > 8 and it % 8 == 5:
                        pair = it // 8 - 1
                        act.wait_ge(st_o, len(SB) * half + 8 * (pair + 1))
                        nc.scalar.activation(so_hi[:, 4 * half + pair, :], ps[:, 4 + pair % 2, :], ACT.Copy)\
                            .then_inc(sb_h, 1)
                pair = 3
                act.wait_ge(st_o, len(SB) * (half + 1))
                nc.scalar.activation(so_hi[:, 4 * half + pair, :], ps[:, 4 + pair % 2, :], ACT.Copy)\
                    .then_inc(sb_h, 1)
            ffn(3, "ffn3n", ACT.Silu, True)
            squares("fin")
            norm_root("fin")
            for u in range(2 * TT):
                act.wait_ge(turned, 1 + 8 + 8 + u + 1)
                nc.scalar.activation(o_tok[:, u // 2, 512 * (u % 2):512 * (u % 2) + 512], ps[:, u % 4, :], ACT.Copy)\
                    .then_inc(turned_read, 1)

        @block.vector
        def _(dve):
            order = Chain(dve, dve_order)
            G = GIDX
            V = nc.vector

            def group_done(n):
                dve.wait_ge(slot_used, SLOT0[n + 1])

            def scaled_full(s, value):
                if s >= 2:
                    dve.wait_ge(full_hi, s - 1)
                    dve.wait_ge(split_ready, s - 1)
                value(full[:, s % 2, :]).then_inc(full_ready, 1)

            def low(s, hi, lo, width=SEQ):
                dve.wait_ge(full_ready, s + 1)
                dve.wait_ge(full_hi, s + 1)
                V.tensor_tensor(lo, full[:, s % 2, 0:width], hi.bitcast(F32), ALU.subtract).then_inc(split_ready, 1)

            def norm_rstd(name, width=SEQ):
                dve.wait_ge(rstd_ready, ROOT_AT[name] + 1)

            def norm(name, hi, lo, src=x, width=SEQ):
                norm_rstd(name, width)
                s0 = SPLITS[name]
                for k in range(KT + 1):
                    if k < KT:
                        scaled_full(s0 + k, lambda o: V.scalar_tensor_tensor(
                            o[:, 0:width], src[:, k, 0:width], gain(GAIN_OF[name], k), rstd[:, 0:width],
                            ALU.mult, ALU.mult))
                    if k:
                        low(s0 + k - 1, hi[:, k - 1, 0:width], lo[:, k - 1, 0:width], width)

            def norm_in_place(name, ready, done):
                norm_rstd(name)
                for k in range(KT):
                    V.scalar_tensor_tensor(x[:, k, :], x[:, k, :], gain(GAIN_OF[name], k), rstd[:],
                                           ALU.mult, ALU.mult).then_inc(done, 1)

            X_DONE, BANKS_DONE = [8], [0]

            def residual(names, first=0):
                for h, name in enumerate(names, first):
                    n = G[name]
                    for j in range(4):
                        if j < 3:
                            BANKS_DONE[0] += 1
                            dve.wait_ge(bank_done, BANKS_DONE[0])
                        else:
                            group_done(n)
                        V.tensor_tensor(x[:, 4 * h + j, :], x[:, 4 * h + j, :], bank(n, j), ALU.add)\
                            .then_inc(x_ready, 1)
                        X_DONE[0] += 1
                        if j == 3:
                            dve.wait_ge(x_ready, X_DONE[0])
                            for b in range(4):
                                dve.sem_inc(set_free[n % 2], 1)

            for k in range(KT):
                dve.wait_ge(turned, 1 + k)
                V.tensor_copy(x[:, k, :], ps[:, 2 + k % 4, :]).then_inc(x_ready, 1)
            dve.wait_ge(turned, 1 + KT)
            V.tensor_copy(vecs[:, 0, 0:GAIN_ROWS], ps[:, 0, 0:GAIN_ROWS]).then_inc(turned_read, 1)
            dve.wait_ge(turned_read, 1)
            norm("mix", h_hi, h_lo)

            group_done(G["kv"])
            for j in range(4):
                V.tensor_copy(kvT[:, j, :], bank(G["kv"], j)).then_inc(set_free[G["kv"] % 2], 1)
            dve.wait_ge(cmp_pe, 2)
            V.tensor_copy(posT[:].rearrange("p a c -> p (a c)"), ps[:, 0, 0:2 * CMPB]).then_inc(cmp_b, 1)
            dve.wait_ge(cmp_b, 1)
            dve.wait_ge(set_free[G["kv"] % 2], 4 * (G["kv"] // 2 + 1))
            for kv in range(2):
                for h in range(KVH):
                    r = slice(HD * h, HD * h + HD)
                    tokens = kvT[r, kv, :].rearrange("p (n c o) -> p o c n", c=8, o=2)
                    places = posT[r, kv, :].rearrange("p (c o) -> p o c", o=2)
                    for half in range(2):
                        for odd in range(2):
                            last = V.tensor_tensor(blk[HD * odd:HD * odd + HD, kv, 8 * half:8 * half + 8, h, :],
                                                   tokens[:, odd, :, half:half + NCMP],
                                                   places[:, odd, 8 * half:8 * half + 8].unsqueeze(2)
                                                   .to_broadcast([HD, 8, NCMP]), ALU.add)
                last.then_inc(cmp_blk, 1)
            group_done(G["vb"])
            for j in range(4):
                V.tensor_copy(vb[:, j, :], bank(G["vb"], j)).then_inc(set_free[G["vb"] % 2], 1)
            dve.wait_ge(cmp_pe, 5)
            for h in range(KVH):
                order.mark(V.tensor_copy(kcT[HD * h:HD * h + HD, 0:NCMP],
                                         ps[HD * h:HD * h + HD, h, 0:NCMP]))
            V.tensor_copy(vc[0:NCMP, :, :], ps[0:NCMP, 2:4, 0:HD]).then_inc(cmp_b, 1)
            group_done(G["tok"])
            for j in range(4):
                V.tensor_copy(tok[:, j, :], bank(G["tok"], j)[:, 0:TOKW]).then_inc(set_free[G["tok"] % 2], 1)
            dve.wait_ge(gate_loaded, 16)
            dve.wait_ge(set_free[0], 4 * (G["tok"] // 2 + 1))
            V.tensor_tensor(gates[:], tok[:, :, 2 * P:2 * P + 24],
                            gate_b[:].unsqueeze(1).to_broadcast([P, TT, 3 * HEADS]), ALU.add).then_inc(gate_a, 1)
            dve.wait_ge(const_ready, 2)
            dve.wait_ge(gate_s, 1)
            g0 = gates[:, 0, :].rearrange("p (h b) -> p h b", b=3)[:, :, 0]
            V.tensor_scalar(g0, g0, row_ok[:, 0:1], None, ALU.mult).then_inc(gate_m, 1)

            def nsa_bias(it):
                qt, h = NSA[it]
                b, bank0 = it % NSA_DEEP, 2 * (it % 2)
                nk, nw = P * (qt + 1), P * min(3, qt + 1)
                dve.wait_ge(att_s, it + 1)
                if it >= NSA_DEEP:
                    dve.wait_ge(att_t, it - NSA_DEEP + 1)
                order.mark(V.scalar_tensor_tensor(s_buf[:, b, 0:nk], d_slc[:, SEQ - nk:SEQ], SLOPES[h],
                                                  ps[:, bank0, 0:nk], ALU.mult, ALU.add))
                order.mark(V.scalar_tensor_tensor(s_buf[:, b, 512:512 + nw], d_win[:, WIN + P - nw:WIN + P],
                                                  SLOPES[h], ps[:, bank0 + 1, 0:nw], ALU.mult, ALU.add))
                V.scalar_tensor_tensor(s_buf[:, b, 896:896 + NCMP], d_cmp[:, qt, 0:NCMP], SLOPES[h],
                                       ps[:, bank0 + 1, 384:384 + NCMP], ALU.mult, ALU.add).then_inc(att_m, 1)
                order.wait()
                order.mark(V.tensor_reduce(att_st[:, b, 1:2], s_buf[:, b, 0:nk], AX_X, ALU.max, negate=True))
                order.mark(V.tensor_reduce(att_st[:, b, 2:3], s_buf[:, b, 512:512 + nw], AX_X, ALU.max,
                                           negate=True))
                dve.wait_ge(att_m, it + 1)
                V.tensor_reduce(att_st[:, b, 0:1], s_buf[:, b, 896:896 + NCMP], AX_X, ALU.max, negate=True)\
                    .then_inc(att_n, 1)

            def nsa_scale(it):
                qt, h = NSA[it]
                b = it % NSA_DEEP
                nk, nw = P * (qt + 1), P * min(3, qt + 1)
                dve.wait_ge(att_e, it + 1)
                order(V.reciprocal(att_st[:, b, 6:9], att_st[:, b, 3:6]))
                order(V.tensor_tensor(att_st[:, b, 9:12], att_st[:, b, 6:9], gates[:, qt, 3 * h:3 * h + 3],
                                      ALU.mult))
                for n, (c, w) in enumerate(((896, NCMP), (0, nk), (512, nw))):
                    last = V.tensor_scalar(s_buf[:, b, c:c + w], s_buf[:, b, c:c + w], att_st[:, b, 9 + n:10 + n],
                                           None, ALU.mult)
                last.then_inc(att_p, 1)

            dve.wait_ge(gate_m, 1)
            for it in range(len(NSA) + 4):
                if it < len(NSA):
                    nsa_bias(it)
                if 1 <= it <= len(NSA):
                    nsa_scale(it - 1)
                if it >= 5 and it % 2:
                    pr = (it - 5) // 2
                    qt, i = pr // GRP, pr % GRP
                    dve.wait_ge(att_h, pr + 1)
                    V.tensor_tensor(o_lo[:, i, P * qt:P * qt + P], ps[:, 6 + pr % 2, 0:P],
                                    o_hi[:, i, P * qt:P * qt + P].bitcast(F32), ALU.subtract).then_inc(att_r, 1)

            for pr in range(2):
                v0, x0 = 3 * pr, 6 * pr
                dve.wait_ge(gla_pe, 2 + 3 * pr)
                if pr:
                    dve.wait_ge(gla_o, 8)
                    dve.wait_ge(gla_x, 6)
                b_al = vecs[:, 0, V_BALPHA + pr:V_BALPHA + pr + 1]
                V.tensor_scalar(ebuf[:], ps[:, 1, :], b_al, -FAR, ALU.add, ALU.max).then_inc(gla_v, 1)
                V.tensor_scalar(la[:], ps[:, 1, :], b_al, None, ALU.add).then_inc(gla_lg, 1)
                dve.wait_ge(gla_x, x0 + 2)
                dve.wait_ge(gla_lg, pr + 1)
                order(V.scalar_tensor_tensor(la[:], ebuf[:], -1.0, la[:], ALU.mult, ALU.min))
                V.tensor_tensor_scan(bcum[:], keep[:], la[:], 0.0, ALU.mult, ALU.add).then_inc(gla_v, 1)
                dve.wait_ge(gla_v, v0 + 2)
                b3 = bcum[:].rearrange("p (c i) -> p c i", i=CH)
                V.tensor_tensor(la[:].rearrange("p (c i) -> p c i", i=CH),
                                b3[:, :, CH - 1:CH].to_broadcast([P, NCH, CH]), b3, ALU.subtract).then_inc(gla_v, 1)
                dve.wait_ge(gla_x, x0 + 6)
                V.tensor_tensor(ks_t[:], ks_t[:], qkb[:, 2 + pr, :], ALU.mult).then_inc(gla_ks, 1)
                order.mark(V.tensor_tensor(qd[:], qd[:], qkb[:, pr, :], ALU.mult))
                V.tensor_tensor(kd[:], kd[:], qkb[:, 2 + pr, :], ALU.mult).then_inc(gla_qk, 1)
                order(V.memset(states[:, 0, :], 0.0))
                dve.wait_ge(gla_pe, 4 + 3 * pr)
                for c in range(NCH - 1):
                    for e in range(2):
                        r = slice(CH * e, CH * e + CH)
                        ins = V.scalar_tensor_tensor(
                            states[r, c + 1, :], states[r, c, :], dec[r, c:c + 1],
                            inc_at(c)[r, P * e:P * e + P], ALU.mult, ALU.add)
                        if c < NCH - 2 or e == 0:
                            order.mark(ins)
                        else:
                            ins.then_inc(gla_st, 1)
                    order.wait()
                for e in range(2):
                    head = 2 * pr + e
                    for t in range(TT):
                        u = 4 * head + t
                        dve.wait_ge(gla_sc, u + 1)
                        if u >= 2:
                            dve.wait_ge(gla_o, u - 1)
                        for q in range(2):
                            r = slice(CH * q, CH * q + CH)
                            last = V.tensor_tensor(attT[r, u % 2, CH * q:CH * q + CH],
                                                   ps[r, 2 + u % 2, CH * q:CH * q + CH], caus[r, :], ALU.mult)
                        last.then_inc(gla_at, 1)
                    dve.wait_ge(rstd_ready, ROOT_AT[f"gla{head}"] + 1)
                    s = SPLITS["gla"] + head
                    if s >= 2:
                        dve.wait_ge(full_hi, s - 1)
                        dve.wait_ge(split_ready, s - 1)
                    f = full[:, s % 2, :]
                    V.tensor_tensor(f, ps[:, 6, :], rstd[:], ALU.mult).then_inc(gla_rd, 1)
                    dve.wait_ge(gla_rd, head + 1)
                    V.scalar_tensor_tensor(f, f, vecs[:, 0, V_GLAG:V_GLAG + 1], rT[:, head, :], ALU.mult, ALU.mult)\
                        .then_inc(full_ready, 1)
                    low(s, o_hi[:, 4 + head, :], o_lo[:, 4 + head, :])

            for h in range(2):
                for j in range(4):
                    if j == 0:
                        group_done(G[f"bn{h}"])
                        dve.wait_ge(set_free[G[f"mn{h}"] % 2], 4 * (G[f"mn{h}"] // 2 + 1))
                    V.tensor_tensor(gN[:, j, :], gN[:, j, :], bank(G[f"bn{h}"], j), ALU.mult)\
                        .then_inc(set_free[G[f"bn{h}"] % 2], 1)
                group_done(G[f"bg{h}"])
                dve.wait_ge(set_free[G[f"mg{h}"] % 2], 4 * (G[f"mg{h}"] // 2 + 1))
                for j in range(4):
                    V.tensor_tensor(gG[:, j, :], gG[:, j, :], bank(G[f"bg{h}"], j), ALU.mult)\
                        .then_inc(set_free[G[f"bg{h}"] % 2], 1)
                dve.wait_ge(set_free[G[f"bg{h}"] % 2], 4 * (G[f"bg{h}"] // 2 + 1))
                dve.wait_ge(set_free[G[f"bn{h}"] % 2], 4 * (G[f"bn{h}"] // 2 + 1))
                for j in range(4 + 1):
                    s = SPLITS["mx"] + 4 * h + j
                    if j < 4:
                        scaled_full(s, lambda o: V.tensor_tensor(o, gN[:, j, :], gG[:, j, :], ALU.add))
                    if j:
                        low(s - 1, mx_hi[:, 4 * h + j - 1, :], mx_lo[:, 4 * h + j - 1, :])
            residual(("out0",))

            for k in range(KT):
                dve.wait_ge(turned, 1 + 8 + k + 1)
                V.tensor_copy(memT[:, k, :], ps[:, 4 + k % 4, 0:MEM]).then_inc(mem_turned_read, 1)
            norm("mem", m_hi, m_lo, memT, MEM)
            residual(("out1",), 1)
            norm("xn", h_hi, h_lo)
            group_done(G["xv"])
            for j in range(4):
                if j < MEM // P:
                    V.tensor_copy(xv[:, j, :], bank(G["xv"], j)).then_inc(set_free[G["xv"] % 2], 1)
                else:
                    dve.sem_inc(set_free[G["xv"] % 2], 1)
            for it in range(XH * TT + 2):
                b = it % 2
                if it < XH * TT:
                    dve.wait_ge(xat_s, it + 1)
                    V.tensor_reduce(x_st[:, b, 0:1], ps[:, b, 0:MEM], AX_X, ALU.max, negate=True).then_inc(xat_m, 1)
                if 1 <= it <= XH * TT:
                    u = it - 1
                    dve.wait_ge(xat_e, u + 1)
                    order(V.reciprocal(x_st[:, u % 2, 2:3], x_st[:, u % 2, 1:2]))
                    V.tensor_scalar(xp[:, u % 2, :], xp[:, u % 2, :], x_st[:, u % 2, 2:3], None, ALU.mult)\
                        .then_inc(xat_p, 1)
                if it >= TT + 1 and (it - 1) % TT == 0:
                    h = (it - 1) // TT - 1
                    dve.wait_ge(xat_h, h + 1)
                    V.tensor_tensor(xo_lo[:, h, :], ps[:, 4 + h % 2, :], xo_hi[:, h, :].bitcast(F32), ALU.subtract)\
                        .then_inc(xat_r, 1)
            dve.wait_ge(conv_turned, 1)
            V.tensor_copy(vecs[:, 1:5, :].rearrange("p r c -> p (r c)"), ps[:, 0, 0:16 * FT])
            V.tensor_copy(vecs[:, 5, :], ps[:, 1, 0:4 * FT]).then_inc(conv_read, 1)
            residual(("xo0", "xo1"))

            def ffn(tag, name, two):
                norm(name, h_hi, h_lo)
                n0 = G[f"up{tag}_0"]
                row = {1: 1, 2: 2, 3: 4}[tag]
                s0 = SPLITS[f"ffn{tag}"]
                per = 4 if two else 2
                cd = CONV0[tag]
                nl0 = 22 * (tag - 1)

                def taps(dst, src, e, col, r, done, own):
                    V.scalar_tensor_tensor(dst[:, e, 2:SEQ], src[:, 0:SEQ - 2], vec(r, col),
                                           dst[:, e, 2:SEQ], ALU.mult, ALU.add).then_inc(dve_order, 1)
                    dve.wait_ge(dve_order, own)
                    V.scalar_tensor_tensor(dst[:, e, 1:SEQ], src[:, 0:SEQ - 1], vec(r, col + FT),
                                           dst[:, e, 1:SEQ], ALU.mult, ALU.add).then_inc(done, 1)

                base = order.n

                def group(n, c, t, s, nl, own):
                    st = set_free[n % 2]
                    for half in range(1 + two):
                        for e in range(2):
                            u = 2 * half + e
                            dve.wait_ge(conv_a, c + u + 1)
                            taps(cv if half else cu, ps[:, 4 * (n % 2) + u, :], e, t + e, row + half, conv_d,
                                 own + u + 1)
                    for e in range(2):
                        dve.wait_ge(nonlin, nl + e + 1)
                        dve.wait_ge(full_hi, s + e - 1)
                        dve.wait_ge(split_ready, s + e - 1)
                        if two:
                            dve.wait_ge(conv_d, c + 4)
                            V.tensor_tensor(full[:, (s0 + e) % 2, :], cu[:, e, :], cv[:, e, :], ALU.mult)\
                                .then_inc(full_ready, 1)
                        else:
                            V.tensor_tensor(full[:, (s0 + e) % 2, :], cu[:, e, :], ps[:, 4 * (n % 2) + 2 + e, :],
                                            ALU.mult).then_inc(full_ready, 1)
                    dve.wait_ge(full_ready, s + 2)
                    for b in range(4):
                        dve.sem_inc(st, 1)
                    for e in range(2):
                        dve.wait_ge(full_hi, s + e + 1)
                        V.tensor_tensor(f_tile(f_lo, t + e), full[:, (s0 + e) % 2, :],
                                        f_tile(f_hi, t + e).bitcast(F32), ALU.subtract).then_inc(split_ready, 1)

                group(n0, cd, 0, s0, nl0, base)
                with dve.Fori(0, 5) as i:
                    for e in range(2):
                        group(n0 + 1 + e, i * (2 * per) + (cd + per * (1 + e)), i * 4 + 2 * (1 + e),
                              i * 4 + (s0 + 2 * (1 + e)), i * 4 + (nl0 + 2 * (1 + e)),
                              i * (2 * per) + (base + per * (1 + e)))
                order.n = base + 11 * per
                residual((f"down{tag}_0", f"down{tag}_1"))

            ffn(1, "ffn1n", False)

            norm_in_place("fin1", x_ready, x_ready)
            X_DONE[0] += 8
            norm("retn", h_hi, h_lo)
            dve.wait_ge(rope_loaded, 32)
            for h in range(RH):
                nq, ng = G[f"rqk{h}"], G[f"rg{h}"]
                group_done(nq)
                if h:
                    dve.wait_ge(ret_s, TT * h)
                for w in range(2):
                    b0, b1 = bank(nq, 2 * w), bank(nq, 2 * w + 1)
                    order.mark(V.tensor_tensor(rq[:, 2 * w, :], b0, cosT[:], ALU.mult))
                    order.mark(V.tensor_tensor(rq[:, 2 * w + 1, :], b0, sinT[:], ALU.mult))
                    order.mark(V.tensor_tensor(r1[:, 0, :], b1, sinT[:], ALU.mult))
                    V.tensor_tensor(r1[:, 1, :], b1, cosT[:], ALU.mult).then_inc(rope_d, 1)
                    order.wait()
                    dve.wait_ge(rope_d, 2 * h + w + 1)
                    order.mark(V.tensor_tensor(rq[:, 2 * w, :], rq[:, 2 * w, :], r1[:, 0, :], ALU.subtract))
                    order(V.tensor_tensor(rq[:, 2 * w + 1, :], rq[:, 2 * w + 1, :], r1[:, 1, :], ALU.add))
                for b in range(4):
                    dve.sem_inc(set_free[nq % 2], 1)
                dve.wait_ge(dmat_loaded, 16 * (h + 1))
                for j in range(TT):
                    dve.wait_ge(ret_s, TT * h + j + 1)
                    w = SEQ - P * j
                    V.scalar_tensor_tensor(rsc[:, j, 0:w], bank(nq, j)[:, 0:w], 1.0 / 16, dmat[:, 0:w],
                                           ALU.mult, ALU.mult).then_inc(ret_sc, 1)
                dve.wait_ge(rstd_ready, ROOT_AT[f"ret{h}"] + 1)
                for e in range(4 + 1):
                    s = SPLITS["ret"] + 4 * h + e
                    if e < 4:
                        order(V.tensor_tensor(ro[:, e, :], ro[:, e, :], rstd[:], ALU.mult))
                        dve.wait_ge(set_free[ng % 2], 4 * (ng // 2) + e + 1)
                        scaled_full(s, lambda o: V.tensor_tensor(o, ro[:, e, :], r1[:, e % 2, :], ALU.mult))
                    if e:
                        low(s - 1, y_hi[:, 4 * h + e - 1, :], y_lo[:, 4 * h + e - 1, :])
            residual(("ro0", "ro1"))
            ffn(2, "ffn2n", True)

            norm("sbn", h_hi, h_lo)
            dve.wait_ge(const_ready, 3)
            for half in range(2):
                n = G[f"sk{half}"]
                group_done(n)
                for j in range(4):
                    V.tensor_copy(skT[:, j, :], bank(n, j)).then_inc(set_free[n % 2], 1)

                def bounded(it):
                    pair, j, e = SB[it]
                    g = len(SB) * half + it
                    w = SEQ - P * j
                    dve.wait_ge(st_z, g + 1)
                    if it >= 4:
                        dve.wait_ge(st_sp, g - 3)
                    V.tensor_scalar(s_ez[:, it % 4, 0:w], sb_bank(it)[:, 0:w], FAR, None, ALU.min)\
                        .then_inc(st_min, 1)

                def softplus(it):
                    pair, j, e = SB[it]
                    g = len(SB) * half + it
                    w = SEQ - P * j
                    dve.wait_ge(st_l, g + 1)
                    sp = s_sp[:, it % 4, 0:w]
                    if it >= 4:
                        dve.wait_ge(st_acc, g - 3)
                        dve.wait_ge(st_up, updates(half, it - 4))
                        order.wait()
                    order(V.tensor_tensor(sp, sb_bank(it)[:, 0:w], s_ez[:, it % 4, 0:w], ALU.max))
                    V.tensor_tensor(sp[:, 0:P], sp[:, 0:P], strict[:], ALU.mult).then_inc(st_sp, 1)

                def update(it):
                    pair, j, e = SB[it]
                    if j == 0:
                        return
                    g = len(SB) * half + it
                    dve.wait_ge(st_acc, g + 1)
                    dve.wait_ge(st_sp, g + 1)
                    if j < TT - 1:
                        order.mark(V.tensor_tensor(s_sum[:, e, P * (j + 1):SEQ], s_sum[:, e, P * (j + 1):SEQ],
                                                   s_sp[:, it % 4, P:SEQ - P * j], ALU.add))
                    V.tensor_copy(s_sum[:, e, P * j:P * (j + 1)], s_sp[:, it % 4, 0:P]).then_inc(st_up, 1)

                def low_part(pair):
                    i = 4 * half + pair
                    dve.wait_ge(sb_h, i + 1)
                    V.tensor_tensor(so_lo[:, i, :], ps[:, 4 + pair % 2, :], so_hi[:, i, :].bitcast(F32),
                                    ALU.subtract).then_inc(sb_r, 1)

                for it in range(len(SB) + 3):
                    if it < len(SB):
                        bounded(it)
                    if 1 <= it <= len(SB):
                        softplus(it - 1)
                    if it >= 3:
                        update(it - 3)
                    if it > 8 and it % 8 == 5:
                        low_part(it // 8 - 1)
                low_part(3)
            residual(("so0", "so1"))
            ffn(3, "ffn3n", True)
            norm_in_place("fin", x_ready, fin_ready)


def shape_constants():
    pos = np.arange(SEQ, dtype=np.float32)
    inv = (np.float32(10000.0) ** (-np.arange(0, 256, 2, dtype=np.float32) / np.float32(256))).astype(np.float32)
    ang = inv[:, None] * pos[None, :]
    key, query = np.arange(P)[:, None], np.arange(SEQ)[None, :]
    decay = np.stack([np.where(query >= key, np.exp(np.maximum(query - key, 0) * np.log(g)), 0.0)
                      for g in RET_DECAY]).astype(np.float32)
    return {"rope_cos": np.cos(ang).astype(np.float32), "rope_sin": np.sin(ang).astype(np.float32),
            "ret_decay": decay}


def kernel(**inputs):
    import concourse.bacc as bacc
    from concourse.bass_utils import run_bass_kernel_spmd

    nc = bacc.Bacc("TRN2", target_bir_lowering=False, num_devices=1)
    arrays, aps = {}, {}
    for name, value in {**inputs, **shape_constants()}.items():
        v = np.ascontiguousarray(value)
        arrays[f"in_{name}"] = v
        aps[name] = nc.dram_tensor(f"in_{name}", v.shape, mybir.dt.from_np(v.dtype), kind="ExternalInput").ap()
    out = nc.dram_tensor("out_x", (1, SEQ, D), F32, kind="ExternalOutput").ap()
    build(nc, aps, out)
    result = run_bass_kernel_spmd(nc, [arrays], core_ids=[0])
    return result.results[0]["out_x"]
```

```python
from contextlib import ExitStack

import numpy as np

import concourse.bass as bass
from concourse import mybir

ALU = mybir.AluOpType
ACT = mybir.ActivationFunctionType
F32 = mybir.dt.float32
F32R = mybir.dt.float32r
AX_X = mybir.AxisListType.X

P = 128
SEQ = 512
D = 1024
MEM = 256
KT = D // P
TT = SEQ // P
FFN = 2816
FT = FFN // P
HEADS = 8
KVH = 2
GRP = HEADS // KVH
HD = 64
NCMP = SEQ // 16 - 1
CMPB = 32
WIN = 256
GH = 4
CH = 64
NCH = SEQ // CH
XH = 4
RH = 4
EPS = 1e-6
MASKED = -1e30
FAR = 40.0

C_Q, C_KV, C_GATE, C_QB = 0, 512, 1280, 1304
C_VB, C_RB, C_AL, C_MERGE = C_QB + 512, C_QB + 1024, C_QB + 1536, C_QB + 1552
TOKW = 2 * P + 3 * HEADS + 16

RING = 4
RAW_RING = 4


class Chain:

    def __init__(self, eng, sem):
        self.eng, self.sem, self.n = eng, sem, 0

    def mark(self, ins):
        self.n += 1
        ins.then_inc(self.sem, 1)

    def wait(self):
        self.eng.wait_ge(self.sem, self.n)

    def __call__(self, ins):
        self.mark(ins)
        self.wait()


NSA = [(qt, h) for qt in reversed(range(TT)) for h in range(HEADS)]
NSA_DEEP = 4
SLOPES = [2.0 ** -(h + 1) for h in range(HEADS)]
SH_D = 64
SB_BANK = (0, 1, 2, 3, 6, 7)
SB = [(pair, j, e) for pair in range(4) for j in reversed(range(TT)) for e in range(2)]
GAIN_ROWS = 83
N_GAIN_LOADS = 12
N_CONV_LOADS = 5 * 4
RET_DECAY = [1.0 - 2.0 ** (-5 - h) for h in range(RH)]

V_BALPHA, V_GLAG = 80, 82

GROUPS = ([("q", 4), ("kv", 4), ("qkb", 4), ("vb", 4), ("tok", 4), ("rb", 4)]
          + [(n + str(h), s) for h in range(2) for n, s in (("mn", 4), ("mg", 4), ("bn", 2), ("bg", 2))]
          + [("out0", 4), ("out1", 4), ("xk", 4), ("xv", 4), ("xq", 4), ("xo0", 2), ("xo1", 2)]
          + [(f"up1_{n}", 4) for n in range(11)] + [("down1_0", 11), ("down1_1", 11)]
          + [(f"{n}{h}", 4) for h in range(RH) for n in ("rqk", "rv", "rg")]
          + [("ro0", 8), ("ro1", 8)]
          + [(f"up2_{n}", 4) for n in range(11)] + [("down2_0", 11), ("down2_1", 11)]
          + [(f"{n}{h}", 4) for h in range(2) for n in ("sq", "sk", "sv")]
          + [("so0", 4), ("so1", 4)]
          + [(f"up3_{n}", 4) for n in range(11)] + [("down3_0", 11), ("down3_1", 11)])
GIDX = {n: i for i, (n, _) in enumerate(GROUPS)}
SLOT0 = [0]
for _n, _s in GROUPS:
    SLOT0.append(SLOT0[-1] + _s)
N_SLOTS = SLOT0[-1]
FIRST_PIECED = 20


def build(nc, a, out):
    with ExitStack() as ctx:
        def sb(name, shape, dt=F32, stack=ctx):
            return stack.enter_context(nc.sbuf_tensor(name, shape, dt))

        def sem(name):
            return ctx.enter_context(nc.semaphore(name))

        ps = ctx.enter_context(nc.psum_tensor("ps", [P, 8, 512], F32))
        x = sb("x", [P, KT, SEQ])
        h_hi = sb("h_hi", [P, KT, SEQ], F32R)
        h_lo = sb("h_lo", [P, KT, SEQ], F32R)
        w_raw = sb("w_raw", [P, RAW_RING, 2, 512])
        w_hi = sb("w_hi", [P, RING, 2, 512], F32R)
        w_lo = sb("w_lo", [P, RING, 2, 512], F32R)
        ident = sb("ident", [P, P])
        mean = sb("mean", [P, P])
        vecs = sb("vecs", [P, 6, 4 * FT])
        rstd = sb("rstd", [P, SEQ])
        eps = sb("eps", [P, 1])
        zero = sb("zero", [P, 1])
        sq = sb("sq", [P, 2, SEQ])
        full = sb("full", [P, 2, SEQ])

        with ExitStack() as m:
            o_hi = sb("o_hi", [P, 8, SEQ], F32R, m)
            o_lo = sb("o_lo", [P, 8, SEQ], F32R, m)
            with ExitStack() as m1:
                tok = sb("tok", [P, TT, TOKW], F32, m1)
                gates = sb("gates", [P, TT, 3 * HEADS], F32, m1)
                gate_b = sb("gate_b", [P, 3 * HEADS], F32, m1)
                qkb = sb("qkb", [P, 4, SEQ], F32, m1)
                vb = sb("vb", [P, TT, 512], F32, m1)
                d_slc = sb("d_slc", [P, SEQ], F32, m1)
                d_win = sb("d_win", [P, WIN + P], F32, m1)
                d_cmp = sb("d_cmp", [P, TT, 32], F32, m1)
                row_ok = sb("row_ok", [P, 1], F32, m1)
                caus = sb("caus", [P, CH], F32, m1)
                with ExitStack() as m2:
                    qT = sb("qT", [P, 4, SEQ], F32, m2)
                    kvT = sb("kvT", [P, 4, SEQ], F32, m2)
                    kcT = sb("kcT", [P, 32], F32, m2)
                    vc = sb("vc", [32, KVH, HD], F32, m2)
                    s_buf = sb("s_buf", [P, NSA_DEEP, 928], F32, m2)
                    pT_buf = sb("pT_buf", [P, 2, 8, P], F32, m2)
                    att_st = sb("att_st", [P, NSA_DEEP, 16], F32, m2)
                with ExitStack() as m2:
                    rT = sb("rT", [P, GH, SEQ], F32, m2)
                    alT = sb("alT", [16, SEQ], F32, m2)
                    wal = sb("wal", [16, 256], F32, m2)
                    la = sb("la", [P, SEQ], F32, m2)
                    keep = sb("keep", [P, SEQ], F32, m2)
                    bcum = sb("bcum", [P, SEQ], F32, m2)
                    ebuf = sb("ebuf", [P, SEQ], F32, m2)
                    ek = sb("ek", [P, SEQ], F32, m2)
                    ks_t = sb("ks_t", [P, SEQ], F32, m2)
                    ks_tok = sb("ks_tok", [P, 2, TT, P], F32, m2)
                    dec = sb("dec", [P, 2, NCH], F32, m2)
                    states = sb("states", [P, 2, NCH, P], F32, m2)
                    attT = sb("attT", [P, 2, TT, P], F32, m2)
            with ExitStack() as m1:
                mx_hi = sb("mx_hi", [P, KT, SEQ], F32R, m1)
                mx_lo = sb("mx_lo", [P, KT, SEQ], F32R, m1)
                gN = sb("gN", [P, 4, SEQ], F32, m1)
                gG = sb("gG", [P, 4, SEQ], F32, m1)
        with ExitStack() as m:
            w1c = sb("w1c", [P, 2, CMPB // 2, P], F32, m)
            w2k = sb("w2k", [P, P], F32, m)
            w2v = sb("w2v", [P, HD], F32, m)
            pos = sb("pos", [CMPB, 2, P], F32, m)
            posT = sb("posT", [P, 2, CMPB], F32, m)
            blk = sb("blk", [P, 2, CMPB // 2, KVH, NCMP], F32, m)
            hid = sb("hid", [P, 2, KVH, 32], F32, m)
        with ExitStack() as m:
            gain_rows = sb("gain_rows", [P, P], F32, m)
            x_tok = sb("x_tok", [P, TT, D], F32, m)
        with ExitStack() as m:
            mem_tok = sb("mem_tok", [P, MEM // P, D], F32, m)
            memT = sb("memT", [P, KT, MEM], F32, m)
            m_hi = sb("m_hi", [P, KT, MEM], F32R, m)
            m_lo = sb("m_lo", [P, KT, MEM], F32R, m)
            xkT = sb("xkT", [P, XH, MEM], F32, m)
            xv = sb("xv", [P, MEM // P, 512], F32, m)
            xqT = sb("xqT", [P, XH, SEQ], F32, m)
            xo_hi = sb("xo_hi", [P, XH, SEQ], F32R, m)
            xo_lo = sb("xo_lo", [P, XH, SEQ], F32R, m)
            xp = sb("xp", [P, 3, MEM], F32, m)
            xpT = sb("xpT", [P, 2, 2, P], F32, m)
            x_st = sb("x_st", [P, 3, 4], F32, m)
            conv_rows = sb("conv_rows", [P, 5, P], F32, m)
        with ExitStack() as m:
            f_hi = sb("f_hi", [P, FT, SEQ], F32R, m)
            f_lo = sb("f_lo", [P, FT, SEQ], F32R, m)
            cu = sb("cu", [P, 2, SEQ], F32, m)
            cv = sb("cv", [P, 2, SEQ], F32, m)
        with ExitStack() as m:
            y_hi = sb("y_hi", [P, 16, SEQ], F32R, m)
            y_lo = sb("y_lo", [P, 16, SEQ], F32R, m)
            rq = sb("rq", [P, 4, SEQ], F32, m)
            rv = sb("rv", [P, TT, 512], F32, m)
            cosT = sb("cosT", [P, SEQ], F32, m)
            sinT = sb("sinT", [P, SEQ], F32, m)
            dmat = sb("dmat", [P, SEQ], F32, m)
            r1 = sb("r1", [P, 2, SEQ], F32, m)
            with ExitStack() as m1:
                rsc = sb("rsc", [P, TT, SEQ], F32, m1)
            with ExitStack() as m1:
                ro = sb("ro", [P, 4, SEQ], F32, m1)
        with ExitStack() as m:
            so_hi = sb("so_hi", [P, 8, SEQ], F32R, m)
            so_lo = sb("so_lo", [P, 8, SEQ], F32R, m)
            sqT = sb("sqT", [P, 4, SEQ], F32, m)
            skT = sb("skT", [P, 4, SEQ], F32, m)
            sv = sb("sv", [P, TT, 512], F32, m)
            s_ez = sb("s_ez", [P, 4, SEQ], F32, m)
            s_sp = sb("s_sp", [P, 4, SEQ], F32, m)
            s_sum = sb("s_sum", [P, 2, SEQ], F32, m)
            s_a = sb("s_a", [P, 4, SEQ], F32, m)
            strict = sb("strict", [P, P], F32, m)
            neg_tri = sb("neg_tri", [P, P], F32, m)
            neg_one = sb("neg_one", [P, P], F32, m)
            unseen_f = sb("unseen_f", [P, P], F32, m)
            unseen = sb("unseen", [P, P], F32R, m)
            ident_r = sb("ident_r", [P, P], F32R, m)
        with ExitStack() as m:
            o_tok = sb("o_tok", [P, TT, D], F32, m)

        raw_loaded = [sem(f"raw_loaded{j}") for j in range(RAW_RING)]
        raw_free = sem("raw_free")
        hi_written = sem("hi_written")
        slot_used = sem("slot_used")
        bank_done = sem("bank_done")
        set_free = [sem("set_free0"), sem("set_free1")]
        in_loaded = sem("in_loaded")
        rows_loaded = sem("rows_loaded")
        conv_loaded = sem("conv_loaded")
        conv_turned = sem("conv_turned")
        conv_read = sem("conv_read")
        gate_loaded = sem("gate_loaded")
        wal_loaded = sem("wal_loaded")
        cw_loaded = sem("cw_loaded")
        cw1_loaded = sem("cw1_loaded")
        cw2_loaded = sem("cw2_loaded")
        mem_loaded = sem("mem_loaded")
        rope_loaded = sem("rope_loaded")
        dmat_loaded = sem("dmat_loaded")
        const_ready = sem("const_ready")
        pool_order = sem("pool_order")
        act_order = sem("act_order")
        dve_order = sem("dve_order")
        turned = sem("turned")
        turned_read = sem("turned_read")
        mem_turned_read = sem("mem_turned_read")
        x_ready = sem("x_ready")
        fin_ready = sem("fin_ready")
        sq_ready = sem("sq_ready")
        sq_used = sem("sq_used")
        weighted_ready = sem("weighted_ready")
        weighted_used = sem("weighted_used")
        weighted_mean = sem("weighted_mean")
        sq_added = sem("sq_added")
        root_ready = sem("root_ready")
        rstd_ready = sem("rstd_ready")
        full_ready = sem("full_ready")
        full_hi = sem("full_hi")
        split_ready = sem("split_ready")
        gate_a = sem("gate_a")
        gate_s = sem("gate_s")
        gate_m = sem("gate_m")
        cmp_pe = sem("cmp_pe")
        cmp_blk = sem("cmp_blk")
        cmp_a = sem("cmp_a")
        cmp_b = sem("cmp_b")
        att_s = sem("att_s")
        att_m = sem("att_m")
        att_n = sem("att_n")
        att_e = sem("att_e")
        att_p = sem("att_p")
        att_t = sem("att_t")
        att_c = sem("att_c")
        att_o = sem("att_o")
        att_h = sem("att_h")
        att_r = sem("att_r")
        gla_pe = sem("gla_pe")
        gla_al = sem("gla_al")
        gla_lg = sem("gla_lg")
        gla_x = sem("gla_x")
        gla_v = sem("gla_v")
        gla_ks = sem("gla_ks")
        gla_kt = sem("gla_kt")
        gla_qk = sem("gla_qk")
        gla_st = sem("gla_st")
        gla_sc = sem("gla_sc")
        gla_at = sem("gla_at")
        gla_o = sem("gla_o")
        gla_sq = sem("gla_sq")
        gla_sum = sem("gla_sum")
        gla_rd = sem("gla_rd")
        merged = sem("merged")
        sig_n = sem("sig_n")
        sig_g = sem("sig_g")
        xat_s = sem("xat_s")
        xat_m = sem("xat_m")
        xat_e = sem("xat_e")
        xat_p = sem("xat_p")
        xat_t = sem("xat_t")
        xat_c = sem("xat_c")
        xat_o = sem("xat_o")
        xat_h = sem("xat_h")
        xat_r = sem("xat_r")
        conv_a = sem("conv_a")
        conv_d = sem("conv_d")
        nonlin = sem("nonlin")
        rope_d = sem("rope_d")
        ret_s = sem("ret_s")
        ret_sc = sem("ret_sc")
        ret_o = sem("ret_o")
        ret_cp = sem("ret_cp")
        ret_q = sem("ret_q")
        ret_m = sem("ret_m")
        ret_si = sem("ret_si")
        st_z = sem("st_z")
        st_min = sem("st_min")
        st_l = sem("st_l")
        st_sp = sem("st_sp")
        st_acc = sem("st_acc")
        st_up = sem("st_up")
        st_ex = sem("st_ex")
        st_o = sem("st_o")
        sb_h = sem("sb_h")
        sb_r = sem("sb_r")
        stored = sem("stored")

        block = ctx.enter_context(nc.Block())

        def gain(n, k):
            return vecs[:, 0, 8 * n + k:8 * n + k + 1]

        def bank(n, j):
            return ps[:, 4 * (n % 2) + j, :]

        def vec(r, col):
            return vecs[:, r, col:col + 1] if isinstance(col, int) else vecs[:, r, bass.ds(col, 1)]

        def f_tile(f, t):
            return f[:, t, :] if isinstance(t, int) else f[:, bass.ds(t, 1), :].rearrange("p a n -> p (a n)")

        def inc_at(pr, c, e):
            return ps[CH * e:CH * e + CH, 6 - 2 * pr + c % 2, P * (c // 2):P * (c // 2) + P]

        def gla_bank(head):
            return ps[:, (6, 7, 4, 5)[head], :]

        def gla_mean_bank(head):
            return ps[:, (0, 1, 6, 7)[head], :]

        def sb_bank(it):
            return ps[:, SB_BANK[it % len(SB_BANK)], :]

        def updates(half, it):
            pair, j, e = SB[it]
            return 24 * half + 6 * pair + (2 * (TT - 1 - j) + e + 1 if j else 6)

        CONV0 = {1: 0, 2: 2 * 11, 3: 6 * 11}

        SPLITS = {}
        n_split = 0
        for what, n in (("mix", 8), ("gla", 4), ("mx", 8), ("mem", 8), ("xn", 8), ("ffn1n", 8), ("ffn1", FT),
                        ("retn", 8), ("ret", 16), ("ffn2n", 8), ("ffn2", FT), ("sbn", 8), ("ffn3n", 8),
                        ("ffn3", FT)):
            SPLITS[what] = n_split
            n_split += n

        NORM_ORDER = ["mix", "mem", "xn", "ffn1n", "fin1", "ffn2n", "sbn", "ffn3n", "fin"]
        NORM_AT = {n: i for i, n in enumerate(NORM_ORDER)}
        GAIN_OF = {"mix": 0, "mem": 1, "xn": 2, "ffn1n": 3, "fin1": 4, "retn": 5, "ffn2n": 6,
                   "sbn": 7, "ffn3n": 8, "fin": 9}
        ROOTS = ["mix", "gla0", "gla1", "gla2", "gla3", "mem", "xn", "ffn1n", "fin1", "retn",
                 "ret0", "ret1", "ret2", "ret3", "ffn2n", "sbn", "ffn3n", "fin"]
        ROOT_AT = {n: i for i, n in enumerate(ROOTS)}
        X_AT = {"mix": 0, "xn": 8, "ffn1n": 16, "fin1": 24, "retn": 32, "ffn2n": 40, "sbn": 48,
                "ffn3n": 56, "fin": 64}
        ADDED = ["ffn1n", "fin1", "ffn2n", "sbn", "ffn3n", "fin"]
        NORM_BANK = {"mix": 7, "mem": 3, "xn": 7, "retn": 4 * (GIDX["down1_0"] % 2) + 2}
        for name, first in (("ffn1n", "xo0"), ("fin1", "down1_0"), ("ffn2n", "ro0"), ("sbn", "down2_0"),
                            ("ffn3n", "so0"), ("fin", "down3_0")):
            NORM_BANK[name] = 4 * (GIDX[first] % 2) + 3

        @block.sync
        def _(sp):
            x2 = a["x"][0].rearrange("(t p) d -> p t d", p=P)
            for t in range(TT):
                sp.dma_start(x_tok[:, t, :], x2[:, t, :]).then_inc(in_loaded, 16)

            w_in = a["w_in"][0]
            w4 = w_in.rearrange("(k p) n -> p k n", p=P)
            for g in range(FIRST_PIECED):
                if g >= RAW_RING:
                    sp.wait_ge(raw_free, g - RAW_RING + 1)
                k0, j = 2 * (g % 4), g % RAW_RING
                if g < 4:
                    for k in range(2):
                        src = w4[:, k0 + k, C_Q:C_Q + 512].rearrange("p (a i d) -> p i a d", a=2, i=4)
                        for b in range(2):
                            dst = w_raw[:, j, k, :].rearrange("p (i a d) -> p i a d", a=2, i=4)
                            sp.dma_start(dst[:, :, b, :], src[:, :, b, :]).then_inc(raw_loaded[j], 16)
                elif g < 8:
                    for dst0, c0, n in ((0, C_KV, 384), (384, C_KV + 512, 128)):
                        for k in range(2):
                            sp.dma_start(w_raw[:, j, k, dst0:dst0 + n], w4[:, k0 + k, c0:c0 + n])\
                                .then_inc(raw_loaded[j], 16)
                elif g < 16:
                    for c0 in (0, 256):
                        for k in range(2):
                            c = (C_QB if g < 12 else C_VB) + c0
                            sp.dma_start(w_raw[:, j, k, c0:c0 + 256], w4[:, k0 + k, c:c + 256])\
                                .then_inc(raw_loaded[j], 16)
                else:
                    for dst0, c0, n in ((0, C_KV + 384, 128), (128, C_KV + 640, 128),
                                        (256, C_GATE, 24), (280, C_AL, 16)):
                        sp.dma_start(w_raw[:, j, :, dst0:dst0 + n], w4[:, k0:k0 + 2, c0:c0 + n])\
                            .then_inc(raw_loaded[j], 16)

            def load(g, first, src):
                j = g % RAW_RING
                sp.wait_ge(raw_free, first - RAW_RING + 1)
                for kk in range(2):
                    dst = w_raw[:, j, kk, :]
                    piece = src(kk)
                    if len(piece.shape) == 3:
                        dst = dst.rearrange("p (a n) -> p a n", a=2)
                    sp.dma_start(dst, piece).then_inc(raw_loaded[j], 16)

            def square(g, w, c0, nk=KT):
                wk = w.rearrange("(k p) n -> p k n", p=P)
                for k0 in range(0, nk, 2):
                    load(g, g, lambda kk: wk[:, k0 + kk, c0:c0 + 512])
                    g += 1
                return g

            def squares(g, w, c0, count):
                wk = w.rearrange("(k p) n -> p k n", p=P)
                with sp.Fori(0, count) as i:
                    for k in range(4):
                        load(g + k, i * 4 + (g + k),
                             lambda kk: wk[:, 2 * k + kk, bass.ds(i * 512 + c0, 512)])
                return g + 4 * count

            g = FIRST_PIECED
            g = square(g, w_in, C_RB)
            for h in range(2):
                g = square(g, w_in, C_MERGE + 512 * h)
                g = square(g, w_in, C_MERGE + D + 512 * h)
                g = square(g, a["w_branch_nsa"][0], 512 * h, 4)
                g = square(g, a["w_branch_gla"][0], 512 * h, 4)
            g = squares(g, a["w_out"][0], 0, 2)
            g = squares(g, a["w_xkv"][0], 0, 2)
            g = square(g, a["w_xq"][0], 0)
            sp.wait_ge(full_ready, SPLITS["mx"] + 8)
            convs = [(a["conv_w"][0], a["conv_b"][0])]
            convs += [(a["ffn_conv_w_2"][l][:, FFN * b:FFN * b + FFN], a["ffn_conv_b_2"][l][FFN * b:FFN * b + FFN])
                      for l in range(2) for b in range(2)]
            for r, (w, bias) in enumerate(convs):
                for t in range(3):
                    sp.dma_start(conv_rows[FT * t:FT * t + FT, r, :], w[t].rearrange("(k p) -> k p", p=P))\
                        .then_inc(conv_loaded, 16)
                sp.dma_start(conv_rows[3 * FT:4 * FT, r, :], bias.rearrange("(k p) -> k p", p=P))\
                    .then_inc(conv_loaded, 16)
            for h in range(2):
                g = square(g, a["w_xo"][0], 512 * h, 4)

            def ffn(g, up, down):
                up4 = up.rearrange("(k p) (a n) -> p k a n", p=P, a=2)
                with sp.Fori(0, FT // 2) as i:
                    for k in range(4):
                        load(g + k, i * 4 + (g + k),
                             lambda kk: up4[:, 2 * k + kk, :, bass.ds(i * 256, 256)])
                g += 2 * FT
                for h in range(2):
                    g = square(g, down, 512 * h, FT)
                return g

            g = ffn(g, a["w_up"][0], a["w_down"][0])
            assert g == SLOT0[GIDX["rqk0"]]
            w = a["ret_w_in_2"][0]
            wqk = w[:, 0:2 * D].rearrange("(k p) (a n) -> p k a n", p=P, a=2)
            wk = w.rearrange("(k p) n -> p k n", p=P)
            with sp.Fori(0, RH) as i:
                for k in range(4):
                    load(g + k, i * 12 + (g + k),
                         lambda kk: wqk[:, 2 * k + kk, :, bass.ds(i * 256, 256)])
                for b in range(2):
                    for k in range(4):
                        g2 = g + 4 + 4 * b + k
                        load(g2, i * 12 + g2,
                             lambda kk: wk[:, 2 * k + kk, bass.ds(i * 512 + (2 * D + 2 * D * b), 512)])
            g += 12 * RH
            for h in range(2):
                g = square(g, a["ret_w_out_2"][0], 512 * h, 16)
            g = ffn(g, a["ffn_w_up_2"][0], a["ffn_w_down_2"][0])
            wk2 = a["sb_w_in_2"][0].rearrange("(k p) n -> p k n", p=P)
            with sp.Fori(0, 2) as i:
                for b in range(3):
                    for k in range(4):
                        g2 = g + 4 * b + k
                        load(g2, i * 12 + g2,
                             lambda kk: wk2[:, 2 * k + kk, bass.ds(i * 512 + D * b, 512)])
            g += 24
            g = squares(g, a["sb_w_out_2"][0], 0, 2)
            g = ffn(g, a["ffn_w_up_2"][1], a["ffn_w_down_2"][1])
            assert g == N_SLOTS
            out2 = out[0].rearrange("(t p) d -> p t d", p=P)
            for t in range(TT):
                sp.wait_ge(turned_read, 2 * t + 3)
                sp.dma_start(out2[:, t, :], o_tok[:, t, :]).then_inc(stored, 16)
            sp.wait_ge(stored, 16 * TT)

        @block.gpsimd
        def _(pool):
            order = Chain(pool, pool_order)
            order.mark(nc.gpsimd.memset(ident[:], 0.0))
            order.mark(nc.gpsimd.memset(eps[:], EPS))
            order.mark(nc.gpsimd.memset(zero[:], 0.0))
            order(nc.gpsimd.memset(mean[:], 1.0 / D))
            order(nc.gpsimd.affine_select(out=ident[:], in_=ident[:], compare_op=ALU.not_equal, fill=1.0,
                                          base=0, pattern=[[-1, P]], channel_multiplier=1))
            pool.sem_inc(const_ready, 1)

            def split(j, r, first, loaded):
                pool.wait_ge(raw_loaded[r], loaded)
                if not isinstance(first, int) or first >= RING:
                    pool.wait_ge(slot_used, first - RING + 1)
                nc.gpsimd.tensor_tensor(w_hi[:, j], w_raw[:, r], zero[:].unsqueeze(1).to_broadcast([P, 2, 512]),
                                        ALU.add).then_inc(hi_written, 1)
                pool.wait_ge(hi_written, first + 1)
                nc.gpsimd.tensor_tensor(w_lo[:, j], w_raw[:, r], w_hi[:, j].bitcast(F32), ALU.subtract)\
                    .then_inc(raw_free, 1)

            def split_tok(j, r, first, loaded):
                pool.wait_ge(raw_loaded[r], loaded)
                pool.wait_ge(slot_used, first - RING + 1)
                nc.gpsimd.tensor_tensor(w_hi[:, j, :, 0:TOKW], w_raw[:, r, :, 0:TOKW],
                                        zero[:].unsqueeze(1).to_broadcast([P, 2, TOKW]),
                                        ALU.add).then_inc(hi_written, 1)
                pool.wait_ge(hi_written, first + 1)
                nc.gpsimd.tensor_tensor(w_lo[:, j, :, 0:TOKW], w_raw[:, r, :, 0:TOKW],
                                        w_hi[:, j, :, 0:TOKW].bitcast(F32), ALU.subtract).then_inc(raw_free, 1)

            for g in range(4):
                split(g % RING, g % RAW_RING, g, 64 * (g // RAW_RING + 1))
            order.mark(nc.gpsimd.iota(d_slc[:], pattern=[[1, SEQ]], base=-(SEQ - P), channel_multiplier=-1,
                                      allow_small_or_imprecise_dtypes=True))
            order.mark(nc.gpsimd.iota(d_win[:], pattern=[[1, WIN + P]], base=-WIN, channel_multiplier=-1,
                                      allow_small_or_imprecise_dtypes=True))
            order.mark(nc.gpsimd.iota(d_cmp[:], pattern=[[-P, TT], [16, 32]], base=CMPB - 1, channel_multiplier=-1,
                                      allow_small_or_imprecise_dtypes=True))
            order.mark(nc.gpsimd.memset(row_ok[:], 1.0))
            order.wait()
            order.mark(nc.gpsimd.affine_select(out=d_slc[:], in_=d_slc[:], compare_op=ALU.is_ge, fill=MASKED,
                                               base=SEQ - P, pattern=[[-1, SEQ]], channel_multiplier=1))
            order.mark(nc.gpsimd.affine_select(out=d_win[:], in_=d_win[:], compare_op=ALU.is_ge, fill=MASKED,
                                               base=WIN, pattern=[[-1, WIN + P]], channel_multiplier=1))
            order.mark(nc.gpsimd.affine_select(out=d_cmp[:], in_=d_cmp[:], compare_op=ALU.is_ge, fill=MASKED,
                                               base=-(CMPB - 1), pattern=[[P, TT], [-16, 32]],
                                               channel_multiplier=1))
            order(nc.gpsimd.affine_select(out=row_ok[:], in_=row_ok[:], compare_op=ALU.is_ge, fill=0.0,
                                          base=-(CMPB - 1), pattern=[[0, 1]], channel_multiplier=1))
            order.mark(nc.gpsimd.affine_select(out=d_win[:], in_=d_win[:], compare_op=ALU.is_ge, fill=MASKED,
                                               base=-1, pattern=[[1, WIN + P]], channel_multiplier=-1))
            order.wait()
            for e in range(2):
                order.mark(nc.gpsimd.memset(caus[64 * e:64 * e + 64, :], 1.0))
            order.wait()
            for e in range(2):
                order.mark(nc.gpsimd.affine_select(out=caus[64 * e:64 * e + 64, :], in_=caus[64 * e:64 * e + 64, :],
                                                   compare_op=ALU.is_ge, fill=0.0, base=0, pattern=[[1, CH]],
                                                   channel_multiplier=-1))
            order.wait()
            pool.sem_inc(const_ready, 1)
            for g in range(4, 16):
                split(g % RING, g % RAW_RING, g, 64 * (g // RAW_RING + 1))
            for g in range(16, FIRST_PIECED):
                split_tok(g % RING, g % RAW_RING, g, 64 * (g // RAW_RING + 1))
            base = 64 * (FIRST_PIECED // RAW_RING)
            rest = SLOT0[GIDX["sk0"]] - FIRST_PIECED
            turns = rest // RING

            def rounds(g0, turns, base):
                with pool.Fori(0, turns) as i:
                    for j in range(RING):
                        split((g0 + j) % RING, (g0 + j) % RAW_RING, i * RING + (g0 + j), i * 32 + (base + 32))
                return g0 + turns * RING, base + 32 * turns

            g, base = rounds(FIRST_PIECED, turns, base)
            order.mark(nc.gpsimd.memset(strict[:], 1.0))
            order.mark(nc.gpsimd.memset(neg_tri[:], -1.0))
            order.mark(nc.gpsimd.memset(unseen_f[:], 0.0))
            order.mark(nc.gpsimd.tensor_copy(ident_r[:], ident[:]))
            order(nc.gpsimd.memset(neg_one[:], -1.0))
            order.mark(nc.gpsimd.affine_select(out=unseen_f[:], in_=unseen_f[:], compare_op=ALU.is_gt,
                                               fill=MASKED, base=0, pattern=[[1, P]], channel_multiplier=-1))
            order.mark(nc.gpsimd.affine_select(out=strict[:], in_=strict[:], compare_op=ALU.is_gt, fill=0.0,
                                               base=0, pattern=[[1, P]], channel_multiplier=-1))
            order(nc.gpsimd.affine_select(out=neg_tri[:], in_=neg_tri[:], compare_op=ALU.is_ge, fill=0.0,
                                          base=0, pattern=[[-1, P]], channel_multiplier=1))
            order(nc.gpsimd.tensor_copy(unseen[:], unseen_f[:]))
            pool.sem_inc(const_ready, 1)
            left = N_SLOTS - g
            g, base = rounds(g, left // RING, base)
            for n in range(N_SLOTS - g):
                split(g % RING, g % RAW_RING, g, base + 32)
                g += 1
            assert g == N_SLOTS

        @block.tensor
        def _(pe):
            def mm(o, l, r, start, stop):
                return nc.tensor.matmul(o, l, r, start=start, stop=stop, skip_group_check=True)

            def three(o, w, xx, start, stop):
                mm(o, w[0], xx[0], start, False)
                mm(o, w[0], xx[1], False, False)
                return mm(o, w[1], xx[0], False, stop)

            def bank_free(n):
                if n >= 2:
                    pe.wait_ge(set_free[n % 2], 4 * (n // 2))

            def evacuated(n):
                pe.wait_ge(set_free[n % 2], 4 * (n // 2 + 1))

            def by_feature(n, act_hi, act_lo, width=SEQ, ready=None, k0=0, i4=0, hook=None, adds=False):
                g0, slots = SLOT0[n], GROUPS[n][1]
                for sl in range(slots):
                    g = g0 + sl
                    pe.wait_ge(raw_free, i4 + (g + 1))
                    for kk in range(2):
                        k = k0 + 2 * sl + kk
                        if ready is not None:
                            pe.wait_ge(split_ready, ready + 2 * sl + kk + 1)
                        for j in range(4):
                            last_mm = three(ps[:, 4 * (n % 2) + j, 0:width],
                                            [w[:, g % RING, kk, P * j:P * j + P] for w in (w_hi, w_lo)],
                                            [t[:, k, 0:width] for t in (act_hi, act_lo)],
                                            sl + kk == 0, sl == slots - 1 and kk == 1)
                            if adds and sl == slots - 1 and kk == 1 and j < 3:
                                last_mm.then_inc(bank_done, 1)
                    last_mm.then_inc(slot_used, 1)
                    if hook and sl in hook:
                        hook[sl]()

            def by_token(n, act_hi, act_lo, tiles=TT, width=512):
                g0 = SLOT0[n]
                for sl in range(GROUPS[n][1]):
                    g = g0 + sl
                    pe.wait_ge(raw_free, g + 1)
                    for kk in range(2):
                        k = 2 * sl + kk
                        for j in range(tiles):
                            last_mm = three(ps[:, 4 * (n % 2) + j, 0:width],
                                            [t[:, k, P * j:P * j + P] for t in (act_hi, act_lo)],
                                            [w[:, g % RING, kk, 0:width] for w in (w_hi, w_lo)],
                                            k == 0, k == KT - 1)
                    last_mm.then_inc(slot_used, 1)


            def norm_part(name, k, width=SEQ, buffer=0):
                pe.wait_ge(sq_ready, 8 * NORM_AT[name] + k + 1)
                mm(ps[:, NORM_BANK[name], 0:width], mean[:], sq[:, (k + buffer) % 2, 0:width], k == 0, k == KT - 1)\
                    .then_inc(sq_used, 1)

            def norm_sum(name, width=SEQ):
                for k in range(KT):
                    norm_part(name, k, width)

            def weighted_part(k):
                pe.wait_ge(weighted_ready, k + 1)
                mm(ps[:, NORM_BANK["retn"], :], mean[:], full[:, k % 2, :], k == 0, k == KT - 1)\
                    .then_inc(weighted_used, 1)

            def last_half(n, act_hi, act_lo, name, ready=None):
                def first_tiles():
                    evacuated(n - 1)
                    pe.wait_ge(sq_added, 3 * ADDED.index(name) + 3)
                    mm(ps[:, NORM_BANK[name], :], mean[:], sq[:, 0, :], True, False).then_inc(sq_used, 4)
                    if name == "fin1":
                        for k in range(4):
                            weighted_part(k)

                assert NORM_BANK[name] // 4 == (n - 1) % 2, name
                by_feature(n, act_hi, act_lo, ready=ready, hook={(GROUPS[n][1] - 1) // 2: first_tiles}, adds=True)
                for k in range(4, KT):
                    norm_part(name, k, buffer=1)
                if name == "fin1":
                    for k in range(4, KT):
                        weighted_part(k)
                norm_read(name)
                evacuated(n)

            def norm_read(name):
                pe.wait_ge(root_ready, ROOT_AT[name] + 1)

            pe.wait_ge(const_ready, 1)
            pe.wait_ge(in_loaded, 16 * TT)
            for k in range(KT):
                b = 2 + k % 4
                if k >= 4:
                    pe.wait_ge(x_ready, k - 3)
                for t in range(TT):
                    last = nc.tensor.transpose(ps[:, b, P * t:P * t + P], x_tok[:, t, P * k:P * k + P], ident[:])
                last.then_inc(turned, 1)
                if k >= 2:
                    norm_part("mix", k - 2)
            norm_part("mix", KT - 2)
            norm_part("mix", KT - 1)
            pe.wait_ge(rows_loaded, 16 * N_GAIN_LOADS)
            nc.tensor.transpose(ps[:, 0, 0:GAIN_ROWS], gain_rows[0:GAIN_ROWS, :], ident[0:GAIN_ROWS, 0:GAIN_ROWS])\
                .then_inc(turned, 1)
            pe.wait_ge(turned_read, 1)
            norm_read("mix")

            G = GIDX
            h_ = (h_hi, h_lo)
            by_feature(G["q"], *h_, ready=SPLITS["mix"])
            by_feature(G["kv"], *h_)
            bank_free(G["qkb"])
            pe.wait_ge(cw_loaded, 16 * 4)
            for kv in range(2):
                nc.tensor.transpose(ps[:, 0, CMPB * kv:CMPB * kv + CMPB], pos[0:CMPB, kv, :],
                                    ident[0:CMPB, 0:CMPB]).then_inc(cmp_pe, 1)
            pe.wait_ge(cmp_b, 1)
            by_feature(G["qkb"], *h_)

            bank_free(G["vb"])
            pe.wait_ge(cw1_loaded, 32)
            pe.wait_ge(cmp_blk, 2)
            for kv in range(2):
                for c in range(CMPB // 2):
                    last = mm(ps[:, 4 + kv, 0:KVH * NCMP], w1c[:, kv, c, :],
                              blk[:, kv, c].rearrange("p h n -> p (h n)"), c == 0, c == CMPB // 2 - 1)
                last.then_inc(cmp_pe, 1)
            pe.wait_ge(cmp_a, 2)
            by_token(G["vb"], *h_)
            bank_free(G["tok"])
            pe.wait_ge(cw2_loaded, 48)
            for h in range(KVH):
                mm(ps[:, h, 0:NCMP], w2k[:], hid[:, 0, h, 0:NCMP], True, True)
                last = mm(ps[0:NCMP, 2 + h, 0:HD], hid[:, 1, h, 0:NCMP], w2v[:], True, True)
            last.then_inc(cmp_pe, 1)
            pe.wait_ge(cmp_b, 2)
            by_token(G["tok"], *h_, width=TOKW)
            evacuated(G["vb"])
            evacuated(G["tok"])

            def nsa_scores(it):
                qt, h = NSA[it]
                r = slice(HD * (h // GRP), HD * (h // GRP) + HD)
                q = qT[r, h % GRP, P * qt:P * qt + P]
                b = 2 * (it % 2)
                if it >= 2:
                    pe.wait_ge(att_m, it - 1)
                mm(ps[:, b, 0:P * (qt + 1)], q, kvT[r, 2, 0:P * (qt + 1)], True, True)
                w0 = P * max(0, qt - 2)
                mm(ps[:, b + 1, 0:P * (qt + 1) - w0], q, kvT[r, 3, w0:P * (qt + 1)], True, True)
                mm(ps[:, b + 1, 384:384 + NCMP], q, kcT[r, 0:NCMP], True, True).then_inc(att_s, 1)

            def nsa_blocks(qt):
                return ([(P * t, P, tok[:, t, 0:P]) for t in range(qt + 1)]
                        + [(512 + P * n, P, tok[:, t, P:2 * P])
                           for n, t in enumerate(range(max(0, qt - 2), qt + 1))]
                        + [(896, NCMP, None)])

            def nsa_turn(it):
                qt, h = NSA[it]
                pe.wait_ge(att_p, it + 1)
                if it >= 1:
                    pe.wait_ge(att_c, it)
                for n, (col, rows, _) in enumerate(nsa_blocks(qt)):
                    last = nc.tensor.transpose(ps[0:rows, 4 + n // 4, P * (n % 4):P * (n % 4) + P],
                                               s_buf[:, it % NSA_DEEP, col:col + rows], ident[:])
                last.then_inc(att_t, 1)

            def nsa_out(it):
                qt, h = NSA[it]
                pe.wait_ge(att_c, it + 1)
                pr = it // 2
                if pr >= 2:
                    pe.wait_ge(att_r, pr - 1)
                kvh = h // GRP
                o = ps[HD * (h % 2):HD * (h % 2) + HD, 6 + pr % 2, 0:P]
                blocks = nsa_blocks(qt)
                for n, (_, rows, v) in enumerate(blocks):
                    v = vc[0:NCMP, kvh, :] if v is None else v[:, HD * kvh:HD * kvh + HD]
                    last = mm(o, v, pT_buf[0:rows, it % 2, n, :], n == 0, n == len(blocks) - 1)
                last.then_inc(att_o, 1)

            for it in range(len(NSA) + 4):
                if it < len(NSA):
                    nsa_scores(it)
                if it >= 4:
                    nsa_out(it - 4)
                if 3 <= it < len(NSA) + 3:
                    nsa_turn(it - 3)
            pe.wait_ge(att_r, 16)
            for t in range(TT):
                last = nc.tensor.transpose(ps[0:16, 0, P * t:P * t + P], tok[:, t, TOKW - 16:TOKW], ident[:])
            last.then_inc(gla_pe, 1)
            pe.wait_ge(gla_al, 1)
            pe.wait_ge(wal_loaded, 16)
            for pr in range(2):
                mm(ps[:, 1 + pr, :], wal[:, P * pr:P * pr + P], alT[:], True, True).then_inc(gla_pe, 1)

            def turn_keys(pr):
                pe.wait_ge(gla_ks, pr + 1)
                for t in range(TT):
                    last = nc.tensor.transpose(ps[:, pr, P * t:P * t + P], ks_t[:, P * t:P * t + P], ident[:])
                last.then_inc(gla_pe, 1)

            by_feature(G["rb"], *h_, hook={1: lambda: turn_keys(0)})
            turn_keys(1)

            def gla_scores(head):
                r = slice(CH * (head % 2), CH * (head % 2) + CH)
                for t in range(TT):
                    for q in range(2):
                        s = slice(P * t + CH * q, P * t + CH * q + CH)
                        last = mm(ps[CH * q:CH * q + CH, 2 + head % 2, s], qkb[r, 2 + head // 2, s],
                                  qkb[r, head // 2, s], True, True)
                last.then_inc(gla_sc, 1)

            def gla_out(head):
                pr, r = head // 2, slice(CH * (head % 2), CH * (head % 2) + CH)
                pe.wait_ge(gla_at, head + 1)
                pe.wait_ge(gla_st, pr + 1)
                o = gla_bank(head)
                for t in range(TT):
                    mm(o[:, P * t:P * t + P], vb[:, t, P * head:P * head + P], attT[:, head % 2, t, :], True, False)
                    for c in (2 * t, 2 * t + 1):
                        if c:
                            last = mm(o[:, CH * c:CH * c + CH], states[r, pr, c, :],
                                      qkb[r, pr, CH * c:CH * c + CH], False, True)
                last.then_inc(gla_o, 1)

            def gla_mean(head):
                pe.wait_ge(gla_sq, head + 1)
                if head >= 2:
                    pe.wait_ge(gla_rd, head - 1)
                mm(gla_mean_bank(head), mean[:], sq[:, head % 2, :], True, True).then_inc(gla_sum, 1)

            pe.wait_ge(gla_qk, 2)
            gla_scores(0)
            gla_scores(1)
            evacuated(G["rb"])
            for pr in range(2):
                pe.wait_ge(gla_kt, pr + 1)
                for c in range(NCH - 1):
                    r = slice(CH * (c % 2), CH * (c % 2) + CH)
                    for e in range(2):
                        last = mm(inc_at(pr, c, e), ks_tok[r, pr, c // 2, CH * e:CH * e + CH],
                                  vb[r, c // 2, P * (2 * pr + e):P * (2 * pr + e) + P], True, True)
                last.then_inc(gla_pe, 1)
            for head in range(GH):
                gla_out(head)
                if head + 2 < GH:
                    gla_scores(head + 2)
                if head:
                    gla_mean(head - 1)

            for h in range(2):
                bank_free(G[f"mn{h}"])
                if h == 0:
                    pe.wait_ge(root_ready, ROOT_AT["gla1"] + 1)
                by_feature(G[f"mn{h}"], *h_, hook={0: lambda: gla_mean(GH - 1)} if h == 0 else None)
                bank_free(G[f"mg{h}"])
                if h == 0:
                    pe.wait_ge(gla_rd, GH)
                by_feature(G[f"mg{h}"], *h_)
                pe.wait_ge(split_ready, SPLITS["gla"] + 4)
                pe.wait_ge(att_r, 16)
                bank_free(G[f"bn{h}"])
                by_feature(G[f"bn{h}"], o_hi, o_lo)
                bank_free(G[f"bg{h}"])
                by_feature(G[f"bg{h}"], o_hi, o_lo, k0=4)
            bank_free(G["out0"])
            by_feature(G["out0"], mx_hi, mx_lo, ready=SPLITS["mx"], adds=True)
            bank_free(G["out1"])
            pe.wait_ge(mem_loaded, 16)
            for k in range(KT):
                if k >= 4:
                    pe.wait_ge(mem_turned_read, k - 3)
                for t in range(MEM // P):
                    last = nc.tensor.transpose(ps[:, 4 + k % 4, P * t:P * t + P], mem_tok[:, t, P * k:P * k + P],
                                               ident[:])
                last.then_inc(turned, 1)
            pe.wait_ge(mem_turned_read, 8)

            def memory_squares():
                evacuated(G["out0"])
                norm_sum("mem", MEM)

            by_feature(G["out1"], mx_hi, mx_lo, hook={0: memory_squares}, adds=True)

            norm_read("mem")
            by_feature(G["xk"], m_hi, m_lo, width=MEM, ready=SPLITS["mem"])
            evacuated(G["out1"])
            norm_sum("xn")
            by_token(G["xv"], m_hi, m_lo, tiles=MEM // P)
            norm_read("xn")
            bank_free(G["xq"])
            by_feature(G["xq"], *h_, ready=SPLITS["xn"])
            evacuated(G["xk"])
            evacuated(G["xv"])
            evacuated(G["xq"])

            def x_scores(it):
                h, qt = it // TT, it % TT
                if it >= 2:
                    pe.wait_ge(xat_e, it - 1)
                mm(ps[:, it % 2, 0:MEM], xqT[:, h, P * qt:P * qt + P], xkT[:, h, :], True, True)\
                    .then_inc(xat_s, 1)

            def x_turn(it):
                pe.wait_ge(xat_p, it + 1)
                if it >= 2:
                    pe.wait_ge(xat_c, it - 1)
                for t in range(MEM // P):
                    last = nc.tensor.transpose(ps[:, 2 + it % 2, P * t:P * t + P], xp[:, it % 3, P * t:P * t + P],
                                               ident[:])
                last.then_inc(xat_t, 1)

            def x_out(it):
                h, qt = it // TT, it % TT
                pe.wait_ge(xat_c, it + 1)
                if h >= 2 and qt == 0:
                    pe.wait_ge(xat_r, h - 1)
                for t in range(MEM // P):
                    last = mm(ps[:, 4 + h % 2, P * qt:P * qt + P], xv[:, t, P * h:P * h + P], xpT[:, it % 2, t, :],
                              t == 0, t == 1)
                last.then_inc(xat_o, 1)

            for it in range(XH * TT + 3):
                if it < XH * TT:
                    x_scores(it)
                if it >= 3:
                    x_out(it - 3)
                if 2 <= it < XH * TT + 2:
                    x_turn(it - 2)
            pe.wait_ge(conv_loaded, 16 * N_CONV_LOADS)
            for r in range(5):
                last = nc.tensor.transpose(ps[:, r // 4, 4 * FT * (r % 4):4 * FT * (r % 4 + 1)],
                                           conv_rows[0:4 * FT, r, :], ident[0:4 * FT, 0:4 * FT])
            last.then_inc(conv_turned, 1)
            pe.wait_ge(xat_r, XH)
            by_feature(G["xo0"], xo_hi, xo_lo, adds=True)
            bank_free(G["xo1"])
            pe.wait_ge(conv_read, 1)
            last_half(G["xo1"], xo_hi, xo_lo, "ffn1n")

            def ffn(tag, name, then):
                n0 = G[f"up{tag}_0"]
                by_feature(n0, *h_, ready=SPLITS[name])
                with pe.Fori(0, 5) as i:
                    for e in range(2):
                        n = n0 + 1 + e
                        pe.wait_ge(set_free[n % 2], i * 4 + 4 * (n // 2))
                        by_feature(n, *h_, i4=i * 8)
                bank_free(G[f"down{tag}_0"])
                by_feature(G[f"down{tag}_0"], f_hi, f_lo, ready=SPLITS[f"ffn{tag}"], adds=True)
                bank_free(G[f"down{tag}_1"])
                last_half(G[f"down{tag}_1"], f_hi, f_lo, then)

            ffn(1, "ffn1n", "fin1")

            norm_read("retn")
            for h in range(RH):
                nq, nv, ng = G[f"rqk{h}"], G[f"rv{h}"], G[f"rg{h}"]
                sa, sc = 4 * (nq % 2), 4 * (nv % 2)
                bank_free(nq)
                if h:
                    pe.wait_ge(root_ready, ROOT_AT[f"ret{h}"])
                by_feature(nq, *h_, ready=SPLITS["retn"] if h == 0 else None)
                bank_free(nv)
                by_token(nv, *h_)
                evacuated(nq)
                for j in range(TT):
                    for kk in range(2):
                        last = mm(ps[:, sa + j, 0:SEQ - P * j], rq[:, 2 + kk, P * j:P * j + P],
                                  rq[:, kk, P * j:SEQ], kk == 0, kk == 1)
                    last.then_inc(ret_s, 1)
                evacuated(nv)
                pe.wait_ge(ret_sc, TT * (h + 1))
                for e in range(4):
                    for j in range(TT):
                        last = mm(ps[:, sc + e, P * j:SEQ], rv[:, j, P * e:P * e + P], rsc[:, j, 0:SEQ - P * j],
                                  j == 0, j == TT - 1)
                    last.then_inc(ret_o, 1)

                def mean_squares():
                    pe.wait_ge(ret_cp, 4 * (h + 1))
                    for e in range(4):
                        pe.wait_ge(ret_q, 4 * h + e + 1)
                        mm(ps[:, sc, :], mean[:], sq[:, e % 2, :], e == 0, e == 3).then_inc(ret_m, 1)

                by_feature(ng, *h_, hook={1: mean_squares})
            bank_free(G["ro0"])
            pe.wait_ge(root_ready, ROOT_AT["ret3"] + 1)
            by_feature(G["ro0"], y_hi, y_lo, ready=SPLITS["ret"], adds=True)
            bank_free(G["ro1"])
            last_half(G["ro1"], y_hi, y_lo, "ffn2n")
            ffn(2, "ffn2n", "sbn")

            pe.wait_ge(const_ready, 3)
            for half in range(2):
                if half:
                    pe.wait_ge(sb_r, 4)
                for name in ("sq", "sk"):
                    n = G[f"{name}{half}"]
                    bank_free(n)
                    by_feature(n, *h_, ready=SPLITS["sbn"] if (name, half) == ("sq", 0) else None)
                n = G[f"sv{half}"]
                bank_free(n)
                by_token(n, *h_)
                for name in ("sq", "sk", "sv"):
                    evacuated(G[f"{name}{half}"])

                def z(it):
                    g = len(SB) * half + it
                    pair, j, e = SB[it]
                    r = slice(SH_D * e, SH_D * e + SH_D)
                    if it >= len(SB_BANK):
                        pe.wait_ge(st_ex, g - len(SB_BANK) + 1)
                    mm(sb_bank(it)[:, 0:SEQ - P * j], skT[r, pair, P * j:P * j + P], sqT[r, pair, P * j:SEQ],
                       True, True).then_inc(st_z, 1)

                def weights(it):
                    g = len(SB) * half + it
                    pair, j, e = SB[it]
                    pe.wait_ge(st_sp, g + 1)
                    o = sb_bank(it)
                    mm(o[:, 0:SEQ - P * j], neg_tri[:], s_sp[:, it % 4, 0:SEQ - P * j], False, False)
                    last = mm(o[:, 0:P], ident_r[:], unseen[:], False, j == TT - 1)
                    if j < TT - 1:
                        pe.wait_ge(st_up, updates(half, it - 2))
                        last = mm(o[:, P:SEQ - P * j], neg_one[:], s_sum[:, e, P * (j + 1):SEQ], False, True)
                    last.then_inc(st_acc, 1)

                def pv(it):
                    g = len(SB) * half + it
                    pair, j, e = SB[it]
                    pe.wait_ge(st_ex, g + 1)
                    if pair >= 2 and j == TT - 1 and e == 0:
                        pe.wait_ge(sb_r, 4 * half + pair - 1)
                    head = 2 * pair + e
                    mm(ps[SH_D * e:SH_D * e + SH_D, 4 + pair % 2, P * j:SEQ], sv[:, j, SH_D * head:SH_D * head + SH_D],
                       s_a[:, it % 4, 0:SEQ - P * j], j == TT - 1, j == 0).then_inc(st_o, 1)

                for it in range(0, len(SB) + 4, 2):
                    for stage, u in ((z, it), (weights, it - 2), (pv, it - 4)):
                        if 0 <= u < len(SB):
                            stage(u)
                            stage(u + 1)
            pe.wait_ge(sb_r, 8)
            by_feature(G["so0"], so_hi, so_lo, adds=True)
            last_half(G["so1"], so_hi, so_lo, "ffn3n")
            ffn(3, "ffn3n", "fin")
            for t in range(TT):
                for b in range(2):
                    u = 2 * t + b
                    if u >= 4:
                        pe.wait_ge(turned_read, u - 2)
                    for k in range(4):
                        if t == 0:
                            pe.wait_ge(fin_ready, 4 * b + k + 1)
                        last = nc.tensor.transpose(ps[:, u % 4, P * k:P * k + P],
                                                   x[:, 4 * b + k, P * t:P * t + P], ident[:])
                    last.then_inc(turned, 1)

        @block.scalar
        def _(act):
            G = GIDX

            def group_done(n):
                act.wait_ge(slot_used, SLOT0[n + 1])

            gains = (a["ln_mix_g"][0], a["ln_mem_g"][0], a["ln_x_g"][0], a["ln_ffn_g"][0], a["ln_final_g"],
                     a["ret_norm_2"][0], a["ffn_norm_2"][0], a["sb_norm_2"][0], a["ffn_norm_2"][1],
                     a["final_norm_2"])
            loads = [(gain_rows[8 * i:8 * i + 8, :], src.rearrange("(k p) -> k p", p=P))
                     for i, src in enumerate(gains)]
            loads += [(gain_rows[80:82, :], a["gla_b_alpha"][0].rearrange("(k p) -> k p", p=P)),
                      (gain_rows[82:83, :], a["gla_norm_g"][0:1, :])]
            assert len(loads) == N_GAIN_LOADS
            for dst, src in loads:
                act.dma_start(dst, src).then_inc(rows_loaded, 16)
            act.dma_start(gate_b[:], a["nsa_gate_b"][0].partition_broadcast(P)).then_inc(gate_loaded, 16)

            def squares(name, src=x, width=SEQ, ready=x_ready, tiles=range(KT)):
                g0 = 8 * NORM_AT[name]
                act.preload_act_table_set("natural_log_exp_and_others")
                added = name in ADDED
                for k in tiles:
                    g = g0 + k
                    b = (k + 1) % 2 if added and k >= 4 else min(k, 1) if added else k % 2
                    act.wait_ge(ready, X_AT.get(name, 0) + k + 1)
                    if added and k < 2:
                        act.wait_ge(sq_used, g0)
                    elif added and k <= 4:
                        act.wait_ge(sq_added, 3 * ADDED.index(name) + k - 1)
                    elif g >= 2:
                        act.wait_ge(sq_used, g - 1)
                    nc.scalar.activation(sq[:, b, 0:width], src[:, k, 0:width], ACT.Square).then_inc(sq_ready, 1)

            def inverse_root(name, src, scale=1.0, width=SEQ, dst=rstd[:]):
                nc.scalar.activation(dst[:, 0:width], src[:, 0:width], ACT.Ln, bias=eps[:, 0:1], scale=scale)\
                    .then_inc(root_ready, 1)
                act.wait_ge(root_ready, ROOT_AT[name] + 1)
                nc.scalar.activation(dst[:, 0:width], dst[:, 0:width], ACT.Exp, scale=-0.5)\
                    .then_inc(rstd_ready, 1)

            def norm_root(name, width=SEQ):
                act.wait_ge(sq_used, 8 * NORM_AT[name] + 8)
                inverse_root(name, ps[:, NORM_BANK[name], :], 1.0, width)

            def high(s, dst, width=SEQ):
                act.wait_ge(full_ready, s + 1)
                nc.scalar.activation(dst, full[:, s % 2, 0:width], ACT.Copy).then_inc(full_hi, 1)

            def highs(name, dst, width=SEQ, n=KT):
                for k in range(n):
                    high(SPLITS[name] + k, dst[:, k, 0:width], width)

            squares("mix")
            norm_root("mix")
            highs("mix", h_hi)
            act.wait_ge(turned, KT + 1)
            for kv, name in enumerate(("cmp_pos_k", "cmp_pos_v")):
                for h in range(KVH):
                    act.dma_start(pos[:, kv, HD * h:HD * h + HD], a[name][0]).then_inc(cw_loaded, 16)

            for kv, name in enumerate(("cmp_w1_k", "cmp_w1_v")):
                act.dma_start(w1c[:, kv], a[name][0].rearrange("(c p) n -> p c n", p=P)).then_inc(cw1_loaded, 16)
            for h in range(KVH):
                act.dma_start(w2k[:, HD * h:HD * h + HD], a["cmp_w2_k"][0]).then_inc(cw2_loaded, 16)
            act.dma_start(w2v[:], a["cmp_w2_v"][0]).then_inc(cw2_loaded, 16)
            group_done(G["q"])
            for j in range(4):
                nc.scalar.activation(qT[:, j, :], bank(G["q"], j), ACT.Copy, scale=HD ** -0.5)\
                    .then_inc(set_free[G["q"] % 2], 1)
            group_done(G["qkb"])
            for j in range(4):
                nc.scalar.activation(qkb[:, j, :], bank(G["qkb"], j), ACT.Copy, scale=CH ** -0.5 if j < 2 else 1.0)\
                    .then_inc(set_free[G["qkb"] % 2], 1)
            for kv in range(2):
                act.wait_ge(cmp_pe, 3 + kv)
                nc.scalar.activation(hid[:, kv, :, 0:NCMP],
                                     ps[:, 4 + kv, 0:KVH * NCMP].rearrange("p (h n) -> p h n", h=KVH),
                                     ACT.Gelu_apprx_tanh).then_inc(cmp_a, 1)
            act.wait_ge(gate_a, 1)
            nc.scalar.activation(gates[:], gates[:], ACT.Sigmoid).then_inc(gate_s, 1)

            def nsa_parts(qt):
                return ((896, NCMP), (0, P * (qt + 1)), (512, P * min(3, qt + 1)))

            def nsa_exp(it):
                qt, b = NSA[it][0], it % NSA_DEEP
                act.wait_ge(att_n, it + 1)
                for n, (c, w) in enumerate(nsa_parts(qt)):
                    last = nc.scalar.activation(s_buf[:, b, c:c + w], s_buf[:, b, c:c + w], ACT.Exp,
                                                bias=att_st[:, b, n:n + 1], accum_out=att_st[:, b, 3 + n:4 + n])
                last.then_inc(att_e, 1)

            def nsa_copy(it):
                qt, b = NSA[it][0], it % 2
                nb = qt + 1 + min(3, qt + 1)
                act.wait_ge(att_t, it + 1)
                if it >= 2:
                    act.wait_ge(att_o, it - 1)
                src = ps[:, 4:6, :].rearrange("p a (b c) -> p (a b) c", c=P)
                nc.scalar.activation(pT_buf[:, b, 0:nb, :], src[:, 0:nb, :], ACT.Copy)
                nc.scalar.activation(pT_buf[0:NCMP, b, nb, :], src[0:NCMP, nb, :], ACT.Copy).then_inc(att_c, 1)

            for it in range(len(NSA) + 6):
                if 3 <= it < len(NSA) + 3:
                    nsa_copy(it - 3)
                if it >= 6 and it % 2 == 0:
                    pr = (it - 6) // 2
                    qt, i = NSA[2 * pr][0], pr % GRP
                    act.wait_ge(att_o, 2 * pr + 2)
                    nc.scalar.activation(o_hi[:, i, P * qt:P * qt + P], ps[:, 6 + pr % 2, 0:P], ACT.Copy)\
                        .then_inc(att_h, 1)
                if it < len(NSA):
                    nsa_exp(it)

            act.preload_act_table_set("natural_log_exp_and_others")
            act.wait_ge(gla_pe, 1)
            act.dma_start(wal[:], a["gla_w_alpha2"][0]).then_inc(wal_loaded, 16)
            nc.scalar.activation(alT[:], ps[0:16, 0, :], ACT.Copy).then_inc(gla_al, 1)
            for pr in range(2):
                x0 = 6 * pr
                act.wait_ge(gla_v, 3 * pr + 1)
                nc.scalar.activation(ebuf[:], ebuf[:], ACT.Exp, scale=-1.0).then_inc(gla_x, 1)
                act.wait_ge(gla_x, x0 + 1)
                nc.scalar.activation(ebuf[:], ebuf[:], ACT.Ln, bias=1.0).then_inc(gla_x, 1)
                act.wait_ge(gla_v, 3 * pr + 3)
                if pr:
                    act.wait_ge(gla_pe, 4)
                nc.scalar.activation(ks_t[:], la[:], ACT.Exp, scale=1.0 / 16).then_inc(gla_x, 1)
                nc.scalar.activation(ek[:], bcum[:], ACT.Exp, scale=-1.0 / 16).then_inc(gla_x, 1)
                nc.scalar.activation(ebuf[:], bcum[:], ACT.Exp, scale=1.0 / 16).then_inc(gla_x, 1)
                nc.scalar.activation(dec[:, pr, :], bcum[:].rearrange("p (c i) -> p c i", i=CH)[:, :, CH - 1],
                                     ACT.Exp, scale=1.0 / 16).then_inc(gla_x, 1)
            for pr in range(2):
                act.wait_ge(gla_pe, 4 + pr)
                nc.scalar.activation(ks_tok[:, pr].rearrange("p t f -> p (t f)"), ps[:, pr, :], ACT.Copy)\
                    .then_inc(gla_kt, 1)
            group_done(G["rb"])
            for j in range(4):
                nc.scalar.activation(rT[:, j, :], bank(G["rb"], j), ACT.Silu).then_inc(set_free[G["rb"] % 2], 1)
            act.preload_act_table_set("natural_log_exp_and_others")
            for head in range(GH):
                act.wait_ge(gla_o, head + 1)
                if head >= 2:
                    act.wait_ge(gla_sum, head - 1)
                nc.scalar.activation(sq[:, head % 2, :], gla_bank(head), ACT.Square).then_inc(gla_sq, 1)
                act.wait_ge(gla_sum, head + 1)
                if head:
                    act.wait_ge(gla_rd, head)
                inverse_root(f"gla{head}", gla_mean_bank(head), float(D) / P)
                high(SPLITS["gla"] + head, o_hi[:, 4 + head, :])

            for h in range(2):
                for name, dst, s in ((f"mn{h}", gN, sig_n), (f"mg{h}", gG, sig_g)):
                    n = G[name]
                    group_done(n)
                    if h:
                        act.wait_ge(full_ready, SPLITS["mx"] + 4)
                    for j in range(4):
                        nc.scalar.activation(dst[:, j, :], bank(n, j), ACT.Sigmoid).then_inc(set_free[n % 2], 1)
                for j in range(4):
                    high(SPLITS["mx"] + 4 * h + j, mx_hi[:, 4 * h + j, :])
            act.wait_ge(slot_used, SLOT0[G["bg1"] + 1])
            act.dma_start(mem_tok[:], a["mem"][0].rearrange("(t p) d -> p t d", p=P)).then_inc(mem_loaded, 16)

            squares("mem", memT, MEM, mem_turned_read)
            norm_root("mem", MEM)
            highs("mem", m_hi, MEM)
            squares("xn")
            group_done(G["xk"])
            for j in range(4):
                nc.scalar.activation(xkT[:, j, :], ps[:, 4 * (G["xk"] % 2) + j, 0:MEM], ACT.Copy)\
                    .then_inc(set_free[G["xk"] % 2], 1)
            norm_root("xn")
            highs("xn", h_hi)
            group_done(G["xq"])
            for j in range(4):
                nc.scalar.activation(xqT[:, j, :], bank(G["xq"], j), ACT.Copy, scale=P ** -0.5)\
                    .then_inc(set_free[G["xq"] % 2], 1)
            for it in range(XH * TT + 3):
                if 2 <= it < XH * TT + 2:
                    u = it - 2
                    act.wait_ge(xat_t, u + 1)
                    if u >= 2:
                        act.wait_ge(xat_o, u - 1)
                    nc.scalar.activation(xpT[:, u % 2].rearrange("p t q -> p (t q)"), ps[:, 2 + u % 2, 0:MEM],
                                         ACT.Copy).then_inc(xat_c, 1)
                if it >= 6 and it % TT == 2:
                    h = it // TT - 1
                    act.wait_ge(xat_o, TT * (h + 1))
                    nc.scalar.activation(xo_hi[:, h, :], ps[:, 4 + h % 2, :], ACT.Copy).then_inc(xat_h, 1)
                if it < XH * TT:
                    act.wait_ge(xat_m, it + 1)
                    if it >= 3:
                        act.wait_ge(xat_t, it - 2)
                    nc.scalar.activation(xp[:, it % 3, :], ps[:, it % 2, 0:MEM], ACT.Exp, bias=x_st[:, it % 3, 0:1],
                                         accum_out=x_st[:, it % 3, 1:2]).then_inc(xat_e, 1)

            def ffn(tag, name, func, two):
                squares(name)
                norm_root(name)
                highs(name, h_hi)
                n0 = G[f"up{tag}_0"]
                row = {1: 1, 2: 2, 3: 4}[tag]

                def group(n, c0, g, t, s):
                    act.wait_ge(slot_used, SLOT0[n + 1] + g)
                    for half in range(1 + two):
                        for e in range(2):
                            col = t + e
                            act.wait_ge(full_ready, s + e - 1)
                            nc.scalar.activation((cv if half else cu)[:, e, :],
                                                 ps[:, 4 * (n % 2) + 2 * half + e, :], ACT.Identity,
                                                 bias=vec(row + half, col + 3 * FT),
                                                 scale=vec(row + half, col + 2 * FT)).then_inc(conv_a, 1)
                    for e in range(2):
                        act.wait_ge(conv_d, c0 + e + 1)
                        nc.scalar.activation(cu[:, e, :], cu[:, e, :], func).then_inc(nonlin, 1)
                    for e in range(2):
                        act.wait_ge(full_ready, s + e + 1)
                        nc.scalar.activation(f_tile(f_hi, t + e), full[:, (s0 + e) % 2, :], ACT.Copy)\
                            .then_inc(full_hi, 1)

                s0 = SPLITS[f"ffn{tag}"]
                per = 4 if two else 2
                cd = CONV0[tag]
                group(n0, cd, 0, 0, s0)
                with act.Fori(0, 5) as i:
                    for e in range(2):
                        group(n0 + 1 + e, i * (2 * per) + (cd + per * (1 + e)), i * 8, i * 4 + 2 * (1 + e),
                              i * 4 + (s0 + 2 * (1 + e)))

            ffn(1, "ffn1n", ACT.Gelu_apprx_tanh, False)

            for half in range(2):
                tiles = range(4 * half, 4 * half + 4)
                squares("fin1", tiles=tiles)
                for k in tiles:
                    if k >= 2:
                        act.wait_ge(weighted_used, k - 1)
                    nc.scalar.activation(full[:, k % 2, :], x[:, k, :], ACT.Square, scale=gain(GAIN_OF["fin1"], k))\
                        .then_inc(weighted_ready, 1)
            norm_root("fin1")
            act.wait_ge(weighted_mean, 1)
            inverse_root("retn", sq[:, 0, :], dst=sq[:, 1, :])
            highs("retn", h_hi)
            act.wait_ge(slot_used, SLOT0[G["rqk0"]])
            act.dma_start(cosT[:], a["rope_cos"]).then_inc(rope_loaded, 16)
            act.dma_start(sinT[:], a["rope_sin"]).then_inc(rope_loaded, 16)
            act.dma_start(dmat[:], a["ret_decay"][0]).then_inc(dmat_loaded, 16)
            for h in range(RH):
                nv, ng = G[f"rv{h}"], G[f"rg{h}"]
                group_done(nv)
                if h:
                    act.wait_ge(ret_o, 4 * h)
                for t in range(TT):
                    nc.scalar.activation(rv[:, t, :], bank(nv, t), ACT.Copy).then_inc(set_free[nv % 2], 1)
                act.wait_ge(ret_o, 4 * h + 4)
                if h < RH - 1:
                    act.wait_ge(ret_sc, TT * (h + 1))
                    act.dma_start(dmat[:], a["ret_decay"][h + 1]).then_inc(dmat_loaded, 16)
                act.preload_act_table_set("natural_log_exp_and_others")
                for e in range(4):
                    nc.scalar.activation(ro[:, e, :], bank(nv, e), ACT.Copy).then_inc(ret_cp, 1)
                for e in range(4):
                    act.wait_ge(ret_cp, 4 * h + e + 1)
                    if 4 * h + e >= 2:
                        act.wait_ge(ret_m, 4 * h + e - 1)
                    nc.scalar.activation(sq[:, e % 2, :], ro[:, e, :], ACT.Square).then_inc(ret_q, 1)
                act.wait_ge(ret_m, 4 * h + 4)
                inverse_root(f"ret{h}", bank(nv, 0), 2.0)
                group_done(ng)
                for e in range(4):
                    s = SPLITS["ret"] + 4 * h + e
                    act.wait_ge(full_ready, s - 1)
                    nc.scalar.activation(r1[:, e % 2, :], bank(ng, e), ACT.Silu).then_inc(set_free[ng % 2], 1)
                    if e:
                        high(s - 1, y_hi[:, 4 * h + e - 1, :])
                high(SPLITS["ret"] + 4 * h + 3, y_hi[:, 4 * h + 3, :])
            ffn(2, "ffn2n", ACT.Silu, True)

            squares("sbn")
            norm_root("sbn")
            highs("sbn", h_hi)
            for half in range(2):
                n = G[f"sq{half}"]
                group_done(n)
                for j in range(4):
                    nc.scalar.activation(sqT[:, j, :], bank(n, j), ACT.Copy, scale=SH_D ** -0.5)\
                        .then_inc(set_free[n % 2], 1)
                n = G[f"sv{half}"]
                group_done(n)
                for j in range(4):
                    nc.scalar.activation(sv[:, j, :], bank(n, j), ACT.Copy).then_inc(set_free[n % 2], 1)
                act.preload_act_table_set("natural_log_exp_and_others")
                for it in range(len(SB) + 3):
                    if it >= 3:
                        u = it - 3
                        pair, j, e = SB[u]
                        w = SEQ - P * j
                        act.wait_ge(st_acc, len(SB) * half + u + 1)
                        if u >= 4:
                            act.wait_ge(st_o, len(SB) * half + u - 3)
                        nc.scalar.activation(s_a[:, u % 4, 0:w], sb_bank(u)[:, 0:w], ACT.Exp).then_inc(st_ex, 1)
                    if it < len(SB):
                        pair, j, e = SB[it]
                        g = len(SB) * half + it
                        ez = s_ez[:, it % 4, 0:SEQ - P * j]
                        act.wait_ge(st_min, g + 1)
                        nc.scalar.activation(ez, ez, ACT.Exp).then_inc(act_order, 1)
                        act.wait_ge(act_order, g + 1)
                        nc.scalar.activation(ez, ez, ACT.Ln, bias=1.0).then_inc(st_l, 1)
                    if it > 8 and it % 8 == 5:
                        pair = it // 8 - 1
                        act.wait_ge(st_o, len(SB) * half + 8 * (pair + 1))
                        nc.scalar.activation(so_hi[:, 4 * half + pair, :], ps[:, 4 + pair % 2, :], ACT.Copy)\
                            .then_inc(sb_h, 1)
                pair = 3
                act.wait_ge(st_o, len(SB) * (half + 1))
                nc.scalar.activation(so_hi[:, 4 * half + pair, :], ps[:, 4 + pair % 2, :], ACT.Copy)\
                    .then_inc(sb_h, 1)
            ffn(3, "ffn3n", ACT.Silu, True)
            squares("fin")
            norm_root("fin")
            for u in range(2 * TT):
                act.wait_ge(turned, 1 + 8 + 8 + u + 1)
                nc.scalar.activation(o_tok[:, u // 2, 512 * (u % 2):512 * (u % 2) + 512], ps[:, u % 4, :], ACT.Copy)\
                    .then_inc(turned_read, 1)

        @block.vector
        def _(dve):
            order = Chain(dve, dve_order)
            G = GIDX
            V = nc.vector

            def group_done(n):
                dve.wait_ge(slot_used, SLOT0[n + 1])

            def scaled_full(s, value):
                if s >= 2:
                    dve.wait_ge(full_hi, s - 1)
                    dve.wait_ge(split_ready, s - 1)
                value(full[:, s % 2, :]).then_inc(full_ready, 1)

            def low(s, hi, lo, width=SEQ):
                dve.wait_ge(full_ready, s + 1)
                dve.wait_ge(full_hi, s + 1)
                V.tensor_tensor(lo, full[:, s % 2, 0:width], hi.bitcast(F32), ALU.subtract).then_inc(split_ready, 1)

            def norm_rstd(name, width=SEQ):
                dve.wait_ge(rstd_ready, ROOT_AT[name] + 1)

            def norm(name, hi, lo, src=x, width=SEQ):
                norm_rstd(name, width)
                s0 = SPLITS[name]
                for k in range(KT + 1):
                    if k < KT:
                        scaled_full(s0 + k, lambda o: V.scalar_tensor_tensor(
                            o[:, 0:width], src[:, k, 0:width], gain(GAIN_OF[name], k), rstd[:, 0:width],
                            ALU.mult, ALU.mult))
                    if k:
                        low(s0 + k - 1, hi[:, k - 1, 0:width], lo[:, k - 1, 0:width], width)

            def norm_in_place(name, ready, done):
                norm_rstd(name)
                for k in range(KT):
                    V.scalar_tensor_tensor(x[:, k, :], x[:, k, :], gain(GAIN_OF[name], k), rstd[:],
                                           ALU.mult, ALU.mult).then_inc(done, 1)

            X_DONE, BANKS_DONE = [8], [0]

            def residual(names, first=0, then=None):
                for h, name in enumerate(names, first):
                    n = G[name]
                    for j in range(4):
                        if j < 3:
                            BANKS_DONE[0] += 1
                            dve.wait_ge(bank_done, BANKS_DONE[0])
                        else:
                            group_done(n)
                        V.tensor_tensor(x[:, 4 * h + j, :], x[:, 4 * h + j, :], bank(n, j), ALU.add)\
                            .then_inc(x_ready, 1)
                        X_DONE[0] += 1
                        if j == 3:
                            dve.wait_ge(x_ready, X_DONE[0])
                            for b in range(4):
                                dve.sem_inc(set_free[n % 2], 1)
                    if then and h == 0:
                        a0 = 3 * ADDED.index(then)
                        for k in range(1, 4):
                            dve.wait_ge(sq_ready, 8 * NORM_AT[then] + k + 1)
                            if k > 1:
                                dve.wait_ge(sq_added, a0 + k - 1)
                            V.tensor_tensor(sq[:, 0, :], sq[:, 0, :], sq[:, 1, :], ALU.add).then_inc(sq_added, 1)

            for k in range(KT):
                dve.wait_ge(turned, 1 + k)
                V.tensor_copy(x[:, k, :], ps[:, 2 + k % 4, :]).then_inc(x_ready, 1)
            dve.wait_ge(turned, 1 + KT)
            V.tensor_copy(vecs[:, 0, 0:GAIN_ROWS], ps[:, 0, 0:GAIN_ROWS]).then_inc(turned_read, 1)
            dve.wait_ge(turned_read, 1)
            norm("mix", h_hi, h_lo)

            group_done(G["kv"])
            for j in range(4):
                V.tensor_copy(kvT[:, j, :], bank(G["kv"], j)).then_inc(set_free[G["kv"] % 2], 1)
            dve.wait_ge(cmp_pe, 2)
            V.tensor_copy(posT[:].rearrange("p a c -> p (a c)"), ps[:, 0, 0:2 * CMPB]).then_inc(cmp_b, 1)
            dve.wait_ge(cmp_b, 1)
            dve.wait_ge(set_free[G["kv"] % 2], 4 * (G["kv"] // 2 + 1))
            for kv in range(2):
                for h in range(KVH):
                    r = slice(HD * h, HD * h + HD)
                    tokens = kvT[r, kv, :].rearrange("p (n c o) -> p o c n", c=8, o=2)
                    places = posT[r, kv, :].rearrange("p (c o) -> p o c", o=2)
                    for half in range(2):
                        for odd in range(2):
                            last = V.tensor_tensor(blk[HD * odd:HD * odd + HD, kv, 8 * half:8 * half + 8, h, :],
                                                   tokens[:, odd, :, half:half + NCMP],
                                                   places[:, odd, 8 * half:8 * half + 8].unsqueeze(2)
                                                   .to_broadcast([HD, 8, NCMP]), ALU.add)
                last.then_inc(cmp_blk, 1)
            group_done(G["vb"])
            for j in range(4):
                V.tensor_copy(vb[:, j, :], bank(G["vb"], j)).then_inc(set_free[G["vb"] % 2], 1)
            dve.wait_ge(cmp_pe, 5)
            for h in range(KVH):
                order.mark(V.tensor_copy(kcT[HD * h:HD * h + HD, 0:NCMP],
                                         ps[HD * h:HD * h + HD, h, 0:NCMP]))
            V.tensor_copy(vc[0:NCMP, :, :], ps[0:NCMP, 2:4, 0:HD]).then_inc(cmp_b, 1)
            group_done(G["tok"])
            for j in range(4):
                V.tensor_copy(tok[:, j, :], bank(G["tok"], j)[:, 0:TOKW]).then_inc(set_free[G["tok"] % 2], 1)
            dve.wait_ge(gate_loaded, 16)
            dve.wait_ge(set_free[0], 4 * (G["tok"] // 2 + 1))
            V.tensor_tensor(gates[:], tok[:, :, 2 * P:2 * P + 24],
                            gate_b[:].unsqueeze(1).to_broadcast([P, TT, 3 * HEADS]), ALU.add).then_inc(gate_a, 1)
            dve.wait_ge(const_ready, 2)
            dve.wait_ge(gate_s, 1)
            g0 = gates[:, 0, :].rearrange("p (h b) -> p h b", b=3)[:, :, 0]
            V.tensor_scalar(g0, g0, row_ok[:, 0:1], None, ALU.mult).then_inc(gate_m, 1)

            def nsa_bias(it):
                qt, h = NSA[it]
                b, bank0 = it % NSA_DEEP, 2 * (it % 2)
                nk, nw = P * (qt + 1), P * min(3, qt + 1)
                dve.wait_ge(att_s, it + 1)
                if it >= NSA_DEEP:
                    dve.wait_ge(att_t, it - NSA_DEEP + 1)
                order.mark(V.scalar_tensor_tensor(s_buf[:, b, 0:nk], d_slc[:, SEQ - nk:SEQ], SLOPES[h],
                                                  ps[:, bank0, 0:nk], ALU.mult, ALU.add))
                order.mark(V.scalar_tensor_tensor(s_buf[:, b, 512:512 + nw], d_win[:, WIN + P - nw:WIN + P],
                                                  SLOPES[h], ps[:, bank0 + 1, 0:nw], ALU.mult, ALU.add))
                V.scalar_tensor_tensor(s_buf[:, b, 896:896 + NCMP], d_cmp[:, qt, 0:NCMP], SLOPES[h],
                                       ps[:, bank0 + 1, 384:384 + NCMP], ALU.mult, ALU.add).then_inc(att_m, 1)
                order.wait()
                order.mark(V.tensor_reduce(att_st[:, b, 1:2], s_buf[:, b, 0:nk], AX_X, ALU.max, negate=True))
                order.mark(V.tensor_reduce(att_st[:, b, 2:3], s_buf[:, b, 512:512 + nw], AX_X, ALU.max,
                                           negate=True))
                dve.wait_ge(att_m, it + 1)
                V.tensor_reduce(att_st[:, b, 0:1], s_buf[:, b, 896:896 + NCMP], AX_X, ALU.max, negate=True)\
                    .then_inc(att_n, 1)

            def nsa_scale(it):
                qt, h = NSA[it]
                b = it % NSA_DEEP
                nk, nw = P * (qt + 1), P * min(3, qt + 1)
                dve.wait_ge(att_e, it + 1)
                order(V.reciprocal(att_st[:, b, 6:9], att_st[:, b, 3:6]))
                order(V.tensor_tensor(att_st[:, b, 9:12], att_st[:, b, 6:9], gates[:, qt, 3 * h:3 * h + 3],
                                      ALU.mult))
                for n, (c, w) in enumerate(((896, NCMP), (0, nk), (512, nw))):
                    last = V.tensor_scalar(s_buf[:, b, c:c + w], s_buf[:, b, c:c + w], att_st[:, b, 9 + n:10 + n],
                                           None, ALU.mult)
                last.then_inc(att_p, 1)

            dve.wait_ge(gate_m, 1)
            for it in range(len(NSA) + 7):
                if it >= 7 and it % 2:
                    pr = (it - 7) // 2
                    qt, i = NSA[2 * pr][0], pr % GRP
                    dve.wait_ge(att_h, pr + 1)
                    V.tensor_tensor(o_lo[:, i, P * qt:P * qt + P], ps[:, 6 + pr % 2, 0:P],
                                    o_hi[:, i, P * qt:P * qt + P].bitcast(F32), ALU.subtract).then_inc(att_r, 1)
                if it < len(NSA):
                    nsa_bias(it)
                if 1 <= it < len(NSA) + 1:
                    nsa_scale(it - 1)

            dve.wait_ge(gla_pe, 3)
            order(V.memset(keep[:], 1.0))
            order(V.memset(keep[:].rearrange("p (c i) -> p c i", i=CH)[:, :, 0:1], 0.0))
            for pr in range(2):
                v0, x0 = 3 * pr, 6 * pr
                if pr:
                    dve.wait_ge(gla_qk, 1)
                    dve.wait_ge(gla_x, 6)
                b_al = vecs[:, 0, V_BALPHA + pr:V_BALPHA + pr + 1]
                V.tensor_scalar(ebuf[:], ps[:, 1 + pr, :], b_al, -FAR, ALU.add, ALU.max).then_inc(gla_v, 1)
                V.tensor_scalar(la[:], ps[:, 1 + pr, :], b_al, None, ALU.add).then_inc(gla_lg, 1)
                dve.wait_ge(gla_x, x0 + 2)
                dve.wait_ge(gla_lg, pr + 1)
                order(V.scalar_tensor_tensor(la[:], ebuf[:], -1.0, la[:], ALU.mult, ALU.min))
                V.tensor_tensor_scan(bcum[:], keep[:], la[:], 0.0, ALU.mult, ALU.add).then_inc(gla_v, 1)
                dve.wait_ge(gla_v, v0 + 2)
                b3 = bcum[:].rearrange("p (c i) -> p c i", i=CH)
                V.tensor_tensor(la[:].rearrange("p (c i) -> p c i", i=CH),
                                b3[:, :, CH - 1:CH].to_broadcast([P, NCH, CH]), b3, ALU.subtract).then_inc(gla_v, 1)
                dve.wait_ge(gla_x, x0 + 3)
                V.tensor_tensor(ks_t[:], ks_t[:], qkb[:, 2 + pr, :], ALU.mult).then_inc(gla_ks, 1)
                dve.wait_ge(gla_ks, pr + 1)
                dve.wait_ge(gla_x, x0 + 6)
                order.mark(V.tensor_tensor(qkb[:, 2 + pr, :], ek[:], qkb[:, 2 + pr, :], ALU.mult))
                V.tensor_tensor(qkb[:, pr, :], ebuf[:], qkb[:, pr, :], ALU.mult).then_inc(gla_qk, 1)
            order.mark(V.memset(attT[:], 0.0))
            order(V.memset(states[:, :, 0, :], 0.0))

            def gla_mask(head):
                dve.wait_ge(gla_sc, head + 1)
                if head >= 2:
                    dve.wait_ge(gla_o, head - 1)
                for q in range(2):
                    r = slice(CH * q, CH * q + CH)
                    last = V.tensor_tensor(
                        attT[r, head % 2, :, CH * q:CH * q + CH],
                        ps[r, 2 + head % 2, :].rearrange("p (t c) -> p t c", t=TT)[:, :, CH * q:CH * q + CH],
                        caus[r, :].unsqueeze(1).to_broadcast([CH, TT, CH]), ALU.mult)
                last.then_inc(gla_at, 1)

            gla_mask(0)
            gla_mask(1)
            for pr in range(2):
                dve.wait_ge(gla_pe, 6 + pr)
                for c in range(NCH - 1):
                    for e in range(2):
                        r = slice(CH * e, CH * e + CH)
                        ins = V.scalar_tensor_tensor(states[r, pr, c + 1, :], states[r, pr, c, :],
                                                     dec[r, pr, c:c + 1], inc_at(pr, c, e), ALU.mult, ALU.add)
                        if c < NCH - 2 or e == 0:
                            order.mark(ins)
                        else:
                            ins.then_inc(gla_st, 1)
                    order.wait()
            for head in range(GH):
                if head + 2 < GH:
                    gla_mask(head + 2)
                dve.wait_ge(rstd_ready, ROOT_AT[f"gla{head}"] + 1)
                s = SPLITS["gla"] + head
                if s >= 2:
                    dve.wait_ge(full_hi, s - 1)
                    dve.wait_ge(split_ready, s - 1)
                f = full[:, s % 2, :]
                V.tensor_tensor(f, gla_bank(head), rstd[:], ALU.mult).then_inc(gla_rd, 1)
                dve.wait_ge(gla_rd, head + 1)
                V.scalar_tensor_tensor(f, f, vecs[:, 0, V_GLAG:V_GLAG + 1], rT[:, head, :], ALU.mult, ALU.mult)\
                    .then_inc(full_ready, 1)
                low(s, o_hi[:, 4 + head, :], o_lo[:, 4 + head, :])

            for h in range(2):
                for j in range(4):
                    if j == 0:
                        group_done(G[f"bn{h}"])
                        dve.wait_ge(set_free[G[f"mn{h}"] % 2], 4 * (G[f"mn{h}"] // 2 + 1))
                    V.tensor_tensor(gN[:, j, :], gN[:, j, :], bank(G[f"bn{h}"], j), ALU.mult)\
                        .then_inc(set_free[G[f"bn{h}"] % 2], 1)
                group_done(G[f"bg{h}"])
                dve.wait_ge(set_free[G[f"mg{h}"] % 2], 4 * (G[f"mg{h}"] // 2 + 1))
                for j in range(4):
                    V.tensor_tensor(gG[:, j, :], gG[:, j, :], bank(G[f"bg{h}"], j), ALU.mult)\
                        .then_inc(set_free[G[f"bg{h}"] % 2], 1)
                dve.wait_ge(set_free[G[f"bg{h}"] % 2], 4 * (G[f"bg{h}"] // 2 + 1))
                dve.wait_ge(set_free[G[f"bn{h}"] % 2], 4 * (G[f"bn{h}"] // 2 + 1))
                for j in range(4 + 1):
                    s = SPLITS["mx"] + 4 * h + j
                    if j < 4:
                        scaled_full(s, lambda o: V.tensor_tensor(o, gN[:, j, :], gG[:, j, :], ALU.add))
                    if j:
                        low(s - 1, mx_hi[:, 4 * h + j - 1, :], mx_lo[:, 4 * h + j - 1, :])
            residual(("out0",))

            for k in range(KT):
                dve.wait_ge(turned, 1 + 8 + k + 1)
                V.tensor_copy(memT[:, k, :], ps[:, 4 + k % 4, 0:MEM]).then_inc(mem_turned_read, 1)
            norm("mem", m_hi, m_lo, memT, MEM)
            residual(("out1",), 1)
            norm("xn", h_hi, h_lo)
            group_done(G["xv"])
            for j in range(4):
                if j < MEM // P:
                    V.tensor_copy(xv[:, j, :], bank(G["xv"], j)).then_inc(set_free[G["xv"] % 2], 1)
                else:
                    dve.sem_inc(set_free[G["xv"] % 2], 1)
            for it in range(XH * TT + 4):
                if it < XH * TT:
                    dve.wait_ge(xat_s, it + 1)
                    if it >= 3:
                        dve.wait_ge(xat_p, it - 2)
                    V.tensor_reduce(x_st[:, it % 3, 0:1], ps[:, it % 2, 0:MEM], AX_X, ALU.max, negate=True)\
                        .then_inc(xat_m, 1)
                if 1 <= it <= XH * TT:
                    u = it - 1
                    dve.wait_ge(xat_e, u + 1)
                    order(V.reciprocal(x_st[:, u % 3, 2:3], x_st[:, u % 3, 1:2]))
                    V.tensor_scalar(xp[:, u % 3, :], xp[:, u % 3, :], x_st[:, u % 3, 2:3], None, ALU.mult)\
                        .then_inc(xat_p, 1)
                if it >= 7 and it % TT == 3:
                    h = it // TT - 1
                    dve.wait_ge(xat_h, h + 1)
                    V.tensor_tensor(xo_lo[:, h, :], ps[:, 4 + h % 2, :], xo_hi[:, h, :].bitcast(F32), ALU.subtract)\
                        .then_inc(xat_r, 1)
            dve.wait_ge(conv_turned, 1)
            V.tensor_copy(vecs[:, 1:5, :].rearrange("p r c -> p (r c)"), ps[:, 0, 0:16 * FT])
            V.tensor_copy(vecs[:, 5, :], ps[:, 1, 0:4 * FT]).then_inc(conv_read, 1)
            residual(("xo0", "xo1"), then="ffn1n")

            def ffn(tag, name, two):
                norm(name, h_hi, h_lo)
                n0 = G[f"up{tag}_0"]
                row = {1: 1, 2: 2, 3: 4}[tag]
                s0 = SPLITS[f"ffn{tag}"]
                per = 4 if two else 2
                cd = CONV0[tag]
                nl0 = 22 * (tag - 1)

                def taps(dst, src, e, col, r, done, own):
                    V.scalar_tensor_tensor(dst[:, e, 2:SEQ], src[:, 0:SEQ - 2], vec(r, col),
                                           dst[:, e, 2:SEQ], ALU.mult, ALU.add).then_inc(dve_order, 1)
                    dve.wait_ge(dve_order, own)
                    V.scalar_tensor_tensor(dst[:, e, 1:SEQ], src[:, 0:SEQ - 1], vec(r, col + FT),
                                           dst[:, e, 1:SEQ], ALU.mult, ALU.add).then_inc(done, 1)

                base = order.n

                def group(n, c, t, s, nl, own):
                    st = set_free[n % 2]
                    for half in range(1 + two):
                        for e in range(2):
                            u = 2 * half + e
                            dve.wait_ge(conv_a, c + u + 1)
                            taps(cv if half else cu, ps[:, 4 * (n % 2) + u, :], e, t + e, row + half, conv_d,
                                 own + u + 1)
                    for e in range(2):
                        dve.wait_ge(nonlin, nl + e + 1)
                        dve.wait_ge(full_hi, s + e - 1)
                        dve.wait_ge(split_ready, s + e - 1)
                        if two:
                            dve.wait_ge(conv_d, c + 4)
                            V.tensor_tensor(full[:, (s0 + e) % 2, :], cu[:, e, :], cv[:, e, :], ALU.mult)\
                                .then_inc(full_ready, 1)
                        else:
                            V.tensor_tensor(full[:, (s0 + e) % 2, :], cu[:, e, :], ps[:, 4 * (n % 2) + 2 + e, :],
                                            ALU.mult).then_inc(full_ready, 1)
                    dve.wait_ge(full_ready, s + 2)
                    for b in range(4):
                        dve.sem_inc(st, 1)
                    for e in range(2):
                        dve.wait_ge(full_hi, s + e + 1)
                        V.tensor_tensor(f_tile(f_lo, t + e), full[:, (s0 + e) % 2, :],
                                        f_tile(f_hi, t + e).bitcast(F32), ALU.subtract).then_inc(split_ready, 1)

                group(n0, cd, 0, s0, nl0, base)
                with dve.Fori(0, 5) as i:
                    for e in range(2):
                        group(n0 + 1 + e, i * (2 * per) + (cd + per * (1 + e)), i * 4 + 2 * (1 + e),
                              i * 4 + (s0 + 2 * (1 + e)), i * 4 + (nl0 + 2 * (1 + e)),
                              i * (2 * per) + (base + per * (1 + e)))
                order.n = base + 11 * per
                residual((f"down{tag}_0", f"down{tag}_1"), then={1: "fin1", 2: "sbn", 3: "fin"}[tag])

            ffn(1, "ffn1n", False)

            norm_rstd("fin1")
            dve.wait_ge(weighted_used, KT)
            order(V.tensor_tensor(sq[:, 0, :], ps[:, NORM_BANK["retn"], :], rstd[:], ALU.mult))
            V.tensor_tensor(sq[:, 0, :], sq[:, 0, :], rstd[:], ALU.mult).then_inc(weighted_mean, 1)
            for k in range(KT + 2):
                if k < KT:
                    V.scalar_tensor_tensor(x[:, k, :], x[:, k, :], gain(GAIN_OF["fin1"], k), rstd[:],
                                           ALU.mult, ALU.mult).then_inc(x_ready, 1)
                if k >= 1:
                    u = k - 1
                    if u == 0:
                        dve.wait_ge(rstd_ready, ROOT_AT["retn"] + 1)
                    if u < KT:
                        dve.wait_ge(x_ready, X_DONE[0] + u + 1)
                        scaled_full(SPLITS["retn"] + u, lambda o: V.scalar_tensor_tensor(
                            o, x[:, u, :], gain(GAIN_OF["retn"], u), sq[:, 1, :], ALU.mult, ALU.mult))
                    if u:
                        low(SPLITS["retn"] + u - 1, h_hi[:, u - 1, :], h_lo[:, u - 1, :])
            X_DONE[0] += KT
            dve.wait_ge(rope_loaded, 32)
            for h in range(RH):
                nq, ng = G[f"rqk{h}"], G[f"rg{h}"]
                group_done(nq)
                if h:
                    dve.wait_ge(ret_s, TT * h)
                for w in range(2):
                    b0, b1 = bank(nq, 2 * w), bank(nq, 2 * w + 1)
                    order.mark(V.tensor_tensor(rq[:, 2 * w, :], b0, cosT[:], ALU.mult))
                    order.mark(V.tensor_tensor(rq[:, 2 * w + 1, :], b0, sinT[:], ALU.mult))
                    order.mark(V.tensor_tensor(r1[:, 0, :], b1, sinT[:], ALU.mult))
                    V.tensor_tensor(r1[:, 1, :], b1, cosT[:], ALU.mult).then_inc(rope_d, 1)
                    order.wait()
                    dve.wait_ge(rope_d, 2 * h + w + 1)
                    order.mark(V.tensor_tensor(rq[:, 2 * w, :], rq[:, 2 * w, :], r1[:, 0, :], ALU.subtract))
                    order(V.tensor_tensor(rq[:, 2 * w + 1, :], rq[:, 2 * w + 1, :], r1[:, 1, :], ALU.add))
                for b in range(4):
                    dve.sem_inc(set_free[nq % 2], 1)
                dve.wait_ge(dmat_loaded, 16 * (h + 1))
                for j in range(TT):
                    dve.wait_ge(ret_s, TT * h + j + 1)
                    w = SEQ - P * j
                    V.scalar_tensor_tensor(rsc[:, j, 0:w], bank(nq, j)[:, 0:w], 1.0 / 16, dmat[:, 0:w],
                                           ALU.mult, ALU.mult).then_inc(ret_sc, 1)
                dve.wait_ge(rstd_ready, ROOT_AT[f"ret{h}"] + 1)
                for e in range(4 + 1):
                    s = SPLITS["ret"] + 4 * h + e
                    if e < 4:
                        order(V.tensor_tensor(ro[:, e, :], ro[:, e, :], rstd[:], ALU.mult))
                        dve.wait_ge(set_free[ng % 2], 4 * (ng // 2) + e + 1)
                        scaled_full(s, lambda o: V.tensor_tensor(o, ro[:, e, :], r1[:, e % 2, :], ALU.mult))
                    if e:
                        low(s - 1, y_hi[:, 4 * h + e - 1, :], y_lo[:, 4 * h + e - 1, :])
            residual(("ro0", "ro1"), then="ffn2n")
            ffn(2, "ffn2n", True)

            norm("sbn", h_hi, h_lo)
            dve.wait_ge(const_ready, 3)
            for half in range(2):
                n = G[f"sk{half}"]
                group_done(n)
                for j in range(4):
                    V.tensor_copy(skT[:, j, :], bank(n, j)).then_inc(set_free[n % 2], 1)

                def bounded(it):
                    pair, j, e = SB[it]
                    g = len(SB) * half + it
                    w = SEQ - P * j
                    dve.wait_ge(st_z, g + 1)
                    if it >= 4:
                        dve.wait_ge(st_sp, g - 3)
                    V.tensor_scalar(s_ez[:, it % 4, 0:w], sb_bank(it)[:, 0:w], FAR, None, ALU.min)\
                        .then_inc(st_min, 1)

                def softplus(it):
                    pair, j, e = SB[it]
                    g = len(SB) * half + it
                    w = SEQ - P * j
                    dve.wait_ge(st_l, g + 1)
                    sp = s_sp[:, it % 4, 0:w]
                    if it >= 4:
                        dve.wait_ge(st_acc, g - 3)
                        dve.wait_ge(st_up, updates(half, it - 4))
                        order.wait()
                    order(V.tensor_tensor(sp, sb_bank(it)[:, 0:w], s_ez[:, it % 4, 0:w], ALU.max))
                    V.tensor_tensor(sp[:, 0:P], sp[:, 0:P], strict[:], ALU.mult).then_inc(st_sp, 1)

                def update(it):
                    pair, j, e = SB[it]
                    if j == 0:
                        return
                    g = len(SB) * half + it
                    dve.wait_ge(st_acc, g + 1)
                    dve.wait_ge(st_sp, g + 1)
                    if j < TT - 1:
                        order.mark(V.tensor_tensor(s_sum[:, e, P * (j + 1):SEQ], s_sum[:, e, P * (j + 1):SEQ],
                                                   s_sp[:, it % 4, P:SEQ - P * j], ALU.add))
                    V.tensor_copy(s_sum[:, e, P * j:P * (j + 1)], s_sp[:, it % 4, 0:P]).then_inc(st_up, 1)

                def low_part(pair):
                    i = 4 * half + pair
                    dve.wait_ge(sb_h, i + 1)
                    V.tensor_tensor(so_lo[:, i, :], ps[:, 4 + pair % 2, :], so_hi[:, i, :].bitcast(F32),
                                    ALU.subtract).then_inc(sb_r, 1)

                for it in range(len(SB) + 3):
                    if it < len(SB):
                        bounded(it)
                    if 1 <= it <= len(SB):
                        softplus(it - 1)
                    if it >= 3:
                        update(it - 3)
                    if it > 8 and it % 8 == 5:
                        low_part(it // 8 - 1)
                low_part(3)
            residual(("so0", "so1"), then="ffn3n")
            ffn(3, "ffn3n", True)
            norm_in_place("fin", x_ready, fin_ready)


def shape_constants():
    pos = np.arange(SEQ, dtype=np.float32)
    inv = (np.float32(10000.0) ** (-np.arange(0, 256, 2, dtype=np.float32) / np.float32(256))).astype(np.float32)
    ang = inv[:, None] * pos[None, :]
    key, query = np.arange(P)[:, None], np.arange(SEQ)[None, :]
    decay = np.stack([np.where(query >= key, np.exp(np.maximum(query - key, 0) * np.log(g)), 0.0)
                      for g in RET_DECAY]).astype(np.float32)
    return {"rope_cos": np.cos(ang).astype(np.float32), "rope_sin": np.sin(ang).astype(np.float32),
            "ret_decay": decay}


def kernel(**inputs):
    import concourse.bacc as bacc
    from concourse.bass_utils import run_bass_kernel_spmd

    nc = bacc.Bacc("TRN2", target_bir_lowering=False, num_devices=1)
    arrays, aps = {}, {}
    for name, value in {**inputs, **shape_constants()}.items():
        v = np.ascontiguousarray(value)
        arrays[f"in_{name}"] = v
        aps[name] = nc.dram_tensor(f"in_{name}", v.shape, mybir.dt.from_np(v.dtype), kind="ExternalInput").ap()
    out = nc.dram_tensor("out_x", (1, SEQ, D), F32, kind="ExternalOutput").ap()
    build(nc, aps, out)
    result = run_bass_kernel_spmd(nc, [arrays], core_ids=[0])
    return result.results[0]["out_x"]
```
